# Optimizing a Trainium2 kernel written in Bass

```python
import math
import numpy as np
import jax
import jax.numpy as jnp
from jax import lax

D_MODEL = 1024
BATCH = 1
SEQ = 256
DEPTH = 1

NSA_HEADS = 8
NSA_KV_GROUPS = 2
NSA_HPG = NSA_HEADS // NSA_KV_GROUPS
NSA_HEAD_DIM = 64
CMP_LEN = 32
CMP_STRIDE = 16
CMP_HIDDEN = 256
SEL_BLOCK = 64
SEL_TOP_N = 16
N_LOCAL_SEL = 2
WINDOW = 512
Q_BLOCK = 128
RET_HEADS = 4
RET_QK_DIM = 128
RET_V_DIM = 256
RET_CHUNK = 128
ROPE_BASE = 10000.0
REL_BUCKETS = 32
REL_MAX_DIST = 128
N_GROUPS = 4
EXPERTS_PER_GROUP = 8
N_EXPERTS = N_GROUPS * EXPERTS_PER_GROUP
EXPERT_TOP_K = 2
EXPERT_FF = 256
EPS = 1e-6

NSA_Q_W = NSA_HEADS * NSA_HEAD_DIM
NSA_KV_W = NSA_KV_GROUPS * NSA_HEAD_DIM
RET_QK_W = RET_HEADS * RET_QK_DIM
RET_V_W = RET_HEADS * RET_V_DIM
SPLITS = (NSA_Q_W, 6 * NSA_KV_W, 3 * NSA_HEADS, RET_QK_W, RET_QK_W, RET_V_W, RET_V_W, D_MODEL, D_MODEL)
IN_PROJ_W = NSA_Q_W + 6 * NSA_KV_W + 3 * NSA_HEADS + 2 * RET_QK_W + 2 * RET_V_W + 2 * D_MODEL

kernel_name = 'hybrid_nsa_retention_hmoe_block'

def rmsnorm(x, w):
    xf = x.astype(jnp.float32)
    y = xf * lax.rsqrt(jnp.mean(xf * xf, axis=-1, keepdims=True) + EPS)
    return (y * w.astype(jnp.float32)).astype(x.dtype)

def t5_bucket(dist):
    dist = jnp.maximum(dist, 0)
    max_exact = REL_BUCKETS // 2
    d_f = jnp.maximum(dist, 1).astype(jnp.float32)
    large = max_exact + (jnp.log(d_f / max_exact) / math.log(REL_MAX_DIST / max_exact)
                         * (REL_BUCKETS - max_exact)).astype(jnp.int32)
    large = jnp.minimum(large, REL_BUCKETS - 1)
    return jnp.where(dist < max_exact, dist, large)

def masked_softmax(s, mask, axis):
    s = jnp.where(mask, s, -1e30)
    m = jnp.max(s, axis=axis, keepdims=True)
    e = jnp.where(mask, jnp.exp(s - m), 0.0)
    return e / jnp.maximum(jnp.sum(e, axis=axis, keepdims=True), 1e-30)

def compress_tokens(kv, pos_emb, w1, w2):
    B, S, G, d = kv.shape
    n_cmp = (S - CMP_LEN) // CMP_STRIDE + 1
    idx = np.arange(n_cmp)[:, None] * CMP_STRIDE + np.arange(CMP_LEN)[None, :]
    blocks = kv[:, idx] + pos_emb[None, None, :, None, :]
    blocks = jnp.moveaxis(blocks, 3, 2).reshape(B, n_cmp, G, CMP_LEN * d)
    return jax.nn.gelu(blocks @ w1) @ w2

def nsa_attention(q, kv, gates, rel_bias, pos_k, k_w1, k_w2, pos_v, v_w1, v_w2):
    B, S = q.shape[0], q.shape[1]
    G, HPG, Dh = NSA_KV_GROUPS, NSA_HPG, NSA_HEAD_DIM
    f32 = jnp.float32
    scale = Dh ** -0.5
    k_cmp, v_cmp, k_sel, v_sel, k_win, v_win = [kv[:, :, j] for j in range(6)]
    kc = compress_tokens(k_cmp, pos_k, k_w1, k_w2)
    vc = compress_tokens(v_cmp, pos_v, v_w1, v_w2)
    n_cmp = kc.shape[1]
    cmp_end = jnp.arange(n_cmp) * CMP_STRIDE + (CMP_LEN - 1)
    n_sel = S // SEL_BLOCK
    top_n = min(SEL_TOP_N, n_sel)
    c_start = np.arange(n_cmp) * CMP_STRIDE
    b_start = np.arange(n_sel) * SEL_BLOCK
    overlap = jnp.asarray((c_start[:, None] <= b_start[None, :] + SEL_BLOCK - 1)
                          & (c_start[:, None] + CMP_LEN - 1 >= b_start[None, :]), dtype=f32)
    ks_blk = jnp.moveaxis(k_sel.reshape(B, n_sel, SEL_BLOCK, G, Dh), 3, 1)
    vs_blk = jnp.moveaxis(v_sel.reshape(B, n_sel, SEL_BLOCK, G, Dh), 3, 1)
    kw = jnp.pad(k_win, ((0, 0), (WINDOW, 0), (0, 0), (0, 0)))
    vw = jnp.pad(v_win, ((0, 0), (WINDOW, 0), (0, 0), (0, 0)))
    bias_g = rel_bias.reshape(REL_BUCKETS, G, HPG)
    b_ix = jnp.arange(B)[:, None, None, None]
    g_ix = jnp.arange(G)[None, None, :, None]
    blk_ids = jnp.arange(n_sel)
    n_qb = S // Q_BLOCK
    qb = jnp.moveaxis(q.reshape(B, n_qb, Q_BLOCK, G, HPG, Dh), 1, 0)
    gb = jnp.moveaxis(gates.reshape(B, n_qb, Q_BLOCK, 3, NSA_HEADS), 1, 0)

    def block(args):
        i, qi, gi = args
        start = i * Q_BLOCK
        t = start + jnp.arange(Q_BLOCK)
        s_c = jnp.einsum('bqgjd,bcgd->bqgjc', qi, kc).astype(f32) * scale
        dist_c = t[:, None] - cmp_end[None, :]
        s_c = s_c + jnp.transpose(bias_g[t5_bucket(dist_c)], (0, 2, 3, 1))[None]
        p_c = masked_softmax(s_c, (dist_c >= 0)[None, :, None, None, :], -1)
        o_c = jnp.einsum('bqgjc,bcgd->bqgjd', p_c.astype(vc.dtype), vc)
        imp = jnp.einsum('bqgc,cn->bqgn', p_c.sum(3), overlap)
        cur = t // SEL_BLOCK
        back = cur[:, None] - blk_ids[None, :]
        valid = back >= 0
        forced = (blk_ids[None, :] == 0) | (valid & (back < N_LOCAL_SEL))
        imp = jnp.where(forced[None, :, None, :], 1e9, jnp.where(valid[None, :, None, :], imp, -1e9))
        _, sel = lax.top_k(imp, top_n)
        k_g = ks_blk[b_ix, g_ix, sel]
        v_g = vs_blk[b_ix, g_ix, sel]
        pos_s = sel[..., None] * SEL_BLOCK + jnp.arange(SEL_BLOCK)
        dist_s = t[None, :, None, None, None] - pos_s
        s_s = jnp.einsum('bqgjd,bqgnkd->bqgjnk', qi, k_g).astype(f32) * scale
        bias_s = jnp.moveaxis(bias_g[t5_bucket(dist_s), g_ix[..., None]], -1, 3)
        p_s = masked_softmax(s_s + bias_s, (dist_s >= 0)[:, :, :, None], (-2, -1))
        o_s = jnp.einsum('bqgjnk,bqgnkd->bqgjd', p_s.astype(v_g.dtype), v_g)
        kw_i = lax.dynamic_slice_in_dim(kw, start, WINDOW + Q_BLOCK, axis=1)
        vw_i = lax.dynamic_slice_in_dim(vw, start, WINDOW + Q_BLOCK, axis=1)
        pos_w = start - WINDOW + jnp.arange(WINDOW + Q_BLOCK)
        dist_w = t[:, None] - pos_w[None, :]
        mask_w = (dist_w >= 0) & (dist_w < WINDOW) & (pos_w[None, :] >= 0)
        s_w = jnp.einsum('bqgjd,bkgd->bqgjk', qi, kw_i).astype(f32) * scale
        s_w = s_w + jnp.transpose(bias_g[t5_bucket(dist_w)], (0, 2, 3, 1))[None]
        p_w = masked_softmax(s_w, mask_w[None, :, None, None, :], -1)
        o_w = jnp.einsum('bqgjk,bkgd->bqgjd', p_w.astype(vw_i.dtype), vw_i)
        gi = gi.reshape(B, Q_BLOCK, 3, G, HPG)[..., None]
        o = gi[:, :, 0] * o_c + gi[:, :, 1] * o_s + gi[:, :, 2] * o_w
        return o.reshape(B, Q_BLOCK, NSA_HEADS * Dh)

    out = lax.map(block, (jnp.arange(n_qb), qb, gb))
    return jnp.moveaxis(out, 0, 1).reshape(B, S, NSA_HEADS * Dh)

def rotary(x, pos):
    half = x.shape[-1] // 2
    inv = ROPE_BASE ** (-jnp.arange(half, dtype=jnp.float32) / half)
    ang = pos[:, None].astype(jnp.float32) * inv[None, :]
    cos = jnp.cos(ang)[None, :, None, :]
    sin = jnp.sin(ang)[None, :, None, :]
    x1 = x[..., :half].astype(jnp.float32)
    x2 = x[..., half:].astype(jnp.float32)
    return jnp.concatenate([x1 * cos - x2 * sin, x1 * sin + x2 * cos], axis=-1).astype(x.dtype)

def retention(q, k, v, g, norm_w):
    B, S, H, dk = q.shape
    dv = v.shape[-1]
    C = RET_CHUNK
    nc = S // C
    f32 = jnp.float32
    pos = jnp.arange(S)
    q = rotary(q, pos)
    k = rotary(k, pos) * (dk ** -0.5)
    log_gamma = jnp.log(1.0 - 2.0 ** (-5.0 - jnp.arange(H, dtype=f32)))
    idx = jnp.arange(C, dtype=f32)
    diff = idx[:, None] - idx[None, :]
    decay_mask = jnp.where(diff >= 0, jnp.exp(jnp.maximum(diff, 0.0)[None] * log_gamma[:, None, None]), 0.0)
    q_decay = jnp.exp((idx + 1.0)[None, :] * log_gamma[:, None])[None, :, :, None]
    k_decay = jnp.exp((C - 1.0 - idx)[None, :] * log_gamma[:, None])[None, :, :, None]
    chunk_decay = jnp.exp(C * log_gamma)[None, :, None, None]

    def to_chunks(a):
        return a.reshape(B, nc, C, H, a.shape[-1]).transpose(1, 0, 3, 2, 4).astype(f32)

    def step(R, inp):
        qc, kc, vc = inp
        inner = jnp.einsum('bhid,bhjd->bhij', qc, kc) * decay_mask[None]
        y = jnp.einsum('bhij,bhjv->bhiv', inner, vc) + jnp.einsum('bhid,bhdv->bhiv', qc, R) * q_decay
        R = R * chunk_decay + jnp.einsum('bhjd,bhjv->bhdv', kc * k_decay, vc)
        return R, y

    R0 = jnp.zeros((B, H, dk, dv), f32)
    _, ys = lax.scan(step, R0, (to_chunks(q), to_chunks(k), to_chunks(v)))
    y = ys.transpose(1, 0, 3, 2, 4).reshape(B, S, H, dv)
    mu = jnp.mean(y, axis=-1, keepdims=True)
    var = jnp.mean(jnp.square(y - mu), axis=-1, keepdims=True)
    y = ((y - mu) * lax.rsqrt(var + EPS)).reshape(B, S, H * dv) * norm_w.astype(f32)
    return (jax.nn.silu(g.astype(f32)) * y).astype(g.dtype)

def hierarchical_moe(h, w_rg, b_rg, w_re, b_re, w_gate, w_up, w_down):
    B, S, _ = h.shape
    f32 = jnp.float32
    lg = (h @ w_rg).astype(f32) + b_rg.astype(f32)
    pg = jax.nn.softmax(lg, axis=-1)
    p_grp, grp = lax.top_k(pg, 1)
    le = ((h @ w_re).astype(f32) + b_re.astype(f32)).reshape(B, S, N_GROUPS, EXPERTS_PER_GROUP)
    le_g = jnp.take_along_axis(le, grp[..., None], axis=2)[:, :, 0]
    top_l, top_i = lax.top_k(le_g, EXPERT_TOP_K)
    w_sel = jax.nn.softmax(top_l, axis=-1) * p_grp
    e_idx = grp * EXPERTS_PER_GROUP + top_i
    combine = jnp.sum(jax.nn.one_hot(e_idx, N_EXPERTS, dtype=f32) * w_sel[..., None], axis=-2)

    def expert(acc, inp):
        wg, wu, wd, c = inp
        hid = jax.nn.silu(h @ wg) * (h @ wu)
        return acc + (hid @ wd) * c[..., None].astype(h.dtype), None

    out, _ = lax.scan(expert, jnp.zeros_like(h), (w_gate, w_up, w_down, jnp.moveaxis(combine, -1, 0)))
    return out

def setup_inputs(seed: int = 0) -> dict:
    key = jax.random.key(seed)
    ks = jax.random.split(key, 24)
    f32 = jnp.float32

    def nrm(k, shape, scale):
        return jax.random.normal(k, shape, f32) * scale

    D = D_MODEL
    return {
        'x': nrm(ks[0], (BATCH, SEQ, D), 1.0),
        'rel_bias': nrm(ks[1], (REL_BUCKETS, NSA_HEADS), 0.5),
        'norm_mix': 1.0 + nrm(ks[2], (DEPTH, D), 0.01),
        'w_in': nrm(ks[3], (DEPTH, D, IN_PROJ_W), D ** -0.5),
        'cmp_pos_k': nrm(ks[4], (DEPTH, CMP_LEN, NSA_HEAD_DIM), 0.1),
        'cmp_k_w1': nrm(ks[5], (DEPTH, CMP_LEN * NSA_HEAD_DIM, CMP_HIDDEN), (CMP_LEN * NSA_HEAD_DIM) ** -0.5),
        'cmp_k_w2': nrm(ks[6], (DEPTH, CMP_HIDDEN, NSA_HEAD_DIM), CMP_HIDDEN ** -0.5),
        'cmp_pos_v': nrm(ks[7], (DEPTH, CMP_LEN, NSA_HEAD_DIM), 0.1),
        'cmp_v_w1': nrm(ks[8], (DEPTH, CMP_LEN * NSA_HEAD_DIM, CMP_HIDDEN), (CMP_LEN * NSA_HEAD_DIM) ** -0.5),
        'cmp_v_w2': nrm(ks[9], (DEPTH, CMP_HIDDEN, NSA_HEAD_DIM), CMP_HIDDEN ** -0.5),
        'ret_norm': 1.0 + nrm(ks[10], (DEPTH, RET_V_W), 0.01),
        'w_nsa_up': nrm(ks[11], (DEPTH, NSA_Q_W, D), NSA_Q_W ** -0.5),
        'w_ret_up': nrm(ks[12], (DEPTH, RET_V_W, D), RET_V_W ** -0.5),
        'w_out': nrm(ks[13], (DEPTH, D, D), D ** -0.5),
        'norm_ffn': 1.0 + nrm(ks[14], (DEPTH, D), 0.01),
        'w_router_group': nrm(ks[15], (DEPTH, D, N_GROUPS), D ** -0.5),
        'b_router_group': nrm(ks[16], (DEPTH, N_GROUPS), 0.01),
        'w_router_expert': nrm(ks[17], (DEPTH, D, N_EXPERTS), D ** -0.5),
        'b_router_expert': nrm(ks[18], (DEPTH, N_EXPERTS), 0.01),
        'moe_w_gate': nrm(ks[19], (DEPTH, N_EXPERTS, D, EXPERT_FF), D ** -0.5),
        'moe_w_up': nrm(ks[20], (DEPTH, N_EXPERTS, D, EXPERT_FF), D ** -0.5),
        'moe_w_down': nrm(ks[21], (DEPTH, N_EXPERTS, EXPERT_FF, D), EXPERT_FF ** -0.5),
        'norm_final': 1.0 + nrm(ks[22], (D,), 0.01),
    }

def reference(x, rel_bias, norm_mix, w_in, cmp_pos_k, cmp_k_w1, cmp_k_w2, cmp_pos_v, cmp_v_w1, cmp_v_w2,
              ret_norm, w_nsa_up, w_ret_up, w_out, norm_ffn, w_router_group, b_router_group,
              w_router_expert, b_router_expert, moe_w_gate, moe_w_up, moe_w_down, norm_final):
    B, S, _ = x.shape
    split_idx = np.cumsum(SPLITS)[:-1].tolist()
    for l in range(DEPTH):
        h = rmsnorm(x, norm_mix[l])
        proj = h @ w_in[l]
        q_a, kv_a, g_a, q_r, k_r, v_r, g_r, gate_a, gate_r = jnp.split(proj, split_idx, axis=-1)
        y_a = nsa_attention(q_a.reshape(B, S, NSA_HEADS, NSA_HEAD_DIM),
                            kv_a.reshape(B, S, 6, NSA_KV_GROUPS, NSA_HEAD_DIM),
                            jax.nn.sigmoid(g_a.reshape(B, S, 3, NSA_HEADS)),
                            rel_bias, cmp_pos_k[l], cmp_k_w1[l], cmp_k_w2[l],
                            cmp_pos_v[l], cmp_v_w1[l], cmp_v_w2[l])
        y_r = retention(q_r.reshape(B, S, RET_HEADS, RET_QK_DIM),
                        k_r.reshape(B, S, RET_HEADS, RET_QK_DIM),
                        v_r.reshape(B, S, RET_HEADS, RET_V_DIM), g_r, ret_norm[l])
        merged = jax.nn.sigmoid(gate_a) * (y_a @ w_nsa_up[l]) + jax.nn.sigmoid(gate_r) * (y_r @ w_ret_up[l])
        x = x + merged @ w_out[l]
        h = rmsnorm(x, norm_ffn[l])
        x = x + hierarchical_moe(h, w_router_group[l], b_router_group[l], w_router_expert[l],
                                 b_router_expert[l], moe_w_gate[l], moe_w_up[l], moe_w_down[l])
    return rmsnorm(x, norm_final)


_drawn_inputs = setup_inputs


def setup_inputs(seed=0):
    import zlib

    import numpy as np

    out = dict(_drawn_inputs(seed))
    spreads = {}
    factors = {'norm_mix': 3.205,
     'cmp_pos_k': 23.311,
     'ret_norm': 37.26,
     'b_router_group': 40.152,
     'b_router_expert': 32.336,
     'norm_final': 180.055,
     'cmp_pos_v': 63.527,
     'norm_ffn': 8.0}
    for name, (base, spread) in spreads.items():
        noise = np.random.default_rng([zlib.crc32(name.encode()), seed]).standard_normal(out[name].shape)
        drawn = base * np.exp(spread * noise) if base else spread * noise
        out[name] = jnp.asarray(drawn.astype(out[name].dtype))
    for name, factor in factors.items():
        out[name] = (out[name] * factor).astype(out[name].dtype)
    return out
```

```python
from contextlib import ExitStack

import numpy as np
import concourse.bass as bass
from concourse import mybir

F32 = mybir.dt.float32
U32 = mybir.dt.uint32
ALU = mybir.AluOpType
ACT = mybir.ActivationFunctionType
AX = mybir.AxisListType.X

P = 128
D, S = 1024, 256
KT = D // P
TT = S // P
HEADS, GROUPS, HD = 8, 2, 64
PAIRS = HEADS // 2
CMP_LEN, CMP_STRIDE, CMP_HID = 32, 16, 256
NCMP = (S - CMP_LEN) // CMP_STRIDE + 1
NC16 = 16
BUCKETS, MAX_DIST = 32, 128
RH, RQ, RV = 4, 128, 256
NG, EPG, NE, FF = 4, 8, 32, 256
EPS = 1e-6
C = 32
BE = P // C
NB = NE // BE
ROUNDS = S // C
NVEC = 3 * KT + CMP_LEN
NEG = -1e30
COLS = dict(q=0, kv=512, ga=1280, qr=1304, kr=1816, vr=2328, gr=3352, gate_a=4376, gate_r=5400)
SLOT = KT * 512
NSLOT = 4


def t5_bucket(dist):
    dist = np.maximum(dist, 0)
    exact = BUCKETS // 2
    d = np.maximum(dist, 1).astype(np.float32)
    large = exact + (np.log(d / np.float32(exact)) / np.float32(np.log(MAX_DIST / exact))
                     * np.float32(BUCKETS - exact)).astype(np.int32)
    return np.where(dist < exact, dist, np.minimum(large, BUCKETS - 1))


OH0 = CMP_STRIDE * (NC16 - 1) + CMP_LEN - 1


def shape_tables():
    def onehot(dist):
        t = np.zeros((BUCKETS + 1, dist.size), np.float32)
        t[t5_bucket(dist), np.arange(dist.size)] = 1.0
        t[BUCKETS] = np.where(dist < 0, np.float32(NEG), 0)
        return t
    oh = onehot(np.arange(OH0 + S) - OH0)
    ohr = onehot(S - 1 - np.arange(384))
    ident = np.eye(P, dtype=np.float32)
    pos = np.arange(S, dtype=np.float32)
    half = RQ // 2
    inv = (np.float32(10000.0) ** (-np.arange(half, dtype=np.float32) / np.float32(half))).astype(np.float32)
    ang = (pos[:, None] * inv[None, :]).astype(np.float32)
    cos, sin = np.cos(ang).astype(np.float32), np.sin(ang).astype(np.float32)
    rot = np.stack([np.concatenate([cos, cos], 1), np.concatenate([-sin, sin], 1)], 1)
    rot = rot.reshape(TT, P, 2, RQ).transpose(1, 0, 2, 3).reshape(P, -1)
    logg = np.log(1.0 - 2.0 ** (-5.0 - np.arange(RH)))
    diff = np.arange(S)[None, :] - np.arange(P)[:, None]
    dec = np.where(diff[None] >= 0, np.exp(np.maximum(diff, 0)[None] * logg[:, None, None]), 0) * RQ ** -0.5
    dec = dec.transpose(1, 0, 2).astype(np.float32).reshape(P, -1)
    t = np.arange(S)
    mc = (t[:, None] - (np.arange(NC16) * CMP_STRIDE + CMP_LEN - 1)[None, :] >= 0).astype(np.float32)
    mc = mc.reshape(TT, P, NC16).transpose(1, 0, 2).reshape(P, -1)
    hm = (np.arange(P)[:, None] // NC16 == np.arange(HEADS)[None, :]).astype(np.float32)
    io = np.broadcast_to(np.arange(NE, dtype=np.float32), (P, NE))
    tri = (np.arange(P)[:, None] < np.arange(P)[None, :]).astype(np.float32)
    fold = np.tile(np.eye(C, dtype=np.float32), (P // C, 1))
    packed = np.concatenate([ident, ident[::-1], mc, hm, io, rot, dec, tri, fold], 1)
    return dict(oh=oh, ohr=ohr, packed=np.ascontiguousarray(packed))


C_ID, C_J = 0, P
C_MC = 2 * P
C_HM = C_MC + TT * NC16
C_IO = C_HM + HEADS
C_ROT = C_IO + NE
C_DEC = C_ROT + TT * 2 * RQ
C_TRI = C_DEC + RH * S
C_FOLD = C_TRI + P
C_END = C_FOLD + C


BLOCKS = ["kv0", "kv1", "q", "qr", "kr", "w1k", "vr0", "w1v", "vr1", "gr0", "gr1",
          "ga0", "ga1", "gb0", "gb1", "upn", "upr0", "upr1", "out0", "out1"]

JOBS = (["vecT"] + [f"xT{i}" for i in range(4)]
        + ["btab", "bcmp", "kvcT", "ksT", "vs", "kwT", "vwg", "qT0", "qT1", "U0", "U1", "U2", "U3", "qr0", "qr1"]
        + ["S0.0", "S1.0", "S0.1", "S1.1", "kr0", "kr1", "S0.2", "S1.2", "S0.3", "S1.3", "hidk", "vr00", "vr01", "hidv"]
        + ["PT0.0", "PT0.1", "PT1.0", "PT1.1", "vr10", "vr11", "cmpkv", "PT2.0", "PT2.1", "PT3.0", "PT3.1"]
        + ["S0.4", "S1.4", "S0.5", "S1.5", "Sc", "gr00", "gr01", "PcT", "S0.6", "S1.6", "S0.7", "S1.7", "PV0", "PV1"]
        + ["gr10", "gr11", "PT4.0", "PT4.1", "PT5.0", "PT5.1", "rTq0", "rTq1", "rTk0", "rTk1", "PV2"]
        + ["PT6.0", "PT6.1", "PT7.0", "PT7.1", "ga0", "PV3", "ST0", "ST1", "ST2", "ST3", "ga1", "ga2", "ga3"]
        + ["Y00", "Y01", "gb0", "Y10", "Y11", "gb1", "gb2", "gb3"]
        + [f"yrT{i}" for i in range(4)] + [f"up{i}" for i in range(8)] + [f"out{i}" for i in range(4)]
        + [f"x2T{i}" for i in range(4)] + ["route", "pos"])
STEP = [("G0", 0), ("G1", 1), ("WT", 2), ("GU0", 3), ("GU1", 0), ("T0", 1), ("GU2", 2), ("T1", 3), ("GU3", 0),
        ("T2", 1), ("T3", 2), ("O0", 3), ("O1", 0)]
STEP_N = [sum(b == i for _, b in STEP) for i in range(4)]
STEP_AT = {j: (b, sum(b == c for _, c in STEP[:i])) for i, (j, b) in enumerate(STEP)}
NBANK = 8
LAST_N = [len(range(b, len(JOBS), NBANK)) for b in range(NBANK)]
PLACE = {j: (i % NBANK, i // NBANK) for i, j in enumerate(JOBS)}
LAST_USE = dict(kv0="vs", kv1="vwg", q="qT1", qr="qr1", kr="kr1", w1k="hidk", w1v="hidv", vr0="vr01", vr1="vr11",
                gr0="gr01", gr1="gr11", ga0="ga1", ga1="ga3", gb0="gb1", gb1="gb3",
                upn="up7", upr0="up7", upr1="up7", out0="out3", out1="out3")


def build(nc, a, out):
    with ExitStack() as ctx:
        def sb(name, shape, dt=F32):
            return ctx.enter_context(nc.sbuf_tensor(name, shape, dt))

        def sem(name):
            return ctx.enter_context(nc.semaphore(name))

        bank = [ctx.enter_context(nc.psum_tensor(f"bank{i}", [P, 512], F32)) for i in range(NBANK)]
        full = [sem(f"full{i}") for i in range(NBANK)]
        emptied = [sem(f"emptied{i}") for i in range(NBANK)]

        def ps(job):
            return bank[PLACE[job][0]]

        def is_full(job):
            b, n = PLACE[job]
            return full[b], n + 1

        def is_emptied(job):
            b, n = PLACE[job]
            return emptied[b], n + 1

        ring = sb("ring", [P, NSLOT * SLOT])
        x = sb("x", [P, TT, D])
        xs = sb("xs", [P, TT, D])
        def region(name, n=2048):
            return sb(name, [P, n])
        pair_a = region("hT_and_y", 4096)
        pair_b = region("vr_and_gr", 4096)
        r_kpad, r_qkT, r_X = region("keys"), region("qkT"), region("windows")
        hT = pair_a[:, 0:2048].rearrange("p (k t) -> p k t", k=KT)
        y = pair_a[:, 2048:4096].rearrange("p (t d) -> p t d", t=TT)
        vr = pair_b[:, 0:2048].rearrange("p (t d) -> p t d", t=TT)
        gr = pair_b[:, 2048:4096].rearrange("p (t d) -> p t d", t=TT)
        cst = sb("cst", [P, C_END])
        oh = sb("oh", [BUCKETS + 1, OH0 + S])
        ohr = sb("ohr", [BUCKETS + 1, 384])
        relb = sb("relb", [BUCKETS + 1, HEADS])
        vecs = sb("vecs", [NVEC, P])
        vecT = sb("vecT_sb", [P, NVEC])
        etab = sb("etab", [HEADS, 384])
        Tb = sb("Tb", [P, HEADS * S])
        qT = sb("qT", [P, PAIRS, S])
        Kpad = r_kpad
        vsel = sb("vsel", [P, TT, P])
        vwin = sb("vwin", [P, TT, P + 24])
        nsa = sb("nsa", [P, 6144])
        qkT = r_qkT[:, :].rearrange("p (s h t) -> p s h t", s=2, h=RH)
        yaT = sb("yaT", [P, PAIRS, S])
        X = r_X[:, 0:1024].rearrange("p (v g t) -> p v g t", v=2, g=GROUPS)
        Xb = r_X[:, 1024:2048].rearrange("p (v l g c) -> p v l g c", v=2, l=CMP_LEN // 2, g=GROUPS)
        w2 = sb("w2", [P, 2, 2, HD])
        hid = sb("hid", [P, 128])
        hid2 = sb("hid2", [P, 128])
        hidv = sb("hidv", [P, 2, P])
        Kc = sb("Kc", [P, GROUPS, 2, NC16])
        Vc = sb("Vc", [P, HEADS, HD])
        bC = sb("bC", [P, TT, HEADS, NC16])
        Pc = sb("Pc", [P, TT, HEADS, NC16])
        PcT = sb("PcT_sb", [P, S])
        sg = sb("sg", [P, TT, 24])
        st = sb("st", [P, 256])
        mneg = sb("mneg", [P, TT, HEADS, 2])
        mx = sb("mx", [P, TT, HEADS, 2])
        sums = sb("sums", [P, TT, HEADS, 2])
        coef = sb("coef", [P, TT, HEADS, 2])
        wr = sb("wr", [P, KT, NG + NE])
        rbias = sb("rbias", [P, NG + NE])
        comb = sb("comb", [P, TT, NE])
        comb1 = sb("member", [P, TT, NE])
        ones = sb("ones", [P, P])
        posm = sb("posm", [P, TT, NE])
        zeros = sb("zeros", [P, P])
        nround = sb("nround", [P, 16])
        nround_i = sb("nround_i", [P, 1], mybir.dt.int32)
        rt = sb("rt", [P, TT, 160])
        ri = sb("ri", [P, TT, 16], U32)
        nffn = yaT[:, :, :].rearrange("p a t -> p (a t)")
        nf = qT[:, :, :].rearrange("p a t -> p (a t)")
        rtmp = yaT[:, 0:2, :].rearrange("p a t -> p (a t)")
        bdram = nc.dram_tensor("bias_rows", (HEADS, 384), F32, kind="Internal").ap()

        ident = cst[:, C_ID:C_ID + P]
        flip = cst[:, C_J:C_J + P]
        maskc = cst[:, C_MC:C_MC + TT * NC16].rearrange("p (t c) -> p t c", t=TT)
        headmask = cst[:, C_HM:C_HM + HEADS]
        tri = cst[:, C_TRI:C_TRI + P]
        fold = cst[:, C_FOLD:C_FOLD + C]
        iota = cst[:, C_IO:C_IO + NE]
        rot = cst[:, C_ROT:C_ROT + TT * 2 * RQ].rearrange("p (t s d) -> p t s d", t=TT, s=2)
        decay = cst[:, C_DEC:C_DEC + RH * S].rearrange("p (h i) -> p h i", h=RH)
        Tt = Tb[:, :].rearrange("p (h j) -> p h j", h=HEADS)
        yrT = Tb[:, :].rearrange("p (k t) -> p k t", k=KT)
        Kp = Kpad[:, :].rearrange("p (g s n) -> p g s n", g=GROUPS, s=2)
        STs = Kpad[:, 0:RH * 384].rearrange("p (h n) -> p h n", h=RH)
        prob = nsa[:, 0:3072].rearrange("p (h b n) -> p h b n", h=4, b=2)
        PT = nsa[:, 3072:6144].rearrange("p (h b n) -> p h b n", h=4, b=2)
        gate = nsa[:, 0:2 * KT * S].rearrange("p (w k t) -> p w k t", w=2, k=KT)
        m0 = nsa[:, 0:4096]
        selG = m0[:, 0:256].rearrange("p (t e s) -> p t e s", t=TT, e=BE)
        selW = m0[:, 256:512].rearrange("p (t e s) -> p t e s", t=TT, e=BE)
        selWT = m0[:, 512:768]
        hg = m0[:, 768:1792].rearrange("p (k s) -> p k s", k=KT)
        gu_sb = m0[:, 1792:2816].rearrange("p (b n) -> p b n", b=2)
        o_sb = m0[:, 2816:3840].rearrange("p (h n) -> p h n", h=2)
        m1 = ring[:, 2 * SLOT:2 * SLOT + 512].rearrange("p (a j f s) -> p a j f s", a=2, j=BE, f=2)
        hide, th_sb = m1[:, 0], m1[:, 1]
        h2T = Tb[:, :].rearrange("p (k t) -> p k t", k=KT)
        U = y[:, :, :].rearrange("p t d -> p (t d)")
        qkr = xs[:, :, :].rearrange("p t (s d) -> p t s d", s=2)

        s_cst, s_vec, s_tab, s_small, s_rw, s_nf = (sem(n) for n in
            ("cst_loaded", "vecs_loaded", "tables_loaded", "small_loaded", "router_loaded", "nf_loaded"))
        s_x = [sem(f"x_loaded{t}") for t in range(TT)]
        s_plg = sem("pool_gelu_chain")
        s_slot = [sem(f"slot_loaded{i}") for i in range(NSLOT)]
        s_U = [sem(f"bias_rows_loaded{h}") for h in range(HEADS)]
        s_brow, s_out = sem("bias_rows_stored"), sem("out_stored")
        s_ms, s_pl = sem("memsets_done"), sem("pool_chain")
        s_dv = sem("vector_chain")
        s_ac = sem("scalar_chain")
        s_xs = sem("xs_ready")
        s_rs, s_rstd = sem("variance_ready"), sem("rstd_ready")
        s_neg, s_exp, s_prob = sem("negmax_ready"), sem("exp_done"), sem("prob_ready")
        s_garg, s_th, s_hid = sem("gelu_arg"), sem("gelu_tanh"), sem("hidden_ready")
        s_Xb = sem("cmp_blocks_ready")
        s_cm, s_ce, s_pc = sem("cmp_max"), sem("cmp_exp"), sem("cmp_prob_ready")
        s_sg, s_sgv = sem("branch_gates_tanh"), sem("branch_gates_ready")
        s_rot = sem("rotary_done")
        s_gt, s_G = sem("swish_tanh"), sem("swish_ready")
        s_y = sem("ret_y_ready")
        s_mrg = sem("merged_ready")
        s_rm, s_re, s_comb = sem("router_args"), sem("router_exps"), sem("combine_ready")
        s_gu = [sem(f"gate_up_loaded{j}") for j in range(BE)]
        s_dw = [sem(f"down_loaded{j}") for j in range(BE)]
        s_nffn, s_h2, s_nr = sem("ffn_norm_loaded"), sem("expert_input_ready"), sem("rounds_ready")
        s_sel, s_tanh, s_added = sem("selection_ready"), sem("expert_tanh"), sem("batch_added")
        s_selg, s_shift = sem("selection_chain"), sem("slots_shifted")
        s_hch = sem("expert_vector_chain")
        s_M, s_seed, s_sum, s_fsq = sem("membership_ready"), sem("sums_seeded"), sem("sums_complete"), sem("final_squares")
        s_fin = sem("final_ready")

        def slot(block):
            i = BLOCKS.index(block)
            return ring[:, (i % NSLOT) * SLOT:(i % NSLOT + 1) * SLOT]

        def loaded(block):
            i = BLOCKS.index(block)
            return s_slot[i % NSLOT], 16 * (i // NSLOT + 1)

        def cols(block, n):
            return slot(block)[:, 0:KT * n].rearrange("p (k n) -> p k n", k=KT)

        w_in = a["w_in"][0].rearrange("(k p) n -> p k n", p=P)
        SRC = {
            "kv0": (w_in[:, :, 512:1024], 512), "kv1": (w_in[:, :, 1024:1304], 280), "q": (w_in[:, :, 0:512], 512),
            "qr": (w_in[:, :, 1304:1816], 512), "kr": (w_in[:, :, 1816:2328], 512),
            "vr0": (w_in[:, :, 2328:2840], 512), "vr1": (w_in[:, :, 2840:3352], 512),
            "gr0": (w_in[:, :, 3352:3864], 512), "gr1": (w_in[:, :, 3864:4376], 512),
            "ga0": (w_in[:, :, 4376:4888], 512), "ga1": (w_in[:, :, 4888:5400], 512),
            "gb0": (w_in[:, :, 5400:5912], 512), "gb1": (w_in[:, :, 5912:6424], 512),
        }
        for nm, src in (("w1k", "cmp_k_w1"), ("w1v", "cmp_v_w1")):
            SRC[nm] = (a[src][0].rearrange("(k p) n -> p k n", p=P), None)
        SRC["upn"] = (a["w_nsa_up"][0].rearrange("(k p) n -> p k n", p=P), None)
        for i in range(2):
            SRC[f"upr{i}"] = (a["w_ret_up"][0].rearrange("(k p) n -> p k n", p=P)[:, 4 * i:4 * i + 4, :], None)
            SRC[f"out{i}"] = (a["w_out"][0].rearrange("(k p) n -> p k n", p=P)[:, 4 * i:4 * i + 4, :], None)

        GU = [b.rearrange("p (k w f) -> p k w f", k=KT, w=2)
              for b in (pair_b[:, :], pair_a[:, :], ring[:, 0:SLOT], ring[:, SLOT:2 * SLOT])]
        DW = [b.rearrange("p (k n) -> p k n", k=2) for b in (r_X[:, :], r_qkT[:, :], nsa[:, 4096:6144], r_kpad[:, :])]

        def step_full(job, n):
            b, i = STEP_AT[job]
            return full[b], n * STEP_N[b] + (LAST_N[b] + i + 1)

        def step_out(job, n):
            b, i = STEP_AT[job]
            return emptied[b], n * STEP_N[b] + (LAST_N[b] + i + 1)

        def rounds(eng, body):
            eng.wait_ge(s_nr, 1)
            left = eng.value_load(nround_i[0:1, 0:1], min_val=1, max_val=ROUNDS)
            with eng.Fori(0, ROUNDS) as r:
                with eng.If(r < left):
                    body(r)

        block = ctx.enter_context(nc.Block())

        @block.sync
        def _(sp):
            for t in range(TT):
                sp.dma_start(x[:, t, :], a["x"][0, t * P:(t + 1) * P, :]).then_inc(s_x[t], 16)
            sp.dma_start(cst[:, :], a["packed"]).then_inc(s_cst, 16)

            def load(bi):
                b = BLOCKS[bi]
                if bi >= NSLOT:
                    sp.wait_ge(*is_full(LAST_USE[BLOCKS[bi - NSLOT]]))
                src, n = SRC[b]
                dst = cols(b, n) if n else slot(b).rearrange("p (k n) -> p k n", k=src.shape[1])
                sp.dma_start(dst, src).then_inc(loaded(b)[0], 16)

            for bi in range(4):
                load(bi)
            sp.wait_ge(*is_emptied("btab"))
            sp.dma_start(bdram, etab[:, :]).then_inc(s_brow, 16)
            sp.wait_ge(s_brow, 16)
            for h in range(HEADS):
                src = bass.AP(bdram.tensor, h * 384, [[1, P], [1, S]])
                sp.dma_start(U[:, h * S:(h + 1) * S], src).then_inc(s_U[h], 16)
            gate_v = a["moe_w_gate"][0].rearrange("e (k p) f -> e p k f", p=P)
            up_v = a["moe_w_up"][0].rearrange("e (k p) f -> e p k f", p=P)
            down_v = a["moe_w_down"][0].rearrange("e (k p) n -> e p k n", p=P)

            def load_gu(j, e):
                for w, v in enumerate((gate_v, up_v)):
                    sp.dma_start(GU[j][:, :, w, :], v[j:NE - BE + j + 1][bass.ds(e, 1)].rearrange("e p k f -> (e p) k f")).then_inc(s_gu[j], 16)

            def load_dw(j, e):
                sp.dma_start(DW[j], down_v[j:NE - BE + j + 1][bass.ds(e, 1)].rearrange("e p k n -> (e p) k n")).then_inc(s_dw[j], 16)

            for bi in range(4, BLOCKS.index("upr1") + 1):
                load(bi)
            load_dw(0, 0)
            load_dw(1, 0)
            sp.wait_ge(*is_full("Y11"))
            load_dw(2, 0)
            load_dw(3, 0)
            load(BLOCKS.index("out0"))
            sp.wait_ge(s_y, TT)
            load_gu(0, 0)
            sp.wait_ge(*is_full("yrT3"))
            load_gu(1, 0)
            load(BLOCKS.index("out1"))
            load_gu(2, 0)
            load_gu(3, 0)

            def vec(dst, src, s):
                sp.dma_start(dst, src.rearrange("(a n) -> a n", a=1).broadcast_to((P, D))).then_inc(s, 16)
            vec(nffn, a["norm_ffn"][0], s_nffn)
            vec(nf, a["norm_final"], s_nf)

            def next_batches(n0):
                with sp.Fori(0, NB - 1) as b:
                    for j in range(BE):
                        sp.wait_ge(*step_full(f"GU{j}", n0 + b))
                        load_gu(j, b * BE + BE)
                    for j in range(BE):
                        sp.wait_ge(*step_full("O1", n0 + b))
                        load_dw(j, b * BE + BE)
            next_batches(0)
            sp.wait_ge(s_nr, 1)
            left = sp.value_load(nround_i[0:1, 0:1], min_val=1, max_val=ROUNDS)
            with sp.Fori(1, ROUNDS) as r:
                with sp.If(r < left):
                    for j in range(BE):
                        sp.wait_ge(*step_full(f"GU{j}", r * NB - 1))
                        load_gu(j, 0)
                    for j in range(BE):
                        sp.wait_ge(*step_full("O1", r * NB - 1))
                        load_dw(j, 0)
                    next_batches(r * NB)
            for t in range(TT):
                for n in range(2):
                    sp.wait_ge(s_fin, 2 * t + n + 1)
                    sp.dma_start(out[0, t * P:(t + 1) * P, n * 512:(n + 1) * 512], x[:, t, n * 512:(n + 1) * 512]).then_inc(s_out, 16)
            sp.wait_ge(s_out, 64)

        @block.gpsimd
        def _(pool):
            pool.memset(relb[:, :], 1.0)
            pool.memset(Kpad[:, :], 0.0)
            pool.memset(X[:, :, :, :], 0.0)
            pool.memset(Xb[:, :, :, :, :], 0.0)
            pool.memset(Kc[:, :, :, :], 0.0)
            pool.memset(rt[:, :, :], -3e38)
            pool.memset(zeros[:, :], 0.0)
            pool.memset(ones[:, :], 1.0)
            pool.memset(st[:, 250:251], -0.5).then_inc(s_ms, 1)
            pool.wait_ge(s_ms, 1)
            pool.dma_start(vecs[0:8, :], a["norm_mix"][0].rearrange("(k p) -> k p", p=P)).then_inc(s_vec, 16)
            pool.dma_start(vecs[8:16, :], a["norm_ffn"][0].rearrange("(k p) -> k p", p=P)).then_inc(s_vec, 16)
            pool.dma_start(vecs[16:24, :], a["ret_norm"][0].rearrange("(k p) -> k p", p=P)).then_inc(s_vec, 16)
            pool.dma_start(oh[:, :], a["oh"]).then_inc(s_tab, 16)
            pool.dma_start(ohr[:, :], a["ohr"]).then_inc(s_tab, 16)
            pool.dma_start(relb[0:BUCKETS, :], a["rel_bias"]).then_inc(s_tab, 16)
            for i, nm in enumerate(("cmp_pos_k", "cmp_pos_v")):
                pool.dma_start(vecs[24 + 16 * i:40 + 16 * i, :],
                               a[nm][0].rearrange("(l two) d -> l (two d)", two=2)).then_inc(s_vec, 16)
            for i, nm in enumerate(("cmp_k_w2", "cmp_v_w2")):
                pool.dma_start(w2[:, i, :, :], a[nm][0].rearrange("(k p) d -> p k d", p=P)).then_inc(s_small, 16)
            pool.dma_start(wr[:, :, 0:NG], a["w_router_group"][0].rearrange("(k p) g -> p k g", p=P)).then_inc(s_rw, 16)
            pool.dma_start(wr[:, :, NG:NG + NE], a["w_router_expert"][0].rearrange("(k p) g -> p k g", p=P)).then_inc(s_rw, 16)
            pool.dma_start(rbias[:, 0:NG], a["b_router_group"].broadcast_to((P, NG))).then_inc(s_rw, 16)
            pool.dma_start(rbias[:, NG:NG + NE], a["b_router_expert"].broadcast_to((P, NE))).then_inc(s_rw, 16)
            def rstd(n, col):
                pool.wait_ge(s_rs, n)
                pool.tensor_tensor(st[:, col + 32:col + 34], st[:, col:col + 2],
                                   st[:, 250:251].broadcast_to((P, 2)), ALU.pow).then_inc(s_rstd, 1)
            rstd(1, 0)
            pool.wait_ge(*is_emptied("kvcT"))
            pool.wait_ge(*is_emptied("vecT"))
            for i in range(2):
                for g in range(GROUPS):
                    win = X[:, i, g, :].rearrange("p (c u two) -> p u c two", u=8, two=2)
                    for hi in range(2):
                        ins = pool.tensor_tensor(Xb[:, i, 8 * hi:8 * hi + 8, g, 0:NCMP], win[:, :, hi:hi + NCMP, 0],
                                                 vecT[:, 24 + 16 * i + 8 * hi:32 + 16 * i + 8 * hi].unsqueeze(2).broadcast_to((P, 8, NCMP)), ALU.add)
            ins.then_inc(s_Xb, 1)

            k = [0]

            def link(ins):
                k[0] += 1
                ins.then_inc(s_plg, 1)
                pool.wait_ge(s_plg, k[0])
            pool.wait_ge(*is_emptied("hidk"))
            pool.wait_ge(*is_emptied("hidv"))
            link(pool.tensor_tensor(hid2[:, :], hid[:, :], hid[:, :], ALU.mult))
            link(pool.tensor_scalar(hid2[:, :], hid2[:, :], 0.044715, 1.0, ALU.mult, ALU.add))
            pool.tensor_tensor(hid2[:, :], hid2[:, :], hid[:, :], ALU.mult).then_inc(s_garg, 1)
            pool.wait_ge(s_th, 1)
            link(pool.tensor_scalar(hid2[:, :], hid2[:, :], 1.0, 1.0, ALU.mult, ALU.add))
            link(pool.tensor_tensor(hid2[:, :], hid2[:, :], hid[:, :], ALU.mult))
            for n in range(2):
                for g in range(GROUPS):
                    c0 = 64 + n * 32 + g * 16
                    ins = pool.tensor_copy(hidv[:, n, g * 64:(g + 1) * 64].rearrange("p (h c) -> p h c", h=4),
                                           hid2[:, c0:c0 + 16].unsqueeze(1).broadcast_to((P, 4, 16)))
            ins.then_inc(s_hid, 1)
            for i in range(4):
                rstd(2 + i, 8 + 4 * i)
            rstd(6, 4)
            rstd(7, 6)

        @block.tensor
        def _(pe):
            def begin(job):
                b, n = PLACE[job]
                if n > 0:
                    pe.wait_ge(emptied[b], n)
                return bank[b]

            def done(job, ins):
                ins.then_inc(full[PLACE[job][0]], 1)

            def have(*jobs):
                for j in jobs:
                    pe.wait_ge(*is_emptied(j))

            def mm(o, l, r, s, e):
                return nc.tensor.matmul(o, l, r, start=s, stop=e)

            def features(job, block, c0s, n=512):
                o = begin(job)
                pe.wait_ge(*loaded(block))
                for i, c0 in enumerate(c0s):
                    for k in range(KT):
                        ins = mm(o[:, i * S:(i + 1) * S], cols(block, n)[:, k, c0:c0 + P], hT[:, k, :], k == 0, k == KT - 1)
                done(job, ins)

            def tokens(job, block, ts, c0, w, n=512):
                o = begin(job)
                pe.wait_ge(*loaded(block))
                for i, t in enumerate(ts):
                    for k in range(KT):
                        ins = mm(o[:, i * w:(i + 1) * w], hT[:, k, t * P:(t + 1) * P], cols(block, n)[:, k, c0:c0 + w],
                                 k == 0, k == KT - 1)
                done(job, ins)

            def transposes(job, srcs):
                o = begin(job)
                for i, s in enumerate(srcs):
                    ins = nc.tensor.transpose(o[:, i * P:(i + 1) * P], s, ident)
                done(job, ins)

            def norm_transposes(pre, n_ready):
                pe.wait_ge(s_xs, n_ready)
                for i in range(4):
                    transposes(f"{pre}{i}", [xs[:, t, k * P:(k + 1) * P] for k in (2 * i, 2 * i + 1) for t in range(TT)])

            def scores(t, h):
                j = f"S{t}.{h}"
                o = begin(j)
                w = (t + 1) * P
                for b in range(2):
                    ins = mm(o[:, b * S:b * S + w], qT[:, h // 2, t * P:(t + 1) * P],
                             Kp[:, h // 4, h % 2, b * S:b * S + w], True, True)
                done(j, ins)

            def prob_transposes(h):
                pe.wait_ge(s_prob, h + 1)
                for b in range(2):
                    transposes(f"PT{h}.{b}", [prob[:, h % 4, b, i * P:(i + 1) * P] for i in range(3)])

            def attend(pr):
                j = f"PV{pr}"
                have(*[f"PT{2 * pr + i}.{b}" for i in range(2) for b in range(2)])
                o = begin(j)
                g = pr // 2
                for i in range(2):
                    h = 2 * pr + i
                    oo = o[i * HD:(i + 1) * HD, :]
                    for b, v in ((0, vsel), (1, vwin)):
                        pt = PT[:, h % 4, b, :]
                        mm(oo[:, 0:S], v[:, 0, g * HD:(g + 1) * HD], pt[:, 0:S], b == 0, False)
                        mm(oo[:, P:S], v[:, 1, g * HD:(g + 1) * HD], pt[:, S:384], False, False)
                    ins = mm(oo[:, 0:S], Vc[:, h, :], PcT[:, :], False, True)
                done(j, ins)

            o = begin("vecT")
            pe.wait_ge(s_cst, 16)
            pe.wait_ge(s_vec, 80)
            done("vecT", nc.tensor.transpose(o[:, 0:NVEC], vecs[:, :], ident[0:NVEC, 0:NVEC]))
            norm_transposes("xT", TT)
            pe.wait_ge(s_tab, 48)
            o = begin("btab")
            done("btab", mm(o[0:HEADS, 0:384], relb[:, :], ohr[:, :], True, True))
            o = begin("bcmp")
            for t in range(TT):
                for c in range(NC16):
                    a0 = OH0 + t * P - (c * CMP_STRIDE + CMP_LEN - 1)
                    n0 = (t * NC16 + c) * HEADS
                    ins = mm(o[:, n0:n0 + HEADS], oh[:, a0:a0 + P], relb[:, :], True, True)
            done("bcmp", ins)
            have(*[f"xT{i}" for i in range(4)])
            features("kvcT", "kv0", (0, 128))
            features("ksT", "kv0", (256,))
            tokens("vs", "kv0", (0, 1), 384, 128)
            features("kwT", "kv1", (0,), 280)
            tokens("vwg", "kv1", (0, 1), 128, 152, 280)
            features("qT0", "q", (0, 128))
            features("qT1", "q", (256, 384))
            for i in range(HEADS):
                pe.wait_ge(s_U[i], 16)
            for i in range(4):
                o = begin(f"U{i}")
                done(f"U{i}", mm(o[:, :], flip, U[:, i * 512:(i + 1) * 512], True, True))
            tokens("qr0", "qr", (0,), 0, 512)
            tokens("qr1", "qr", (1,), 0, 512)
            have("qT0", "qT1", "ksT", "kwT")
            for h in range(2):
                scores(0, h)
                scores(1, h)
            tokens("kr0", "kr", (0,), 0, 512)
            tokens("kr1", "kr", (1,), 0, 512)
            for h in range(2, 4):
                scores(0, h)
                scores(1, h)
            def compress_hidden(i, block):
                j = "hid" + "kv"[i]
                o = begin(j)
                pe.wait_ge(*loaded(block))
                w = slot(block).rearrange("p (l n) -> p l n", l=16)
                for n in range(2):
                    for l in range(16):
                        ins = mm(o[:, n * 32:(n + 1) * 32], w[:, l, n * P:(n + 1) * P],
                                 Xb[:, i, l, :, :].rearrange("p g c -> p (g c)"), l == 0, l == 15)
                done(j, ins)
            pe.wait_ge(s_Xb, 1)
            compress_hidden(0, "w1k")
            tokens("vr00", "vr0", (0,), 0, 512)
            tokens("vr01", "vr0", (1,), 0, 512)
            compress_hidden(1, "w1v")
            prob_transposes(0)
            prob_transposes(1)
            tokens("vr10", "vr1", (0,), 0, 512)
            tokens("vr11", "vr1", (1,), 0, 512)
            o = begin("cmpkv")
            pe.wait_ge(s_small, 32)
            pe.wait_ge(s_hid, 1)
            for r in range(2):
                for n in range(2):
                    mm(o[r * HD:(r + 1) * HD, 0:32], w2[:, 0, n, :], hid2[:, n * 32:(n + 1) * 32], n == 0, n == 1)
            for n in range(2):
                ins = mm(o[:, 64:128], hidv[:, n, :], w2[:, 1, n, :], n == 0, n == 1)
            done("cmpkv", ins)
            prob_transposes(2)
            prob_transposes(3)
            for h in range(4, 6):
                scores(0, h)
                scores(1, h)
            have("cmpkv")
            o = begin("Sc")
            for t in range(TT):
                for pr in range(PAIRS):
                    ins = mm(o[:, t * P + pr * 32:t * P + pr * 32 + 32], qT[:, pr, t * P:(t + 1) * P],
                             Kc[:, pr // 2, :, :].rearrange("p a c -> p (a c)"), True, True)
            done("Sc", ins)
            tokens("gr00", "gr0", (0,), 0, 512)
            tokens("gr01", "gr0", (1,), 0, 512)
            pe.wait_ge(s_pc, 1)
            transposes("PcT", [Pc[:, t, :, :].rearrange("p h c -> p (h c)") for t in range(TT)])
            for h in range(6, 8):
                scores(0, h)
                scores(1, h)
            have("vs", "vwg", "PcT")
            attend(0)
            attend(1)
            tokens("gr10", "gr1", (0,), 0, 512)
            tokens("gr11", "gr1", (1,), 0, 512)
            prob_transposes(4)
            prob_transposes(5)
            for s, nm in enumerate("qk"):
                for t in range(TT):
                    pe.wait_ge(*is_emptied(f"{nm}r{t}"))
                    transposes(f"rT{nm}{t}", [qkr[:, t, s, h * P:(h + 1) * P] for h in range(RH)])
            attend(2)
            prob_transposes(6)
            prob_transposes(7)
            features("ga0", "ga0", (0, 128))
            attend(3)
            have("rTq0", "rTq1", "rTk0", "rTk1")
            for h in range(RH):
                o = begin(f"ST{h}")
                mm(o[:, 0:S], qkT[:, 1, h, 0:P], qkT[:, 0, h, :], True, True)
                done(f"ST{h}", mm(o[:, S:384], qkT[:, 1, h, P:S], qkT[:, 0, h, P:S], True, True))
            features("ga1", "ga0", (256, 384))
            features("ga2", "ga1", (0, 128))
            features("ga3", "ga1", (256, 384))

            def retain(t, hp):
                j = f"Y{t}{hp}"
                o = begin(j)
                for i in range(2):
                    h = 2 * hp + i
                    oo = o[:, i * RV:(i + 1) * RV]
                    ins = mm(oo, STs[:, h, t * P:(t + 1) * P], vr[:, 0, h * RV:(h + 1) * RV], True, t == 0)
                    if t == 1:
                        ins = mm(oo, STs[:, h, S:384], vr[:, 1, h * RV:(h + 1) * RV], False, True)
                done(j, ins)
            have(*[f"ST{h}" for h in range(RH)])
            have("vr00", "vr01", "vr10", "vr11")
            retain(0, 0)
            retain(0, 1)
            features("gb0", "gb0", (0, 128))
            retain(1, 0)
            retain(1, 1)
            features("gb1", "gb0", (256, 384))
            features("gb2", "gb1", (0, 128))
            features("gb3", "gb1", (256, 384))
            pe.wait_ge(s_y, TT)
            for i in range(4):
                transposes(f"yrT{i}", [y[:, t, k * P:(k + 1) * P] for k in (2 * i, 2 * i + 1) for t in range(TT)])
            have(*[f"PV{i}" for i in range(4)])
            have(*[f"yrT{i}" for i in range(4)])
            for b in ("upn", "upr0", "upr1"):
                pe.wait_ge(*loaded(b))
            wn = slot("upn").rearrange("p (k n) -> p k n", k=4)
            for i in range(KT):
                o = begin(f"up{i}")
                for k in range(4):
                    mm(o[:, 0:S], wn[:, k, i * P:(i + 1) * P], yaT[:, k, :], k == 0, k == 3)
                for k in range(KT):
                    w = slot(f"upr{k // 4}").rearrange("p (k n) -> p k n", k=4)
                    ins = mm(o[:, S:2 * S], w[:, k % 4, i * P:(i + 1) * P], yrT[:, k, :], k == 0, k == KT - 1)
                done(f"up{i}", ins)
            for b in ("out0", "out1"):
                pe.wait_ge(*loaded(b))
            pe.wait_ge(s_mrg, KT)
            for t in range(TT):
                for n in range(2):
                    o = begin(f"out{2 * t + n}")
                    for k in range(KT):
                        w = slot(f"out{k // 4}").rearrange("p (k n) -> p k n", k=4)
                        ins = mm(o[:, :], gate[:, 0, k, t * P:(t + 1) * P], w[:, k % 4, n * 512:(n + 1) * 512],
                                 k == 0, k == KT - 1)
                    done(f"out{2 * t + n}", ins)
            norm_transposes("x2T", 2 * TT)
            have(*[f"x2T{i}" for i in range(4)])
            pe.wait_ge(s_rw, 64)
            o = begin("route")
            for t in range(TT):
                for k in range(KT):
                    ins = mm(o[:, t * 36:(t + 1) * 36], h2T[:, k, t * P:(t + 1) * P], wr[:, k, :], k == 0, k == KT - 1)
            done("route", ins)

            o = begin("pos")
            pe.wait_ge(s_M, 1)
            mm(o[:, 0:NE], tri, comb1[:, 0, :], True, True)
            mm(o[:, NE:2 * NE], tri, comb1[:, 1, :], True, False)
            mm(o[:, NE:2 * NE], ones[:, :], comb1[:, 0, :], False, True)
            for t in range(TT):
                ins = mm(o[:, 2 * NE:3 * NE], ones[:, :], comb1[:, t, :], t == 0, t == 1)
            done("pos", ins)
            for b in range(NBANK):
                pe.wait_ge(emptied[b], LAST_N[b])

            def add(q, l, r, s, e, w=512):
                return nc.tensor.matmul(bank[4 + q][:, 0:w], l, r, start=s, stop=e, skip_group_check=True)
            for q in range(4):
                add(q, ident, x[:, q // 2, (q % 2) * 512:(q % 2 + 1) * 512], True, False)

            def batch(n):
                def start(job):
                    b, i = STEP_AT[job]
                    pe.wait_ge(emptied[b], n * STEP_N[b] + (LAST_N[b] + i))
                    return bank[b]

                def end(job, ins):
                    ins.then_inc(full[STEP_AT[job][0]], 1)

                pe.wait_ge(s_sel, n + 1)
                for h in range(2):
                    o = start(f"G{h}")
                    for k in range(4):
                        for t in range(TT):
                            ins = mm(o[:, k * P:(k + 1) * P], xs[:, t, (4 * h + k) * P:(4 * h + k + 1) * P],
                                     selG[:, t, :, :].rearrange("p e s -> p (e s)"), t == 0, t == 1)
                    end(f"G{h}", ins)
                o = start("WT")
                for t in range(TT):
                    ins = nc.tensor.transpose(o[:, t * P:(t + 1) * P], selW[:, t, :, :].rearrange("p e s -> p (e s)"), ident)
                end("WT", ins)

                def gate_up(j):
                    pe.wait_ge(s_gu[j], n * 32 + 32)
                    o = start(f"GU{j}")
                    for kk in range(2):
                        for c in range(4):
                            k = 4 * kk + c
                            ins = mm(o[c * C:(c + 1) * C, :], hg[:, k, j * C:(j + 1) * C],
                                     GU[j][:, k, :, :].rearrange("p w f -> p (w f)"), kk == 0, kk == 1)
                    end(f"GU{j}", ins)

                def turn(j):
                    pe.wait_ge(*step_out(f"GU{j}", n))
                    o = start(f"T{j}")
                    for q in range(4):
                        ins = mm(o[:, q * C:(q + 1) * C], gu_sb[:, j % 2, q * P:(q + 1) * P], fold, True, True)
                    end(f"T{j}", ins)

                pe.wait_ge(*step_out("G0", n))
                pe.wait_ge(*step_out("G1", n))
                gate_up(0)
                gate_up(1)
                turn(0)
                gate_up(2)
                turn(1)
                gate_up(3)
                turn(2)
                turn(3)
                for j in range(BE):
                    pe.wait_ge(s_dw[j], n * 16 + 16)
                for j in range(BE):
                    pe.wait_ge(*step_out(f"T{j}", n))
                for h in range(2):
                    o = start(f"O{h}")
                    for f in range(2):
                        for j in range(BE):
                            ins = mm(o[j * C:(j + 1) * C, :], hide[:, j, f, :], DW[j][:, f, h * 512:(h + 1) * 512], f == 0, f == 1)
                    end(f"O{h}", ins)
                pe.wait_ge(*step_out("WT", n))
                for h in range(2):
                    pe.wait_ge(*step_out(f"O{h}", n))
                    for t in range(TT):
                        ins = add(2 * t + h, selWT[:, t * P:(t + 1) * P], o_sb[:, h, :], False, False)
                ins.then_inc(s_added, 1)

            def one_round(r):
                with pe.Fori(0, NB) as b:
                    batch(r * NB + b)
            rounds(pe, one_round)
            for q in range(4):
                ins = add(q, zeros[:, :], zeros[:, 0:1], False, True, 1)
            ins.then_inc(s_sum, 1)

        @block.scalar
        def _(act):
            def take(job):
                act.wait_ge(*is_full(job))
                return ps(job)

            def freed(job, ins):
                ins.then_inc(emptied[PLACE[job][0]], 1)

            def norm_cols(pre, i, c0):
                o = take(f"{pre}{i}")
                act.wait_ge(*is_emptied("vecT"))
                for j in range(2):
                    k = 2 * i + j
                    ins = nc.scalar.activation(hT[:, k, :], o[:, j * S:(j + 1) * S], ACT.Copy, scale=vecT[:, c0 + k:c0 + k + 1])
                freed(f"{pre}{i}", ins)

            def copy(job, dst, src, scale=1.0):
                freed(job, nc.scalar.activation(dst, src, ACT.Copy, scale=scale))

            o = take("vecT")
            copy("vecT", vecT[:, :], o[:, 0:NVEC])
            norm_cols("xT", 1, 0)
            norm_cols("xT", 3, 0)
            o = take("btab")
            copy("btab", etab[:, :], o[0:HEADS, 0:384])
            o = take("vs")
            copy("vs", vsel[:, :, :], o[:, 0:2 * P].rearrange("p (t d) -> p t d", t=TT))
            o = take("vwg")
            copy("vwg", vwin[:, :, :], o[:, 0:304].rearrange("p (t d) -> p t d", t=TT))
            act.wait_ge(*is_emptied("vwg"))
            nc.scalar.activation(sg[:, :, :], vwin[:, :, P:P + 24], ACT.Tanh, scale=0.5).then_inc(s_sg, 1)
            for i in range(2):
                o = take(f"qT{i}")
                copy(f"qT{i}", qT[:, 2 * i:2 * i + 2, :], o[:, :].rearrange("p (a t) -> p a t", a=2), HD ** -0.5)
            for i in range(4):
                o = take(f"U{i}")
                copy(f"U{i}", Tb[:, i * 512:(i + 1) * 512], o[:, :])

            def exps(h):
                act.wait_ge(s_neg, h + 1)
                for t in range(TT):
                    for b in range(2):
                        p = prob[:, h % 4, b, t * P:(2 * t + 1) * P] if t == 0 else prob[:, h % 4, b, P:384]
                        ins = nc.scalar.activation(p, p, ACT.Exp, bias=mneg[:, t, h, b:b + 1],
                                                   accum_out=sums[:, t, h, b:b + 1])
                ins.then_inc(s_exp, 1)

            def probs_out(h):
                for b in range(2):
                    o = take(f"PT{h}.{b}")
                    if h >= 4:
                        act.wait_ge(*is_full(f"PV{(h - 4) // 2}"))
                    copy(f"PT{h}.{b}", PT[:, h % 4, b, :], o[:, 0:384])

            def swish(t, n):
                o = take(f"gr{n}{t}")
                nc.scalar.activation(gr[:, t, n * 512:(n + 1) * 512], o[:, :], ACT.Tanh, scale=0.5).then_inc(s_gt, 1)

            exps(0)
            exps(1)
            o = take("hidk")
            copy("hidk", hid[:, 0:64], o[:, 0:64])
            exps(2)
            exps(3)
            for t in range(TT):
                o = take(f"vr0{t}")
                copy(f"vr0{t}", vr[:, t, 0:512], o[:, :])
            o = take("hidv")
            copy("hidv", hid[:, 64:128], o[:, 0:64])
            act.wait_ge(s_garg, 1)
            nc.scalar.activation(hid2[:, :], hid2[:, :], ACT.Tanh, scale=0.7978845608028654).then_inc(s_th, 1)
            probs_out(0)
            probs_out(1)
            for t in range(TT):
                o = take(f"vr1{t}")
                copy(f"vr1{t}", vr[:, t, 512:1024], o[:, :])
            o = take("cmpkv")
            act.wait_ge(s_ms, 1)
            for g in range(GROUPS):
                for r in range(2):
                    nc.scalar.activation(Kc[r * HD:(r + 1) * HD, g, r, :], o[r * HD:(r + 1) * HD, g * 16:(g + 1) * 16],
                                         ACT.Copy, scale=0.5).then_inc(s_ac, 1)
            probs_out(2)
            probs_out(3)
            exps(4)
            exps(5)
            act.wait_ge(s_cm, 1)
            pcf = Pc[:, :, :, :].rearrange("p t h c -> p (t h c)")
            nc.scalar.activation(pcf, pcf, ACT.Exp).then_inc(s_ce, 1)
            swish(0, 0)
            swish(1, 0)
            o = take("PcT")
            copy("PcT", PcT[:, :], o[:, 0:S])
            exps(6)
            exps(7)
            for pr in range(2):
                o = take(f"PV{pr}")
                copy(f"PV{pr}", yaT[:, pr, :], o[:, 0:S])
            swish(0, 1)
            swish(1, 1)
            probs_out(4)
            probs_out(5)
            for s, nm in enumerate("qk"):
                for t in range(TT):
                    o = take(f"rT{nm}{t}")
                    copy(f"rT{nm}{t}", qkT[:, s, :, t * P:(t + 1) * P], o[:, :].rearrange("p (h i) -> p h i", h=RH))
            o = take("PV2")
            copy("PV2", yaT[:, 2, :], o[:, 0:S])
            probs_out(6)
            probs_out(7)

            def merge_gate(w, i):
                j = f"g{'ab'[w]}{i}"
                o = take(j)
                freed(j, nc.scalar.activation(gate[:, w, 2 * i:2 * i + 2, :], o[:, :].rearrange("p (a t) -> p a t", a=2),
                                              ACT.Tanh, scale=0.5))
            act.wait_ge(*is_full("PV3"))
            merge_gate(0, 0)
            o = take("PV3")
            copy("PV3", yaT[:, 3, :], o[:, 0:S])
            for i in range(1, 4):
                merge_gate(0, i)
            for i in range(4):
                merge_gate(1, i)
            for i in (1, 3):
                o = take(f"x2T{i}")
                copy(f"x2T{i}", h2T[:, 2 * i:2 * i + 2, :], o[:, :].rearrange("p (a t) -> p a t", a=2))
            act.wait_ge(s_rm, 1)
            for t in range(TT):
                nc.scalar.activation(rt[:, t, 110:114], rt[:, t, 0:4], ACT.Exp, bias=rt[:, t, 108:109],
                                     accum_out=rt[:, t, 109:110]).then_inc(s_re, 1)
            act.wait_ge(s_rm, 2)
            nc.scalar.activation(rt[:, :, 106:107], rt[:, :, 106:107], ACT.Exp).then_inc(s_re, 1)

            def batch(n):
                def out_of(job, dst, src=slice(0, 512)):
                    b, _ = STEP_AT[job]
                    act.wait_ge(*step_full(job, n))
                    nc.scalar.activation(dst, bank[b][:, src], ACT.Copy).then_inc(emptied[b], 1)

                def tanh(j):
                    act.wait_ge(*step_full(f"T{j}", n))
                    b, _ = STEP_AT[f"T{j}"]
                    nc.scalar.activation(th_sb[:, j, :, :].rearrange("p f s -> p (f s)"), bank[b][:, 0:2 * C],
                                         ACT.Tanh, scale=0.5).then_inc(s_tanh, 1)
                out_of("G0", hg[:, 0:4, :].rearrange("p k s -> p (k s)"))
                out_of("WT", selWT[:, :], slice(0, S))
                out_of("GU1", gu_sb[:, 1, :])
                tanh(0)
                tanh(1)
                out_of("GU3", gu_sb[:, 1, :])
                tanh(2)
                tanh(3)
                out_of("O0", o_sb[:, 0, :])

            def one_round(r):
                with act.Fori(0, NB) as b:
                    batch(r * NB + b)
            rounds(act, one_round)
            act.wait_ge(s_sum, 1)
            for q in range(4):
                nc.scalar.activation(xs[:, q // 2, (q % 2) * 512:(q % 2 + 1) * 512], bank[4 + q][:, :], ACT.Square,
                                     accum_out=st[:, 210 + q:211 + q]).then_inc(s_fsq, 1)

        @block.vector
        def _(dve):
            chain = [0]

            def link(ins):
                chain[0] += 1
                ins.then_inc(s_dv, 1)
                dve.wait_ge(s_dv, chain[0])

            V = nc.vector

            def take(job):
                dve.wait_ge(*is_full(job))
                return ps(job)

            def freed(job, ins):
                ins.then_inc(emptied[PLACE[job][0]], 1)

            def tsc(o, i, s1, s2, op0, op1):
                return V.tensor_scalar(o, i, s1, s2, op0, op1)

            def rms_scale(col, n_rstd, n_x):
                for t in range(TT):
                    if n_x:
                        dve.wait_ge(s_x[t], 16)
                    ins = V.tensor_tensor_reduce(xs[:, t, :], x[:, t, :], x[:, t, :], 1.0, 0.0, ALU.mult, ALU.add,
                                                 st[:, 200 + t:201 + t])
                link(ins)
                tsc(st[:, col:col + 2], st[:, 200:202], 1.0 / D, EPS, ALU.mult, ALU.add).then_inc(s_rs, 1)
                dve.wait_ge(s_rstd, n_rstd)

            def norm_cols(pre, i, c0):
                o = take(f"{pre}{i}")
                dve.wait_ge(*is_emptied("vecT"))
                for j in range(2):
                    k = 2 * i + j
                    ins = tsc(hT[:, k, :], o[:, j * S:(j + 1) * S], vecT[:, c0 + k:c0 + k + 1], None, ALU.mult, ALU.bypass)
                freed(f"{pre}{i}", ins)

            rms_scale(0, 1, True)
            for t in range(TT):
                tsc(xs[:, t, :], x[:, t, :], st[:, 32 + t:33 + t], None, ALU.mult, ALU.bypass).then_inc(s_xs, 1)
            norm_cols("xT", 0, 0)
            norm_cols("xT", 2, 0)
            o = take("bcmp")
            for t in range(TT):
                ins = V.tensor_copy(bC[:, t, :, :].rearrange("p h c -> p c h"),
                                    o[:, t * P:(t + 1) * P].rearrange("p (c h) -> p c h", c=NC16))
            freed("bcmp", ins)
            o = take("kvcT")
            dve.wait_ge(s_ms, 1)
            for par in range(2):
                for g in range(GROUPS):
                    src = o[g * HD:(g + 1) * HD, :].rearrange("p (v t) -> p v t", v=2)[:, :, par:S]
                    ins = V.tensor_copy(X[par * HD:(par + 1) * HD, :, g, 0:S - par], src)
            freed("kvcT", ins)
            for job, n0 in (("ksT", 0), ("kwT", S)):
                o = take(job)
                for par in range(2):
                    for g in range(GROUPS):
                        ins = V.tensor_copy(Kp[par * HD:(par + 1) * HD, g, par, n0:n0 + S], o[g * HD:(g + 1) * HD, 0:S])
                freed(job, ins)
            dve.wait_ge(s_sg, 1)
            link(tsc(sg[:, :, :], sg[:, :, :], 1.0, 0.5, ALU.add, ALU.mult))

            dve.wait_ge(*is_full("xT3"))

            def rotate(nm, s, t):
                o = take(f"{nm}r{t}").rearrange("p (h a d) -> p h a d", h=RH, a=2) if False else take(f"{nm}r{t}")
                ov = o[:, :].rearrange("p (h d) -> p h d", h=RH)
                q = qkr[:, t, s, :].rearrange("p (h d) -> p h d", h=RH)
                tmp = rtmp.rearrange("p (h d) -> p h d", h=RH)
                V.tensor_tensor(q, ov, rot[:, t, 0:1, :].broadcast_to((P, RH, RQ)), ALU.mult)
                V.tensor_tensor(tmp[:, :, 0:64], ov[:, :, 64:128], rot[:, t, 1:2, 0:64].broadcast_to((P, RH, 64)), ALU.mult)
                link(V.tensor_tensor(tmp[:, :, 64:128], ov[:, :, 0:64], rot[:, t, 1:2, 64:128].broadcast_to((P, RH, 64)), ALU.mult))
                freed(f"{nm}r{t}", V.tensor_tensor(q, q, tmp, ALU.add))
                dve.wait_ge(*is_emptied(f"{nm}r{t}"))

            def biased(h):
                if h == 0:
                    for i in range(4):
                        dve.wait_ge(*is_emptied(f"U{i}"))
                if h >= 4:
                    dve.wait_ge(*is_full(f"PT{h - 4}.1"))
                for t in range(TT):
                    j = f"S{t}.{h}"
                    o = take(j)
                    w = (t + 1) * P
                    for b in range(2):
                        dst = prob[:, h % 4, b, 0:P] if t == 0 else prob[:, h % 4, b, P:384]
                        ins = V.tensor_tensor_reduce(dst, o[:, b * S:b * S + w], Tt[:, h, S - w:S], 1.0, -3e38, ALU.add, ALU.max,
                                                     mx[:, t, h, b:b + 1])
                    freed(j, ins)
                for t in range(TT):
                    dve.wait_ge(*is_emptied(f"S{t}.{h}"))
                tsc(mneg[:, :, h, :], mx[:, :, h, :], -1.0, None, ALU.mult, ALU.bypass).then_inc(s_neg, 1)

            def scaled(h):
                dve.wait_ge(s_exp, h + 1)
                link(V.reciprocal(coef[:, :, h, :], sums[:, :, h, :]))
                link(V.tensor_tensor(coef[:, :, h, :], coef[:, :, h, :],
                                     sg[:, :, :].rearrange("p t (b h) -> p t b h", b=3)[:, :, 1:3, h], ALU.mult))
                for b in range(2):
                    for t in range(TT):
                        p = prob[:, h % 4, b, 0:P] if t == 0 else prob[:, h % 4, b, P:384]
                        ins = tsc(p, p, coef[:, t, h, b:b + 1], None, ALU.mult, ALU.bypass)
                ins.then_inc(s_prob, 1)

            rotate("q", 0, 0)
            rotate("q", 0, 1)
            biased(0)
            biased(1)
            rotate("k", 1, 0)
            rotate("k", 1, 1)
            scaled(0)
            scaled(1)
            biased(2)
            biased(3)
            scaled(2)
            scaled(3)
            o = take("cmpkv")
            dve.wait_ge(s_ac, 4)
            freed("cmpkv", V.scalar_tensor_tensor(Vc[:, :, :], o[:, 64:128].unsqueeze(1).broadcast_to((P, HEADS, HD)), 0.5,
                                                  headmask.unsqueeze(2).broadcast_to((P, HEADS, HD)), ALU.mult, ALU.mult))
            biased(4)
            biased(5)
            o = take("Sc")
            p3 = Pc[:, :, :, :].rearrange("p t h c -> p (t h) c")
            m16, s16 = st[:, 64:80], st[:, 80:96]

            def over_blocks(v):
                return v.unsqueeze(2).broadcast_to((P, TT * HEADS, NC16))
            freed("Sc", V.tensor_tensor(p3, o[:, 0:S].rearrange("p (a c) -> p a c", c=NC16),
                                        bC[:, :, :, :].rearrange("p t h c -> p (t h) c"), ALU.add))
            dve.wait_ge(*is_emptied("Sc"))
            link(V.tensor_reduce(m16, p3, AX, ALU.max))
            V.tensor_tensor(p3, p3, over_blocks(m16), ALU.subtract).then_inc(s_cm, 1)
            scaled(4)
            dve.wait_ge(s_ce, 1)
            for t in range(TT):
                ins = V.tensor_tensor(Pc[:, t, :, :], Pc[:, t, :, :], maskc[:, t:t + 1, :].broadcast_to((P, HEADS, NC16)), ALU.mult)
            link(ins)
            link(V.tensor_reduce(s16, p3, AX, ALU.add))
            link(tsc(s16, s16, 1e-30, None, ALU.max, ALU.bypass))
            link(V.reciprocal(s16, s16))
            link(V.tensor_tensor(s16.rearrange("p (t h) -> p t h", t=TT), s16.rearrange("p (t h) -> p t h", t=TT),
                                 sg[:, :, 0:HEADS], ALU.mult))
            V.tensor_tensor(p3, p3, over_blocks(s16), ALU.mult).then_inc(s_pc, 1)
            scaled(5)

            n_sw = [0]

            def swish(t, n):
                o = take(f"gr{n}{t}")
                n_sw[0] += 1
                dve.wait_ge(s_gt, n_sw[0])
                g = gr[:, t, n * 512:(n + 1) * 512]
                freed(f"gr{n}{t}", V.scalar_tensor_tensor(g, g, 1.0, o[:, :], ALU.add, ALU.mult))
            swish(0, 0)
            swish(1, 0)
            biased(6)
            biased(7)
            scaled(6)
            scaled(7)
            swish(0, 1)
            swish(1, 1)
            for h in range(RH):
                o = take(f"ST{h}")
                V.tensor_tensor(STs[:, h, 0:S], o[:, 0:S], decay[:, h, :], ALU.mult)
                freed(f"ST{h}", V.tensor_tensor(STs[:, h, S:384], o[:, S:384], decay[:, h, 0:P], ALU.mult))
            for i, (t, hp) in enumerate(((0, 0), (0, 1), (1, 0), (1, 1))):
                o = take(f"Y{t}{hp}")
                for j in range(2):
                    ins = V.bn_stats(st[:, 100 + 6 * j:106 + 6 * j], o[:, j * RV:(j + 1) * RV])
                link(ins)
                for j in range(2):
                    ins = V.bn_aggr(st[:, 120 + 2 * j:122 + 2 * j], st[:, 100 + 6 * j:106 + 6 * j])
                link(ins)
                tsc(st[:, 8 + 4 * i:10 + 4 * i], st[:, 120:124].rearrange("p (a b) -> p b a", b=2)[:, 1, :], EPS, None,
                    ALU.add, ALU.bypass).then_inc(s_rs, 1)
                dve.wait_ge(s_rstd, 2 + i)
                if i == 0:
                    for q in range(4):
                        dve.wait_ge(*is_full(f"U{q}"))
                for j in range(2):
                    ins = tsc(y[:, t, (2 * hp + j) * RV:(2 * hp + j + 1) * RV], o[:, j * RV:(j + 1) * RV],
                              st[:, 120 + 2 * j:121 + 2 * j], st[:, 40 + 4 * i + j:41 + 4 * i + j], ALU.subtract, ALU.mult)
                freed(f"Y{t}{hp}", ins)
                if hp == 1:
                    for q in range(2):
                        dve.wait_ge(*is_emptied(f"Y{t}{q}"))
                    if t == 0:
                        for q in ("gr00", "gr01", "gr10", "gr11"):
                            dve.wait_ge(*is_emptied(q))
                    V.tensor_tensor(y[:, t, :], y[:, t, :], gr[:, t, :], ALU.mult).then_inc(s_y, 1)
            for i in range(4):
                o = take(f"yrT{i}")
                for j in range(2):
                    k = 2 * i + j
                    ins = tsc(yrT[:, k, :], o[:, j * S:(j + 1) * S], vecT[:, 16 + k:17 + k], 0.5, ALU.mult, ALU.mult)
                freed(f"yrT{i}", ins)
            for i in range(KT):
                o = take(f"up{i}")
                if i % 2 == 0:
                    for w in "ab":
                        dve.wait_ge(*is_emptied(f"g{w}{i // 2}"))
                V.scalar_tensor_tensor(gate[:, 0, i, :], gate[:, 0, i, :], 1.0, o[:, 0:S], ALU.add, ALU.mult)
                freed(f"up{i}", V.scalar_tensor_tensor(gate[:, 1, i, :], gate[:, 1, i, :], 1.0, o[:, S:2 * S], ALU.add, ALU.mult))
                dve.wait_ge(*is_emptied(f"up{i}"))
                V.tensor_tensor(gate[:, 0, i, :], gate[:, 0, i, :], gate[:, 1, i, :], ALU.add).then_inc(s_mrg, 1)
            for i in range(4):
                o = take(f"out{i}")
                xx = x[:, i // 2, (i % 2) * 512:(i % 2 + 1) * 512]
                freed(f"out{i}", V.scalar_tensor_tensor(xx, o[:, :], 0.5, xx, ALU.mult, ALU.add))
            for i in range(4):
                dve.wait_ge(*is_emptied(f"out{i}"))
            rms_scale(4, 6, False)
            for t in range(TT):
                if t == 0:
                    dve.wait_ge(s_nffn, 16)
                V.scalar_tensor_tensor(xs[:, t, :], x[:, t, :], st[:, 36 + t:37 + t], nffn, ALU.mult, ALU.mult).then_inc(s_xs, 1)
            for i in (0, 2):
                o = take(f"x2T{i}")
                freed(f"x2T{i}", V.tensor_copy(h2T[:, 2 * i:2 * i + 2, :], o[:, :].rearrange("p (a t) -> p a t", a=2)))

            o = take("route")
            dve.wait_ge(s_rw, 64)
            dve.wait_ge(s_ms, 1)
            freed("route", V.tensor_tensor(rt[:, :, 0:36], o[:, 0:72].rearrange("p (t n) -> p t n", t=TT),
                                           rbias[:, :].unsqueeze(1).broadcast_to((P, TT, 36)), ALU.add))
            dve.wait_ge(*is_emptied("route"))
            link(V.tensor_copy(rt[:, :, 40:44], rt[:, :, 0:4]))
            for t in range(TT):
                ins = V.max(rt[:, t, 48:56], rt[:, t, 40:48])
            link(ins)
            tsc(rt[:, :, 108:109], rt[:, :, 48:49], -1.0, None, ALU.mult, ALU.bypass).then_inc(s_rm, 1)
            for t in range(TT):
                ins = V.max_index(ri[:, t, 0:8], rt[:, t, 48:56], rt[:, t, 40:48])
            link(ins)
            link(V.tensor_copy(rt[:, :, 104:105], ri[:, :, 0:1]))
            for t in range(TT):
                ins = tsc(rt[:, t, 56:60], iota[:, 0:4], rt[:, t, 104:105], None, ALU.is_equal, ALU.bypass)
            link(ins)
            V.tensor_scalar(rt[:, :, 60:64], rt[:, :, 56:60], -1.0, 1e30, ALU.add, ALU.mult)
            for t in range(TT):
                ins = V.tensor_tensor(rt[:, t, 64:96].rearrange("p (g e) -> p g e", g=NG),
                                      rt[:, t, 4:36].rearrange("p (g e) -> p g e", g=NG),
                                      rt[:, t, 56:60].unsqueeze(2).broadcast_to((P, NG, EPG)), ALU.mult)
            link(ins)
            for t in range(TT):
                ins = V.tensor_tensor(rt[:, t, 64:96].rearrange("p (g e) -> p g e", g=NG),
                                      rt[:, t, 64:96].rearrange("p (g e) -> p g e", g=NG),
                                      rt[:, t, 60:64].unsqueeze(2).broadcast_to((P, NG, EPG)), ALU.add)
            link(ins)
            for t in range(TT):
                ins = V.max(rt[:, t, 96:104], rt[:, t, 64:96])
            link(ins)
            V.tensor_tensor(rt[:, :, 106:107], rt[:, :, 97:98], rt[:, :, 96:97], ALU.subtract).then_inc(s_rm, 1)
            for t in range(TT):
                ins = V.max_index(ri[:, t, 8:16], rt[:, t, 96:104], rt[:, t, 64:96])
            link(ins)
            link(V.tensor_copy(rt[:, :, 104:106], ri[:, :, 8:10]))
            for t in range(TT):
                tsc(comb1[:, t, :], iota, rt[:, t, 104:105], None, ALU.is_equal, ALU.bypass)
                ins = tsc(rt[:, t, 124:156], iota, rt[:, t, 105:106], None, ALU.is_equal, ALU.bypass)
            link(ins)
            V.tensor_tensor(comb1[:, :, :], comb1[:, :, :], rt[:, :, 124:156], ALU.add).then_inc(s_M, 1)
            dve.wait_ge(s_re, 3)
            link(tsc(rt[:, :, 107:108], rt[:, :, 106:107], 1.0, None, ALU.add, ALU.bypass))
            link(V.tensor_tensor(rt[:, :, 107:108], rt[:, :, 107:108], rt[:, :, 109:110], ALU.mult))
            link(V.reciprocal(rt[:, :, 107:108], rt[:, :, 107:108]))
            link(tsc(rt[:, :, 120:121], rt[:, :, 107:108], 0.5, None, ALU.mult, ALU.bypass))
            link(V.tensor_tensor(rt[:, :, 121:122], rt[:, :, 120:121], rt[:, :, 106:107], ALU.mult))
            for t in range(TT):
                ins = tsc(comb[:, t, :], iota, rt[:, t, 104:105], rt[:, t, 120:121], ALU.is_equal, ALU.mult)
                ins = tsc(rt[:, t, 124:156], iota, rt[:, t, 105:106], rt[:, t, 121:122], ALU.is_equal, ALU.mult)
            link(ins)
            link(V.tensor_tensor(comb[:, :, :], comb[:, :, :], rt[:, :, 124:156], ALU.add))
            o = take("pos")
            link(V.tensor_reduce(nround[:, 0:1], o[:, 2 * NE:3 * NE], AX, ALU.max))
            link(tsc(nround[:, 8:16], iota[:, 0:ROUNDS], -float(C), nround[:, 0:1], ALU.mult, ALU.add))
            link(tsc(nround[:, 8:16], nround[:, 8:16], 0.0, None, ALU.is_gt, ALU.bypass))
            link(V.tensor_reduce(nround[:, 1:2], nround[:, 8:16], AX, ALU.add))
            V.tensor_copy(nround_i[:, :], nround[:, 1:2]).then_inc(s_nr, 1)
            link(tsc(posm[:, :, :], comb1[:, :, :], -1.0, 1e9, ALU.add, ALU.mult))
            freed("pos", V.scalar_tensor_tensor(posm[:, :, :], o[:, 0:2 * NE].rearrange("p (t e) -> p t e", t=TT), float(C),
                                                posm[:, :, :], ALU.add, ALU.add))
            dve.wait_ge(*is_emptied("pos"))

            def batch(n, b):
                def out_of(job, dst, src=slice(0, 512)):
                    bk, _ = STEP_AT[job]
                    dve.wait_ge(*step_full(job, n))
                    V.tensor_copy(dst, bank[bk][:, src]).then_inc(emptied[bk], 1)

                def hidden(j):
                    dve.wait_ge(s_tanh, n * BE + j + 1)
                    bk, _ = STEP_AT[f"T{j}"]
                    h, t = (v[:, j, :, :].rearrange("p f s -> p (f s)") for v in (hide, th_sb))
                    V.scalar_tensor_tensor(h, t, 1.0, bank[bk][:, 0:2 * C], ALU.add, ALU.mult).then_inc(s_hch, 1)
                    dve.wait_ge(s_hch, n * BE + j + 1)
                    V.tensor_tensor(h, h, bank[bk][:, 2 * C:4 * C], ALU.mult).then_inc(emptied[bk], 1)

                for t in range(TT):
                    V.tensor_tensor(selG[:, t, :, :], iota[:, 0:C].unsqueeze(1).broadcast_to((P, BE, C)),
                                    posm[:, t, bass.ds(b * BE, BE)].unsqueeze(2).broadcast_to((P, BE, C)),
                                    ALU.is_equal).then_inc(s_selg, 1)
                dve.wait_ge(s_selg, n * TT + TT)
                for t in range(TT):
                    ins = V.tensor_tensor(selW[:, t, :, :], selG[:, t, :, :],
                                          comb[:, t, bass.ds(b * BE, BE)].unsqueeze(2).broadcast_to((P, BE, C)), ALU.mult)
                ins.then_inc(s_sel, 1)
                out_of("G1", hg[:, 4:8, :].rearrange("p k s -> p (k s)"))
                out_of("GU0", gu_sb[:, 0, :])
                hidden(0)
                out_of("GU2", gu_sb[:, 0, :])
                hidden(1)
                hidden(2)
                hidden(3)
                out_of("O1", o_sb[:, 1, :])

            def one_round(r):
                V.tensor_scalar(posm[:, :, :], posm[:, :, :], -float(C), None, ALU.add, ALU.bypass).then_inc(s_shift, 1)
                with dve.Fori(0, NB) as b:
                    dve.wait_ge(s_shift, r + 1)
                    batch(r * NB + b, b)
            rounds(dve, one_round)

            dve.wait_ge(s_fsq, 4)
            link(V.tensor_reduce(st[:, 200:202], st[:, 210:214].rearrange("p (t n) -> p t n", t=TT), AX, ALU.add))
            tsc(st[:, 6:8], st[:, 200:202], 1.0 / D, EPS, ALU.mult, ALU.add).then_inc(s_rs, 1)
            dve.wait_ge(s_rstd, 7)
            dve.wait_ge(s_nf, 16)
            for q in range(4):
                t, w = q // 2, slice((q % 2) * 512, (q % 2 + 1) * 512)
                V.scalar_tensor_tensor(x[:, t, w], bank[4 + q][:, :], st[:, 38 + t:39 + t], nf[:, w], ALU.mult, ALU.mult).then_inc(s_fin, 1)


_INS = ["x", "rel_bias", "norm_mix", "w_in", "cmp_pos_k", "cmp_k_w1", "cmp_k_w2", "cmp_pos_v", "cmp_v_w1", "cmp_v_w2",
        "ret_norm", "w_nsa_up", "w_ret_up", "w_out", "norm_ffn", "w_router_group", "b_router_group",
        "w_router_expert", "b_router_expert", "moe_w_gate", "moe_w_up", "moe_w_down", "norm_final"]


def kernel(**inputs):
    import concourse.bacc as bacc
    from concourse.bass_utils import run_bass_kernel_spmd

    nc = bacc.Bacc("TRN2", target_bir_lowering=False, num_devices=1)
    arrays, aps = {}, {}
    tables = shape_tables()
    for name in _INS + list(tables):
        v = np.ascontiguousarray(inputs[name] if name in inputs else tables[name])
        arrays[f"in_{name}"] = v
        aps[name] = nc.dram_tensor(f"in_{name}", v.shape, mybir.dt.from_np(v.dtype), kind="ExternalInput").ap()
    out = nc.dram_tensor("out_0", (1, S, D), F32, kind="ExternalOutput").ap()
    build(nc, aps, out)
    r = run_bass_kernel_spmd(nc, [arrays], core_ids=[0])
    return r.results[0]["out_0"]
```

```python
from contextlib import ExitStack

import numpy as np
import concourse.bass as bass
from concourse import mybir

F32 = mybir.dt.float32
U32 = mybir.dt.uint32
ALU = mybir.AluOpType
ACT = mybir.ActivationFunctionType
AX = mybir.AxisListType.X

P = 128
D, S = 1024, 256
KT = D // P
TT = S // P
HEADS, GROUPS, HD = 8, 2, 64
PAIRS = HEADS // 2
CMP_LEN, CMP_STRIDE, CMP_HID = 32, 16, 256
NCMP = (S - CMP_LEN) // CMP_STRIDE + 1
NC16 = 16
BUCKETS, MAX_DIST = 32, 128
RH, RQ, RV = 4, 128, 256
NG, EPG, NE, FF = 4, 8, 32, 256
EPS = 1e-6
C = 32
BE = P // C
NRES = 2
NB = NE // BE
ROUNDS = S // C
NVEC = 3 * KT + CMP_LEN
NEG = -1e30
COLS = dict(q=0, kv=512, ga=1280, qr=1304, kr=1816, vr=2328, gr=3352, gate_a=4376, gate_r=5400)
SLOT = KT * 512
NSLOT = 4
PARTS0 = 4


def t5_bucket(dist):
    dist = np.maximum(dist, 0)
    exact = BUCKETS // 2
    d = np.maximum(dist, 1).astype(np.float32)
    large = exact + (np.log(d / np.float32(exact)) / np.float32(np.log(MAX_DIST / exact))
                     * np.float32(BUCKETS - exact)).astype(np.int32)
    return np.where(dist < exact, dist, np.minimum(large, BUCKETS - 1))


def shape_tables():
    def onehot(dist):
        t = np.zeros((BUCKETS + 1, dist.size), np.float32)
        t[t5_bucket(dist), np.arange(dist.size)] = 1.0
        t[BUCKETS] = np.where(dist < 0, np.float32(NEG), 0)
        return t
    buckets = onehot(S - 1 - np.arange(S + P))
    ident = np.eye(P, dtype=np.float32)
    pos = np.arange(S, dtype=np.float32)
    half = RQ // 2
    inv = (np.float32(10000.0) ** (-np.arange(half, dtype=np.float32) / np.float32(half))).astype(np.float32)
    ang = (pos[:, None] * inv[None, :]).astype(np.float32)
    cos, sin = np.cos(ang).astype(np.float32), np.sin(ang).astype(np.float32)
    rot = np.stack([np.concatenate([cos, cos], 1), np.concatenate([-sin, sin], 1)], 1)
    rot = rot.reshape(TT, P, 2, RQ).transpose(1, 0, 2, 3).reshape(P, -1)
    logg = np.log(1.0 - 2.0 ** (-5.0 - np.arange(RH)))
    diff = np.arange(S)[None, :] - np.arange(P)[:, None]
    dec = np.where(diff[None] >= 0, np.exp(np.maximum(diff, 0)[None] * logg[:, None, None]), 0) * RQ ** -0.5
    dec = dec.transpose(1, 0, 2).astype(np.float32).reshape(P, -1)
    t = np.arange(S)
    mc = (t[:, None] - (np.arange(NC16) * CMP_STRIDE + CMP_LEN - 1)[None, :] >= 0).astype(np.float32)
    mc = mc.reshape(TT, P, NC16).transpose(1, 0, 2).reshape(P, -1)
    hm = (np.arange(P)[:, None] // NC16 == np.arange(HEADS)[None, :]).astype(np.float32)
    io = np.broadcast_to(np.arange(NE, dtype=np.float32), (P, NE))
    tri = (np.arange(P)[:, None] < np.arange(P)[None, :]).astype(np.float32)
    fold = np.tile(np.eye(C, dtype=np.float32), (P // C, 1))
    packed = np.concatenate([ident, ident[::-1], mc, hm, io, rot, dec, tri, fold], 1)
    return dict(buckets=buckets, packed=np.ascontiguousarray(packed))


C_ID, C_J = 0, P
C_MC = 2 * P
C_HM = C_MC + TT * NC16
C_IO = C_HM + HEADS
C_ROT = C_IO + NE
C_DEC = C_ROT + TT * 2 * RQ
C_TRI = C_DEC + RH * S
C_FOLD = C_TRI + P
C_END = C_FOLD + C


BLOCKS = ["kv0", "kv1", "q", "qr", "kr", "w1k", "vr0", "w1v", "vr1", "gr0", "gr1",
          "ga0", "ga1", "gb0", "gb1", "upn", "upr0", "upr1", "out0"]

JOBS = (["vecT"] + [f"xT{i}" for i in range(4)]
        + ["btab", "kvcT", "ksT", "vs", "kwT", "vwg", "qT0", "qT1", "U0", "U1", "U2", "U3", "qr0", "qr1"]
        + ["S0.0", "S1.0", "S0.1", "S1.1", "kr0", "kr1", "S0.2", "S1.2", "S0.3", "S1.3", "hidk", "vr00", "vr01", "hidv"]
        + ["PT0.0", "PT0.1", "PT1.0", "PT1.1", "vr10", "vr11", "cmpkv", "PT2.0", "PT2.1", "PT3.0", "PT3.1"]
        + ["S0.4", "S1.4", "S0.5", "S1.5", "Sc", "gr00", "gr01", "PcT", "S0.6", "S1.6", "S0.7", "S1.7", "PV0", "PV1"]
        + ["gr10", "gr11", "PT4.0", "PT4.1", "PT5.0", "PT5.1", "rTq0", "rTq1", "rTk0", "rTk1", "PV2"]
        + ["PT6.0", "PT6.1", "PT7.0", "PT7.1", "ga0", "PV3", "ST0", "ST1", "ST2", "ST3", "ga1", "ga2", "ga3"]
        + ["Y00", "Y01", "gb0", "Y10", "Y11", "gb1", "gb2", "gb3"]
        + [f"yrT{i}" for i in range(4)] + [f"up{i}" for i in range(8)])
END_JOBS = [("out0", 4), ("out1", 5), ("out2", 6), ("x2T00", 0), ("x2T01", 1), ("out3", 7), ("x2T10", 2), ("route0", 3),
            ("x2T11", 0), ("route1", 1), ("pos", 2)]
STEP = [("G0", 0), ("G1", 1), ("WT", 2), ("GU0", 3), ("GU1", 0), ("T0", 1), ("GU2", 2), ("T1", 3), ("GU3", 0),
        ("T2", 1), ("T3", 2), ("O0", 3), ("O1", 0)]
STEP_N = [sum(b == i for _, b in STEP) for i in range(4)]
STEP_AT = {j: (b, sum(b == c for _, c in STEP[:i])) for i, (j, b) in enumerate(STEP)}
NBANK = 8
PLACE = {j: (i % NBANK, i // NBANK) for i, j in enumerate(JOBS)}
LAST_N = [len(range(b, len(JOBS), NBANK)) for b in range(NBANK)]
for _job, _b in END_JOBS:
    PLACE[_job] = (_b, LAST_N[_b])
    LAST_N[_b] += 1
LAST_USE = dict(kv0="vs", kv1="vwg", q="qT1", qr="qr1", kr="kr1", w1k="hidk", w1v="hidv", vr0="vr01", vr1="vr11",
                gr0="gr01", gr1="gr11", ga0="ga1", ga1="ga3", gb0="gb1", gb1="gb3",
                upn="up7", upr0="up7", upr1="up7", out0="out3", out1="out3")


def build(nc, a, out):
    with ExitStack() as ctx:
        def sb(name, shape, dt=F32):
            return ctx.enter_context(nc.sbuf_tensor(name, shape, dt))

        def sem(name):
            return ctx.enter_context(nc.semaphore(name))

        bank = [ctx.enter_context(nc.psum_tensor(f"bank{i}", [P, 512], F32)) for i in range(NBANK)]
        full = [sem(f"full{i}") for i in range(NBANK)]
        emptied = [sem(f"emptied{i}") for i in range(NBANK)]

        def ps(job):
            return bank[PLACE[job][0]]

        def is_full(job):
            b, n = PLACE[job]
            return full[b], n + 1

        def is_emptied(job):
            b, n = PLACE[job]
            return emptied[b], n + 1

        ring = sb("ring", [P, NSLOT * SLOT])
        x = sb("x", [P, TT, D])
        xs = sb("xs", [P, TT, D])
        def region(name, n=2048):
            return sb(name, [P, n])
        pair_a = region("hT_and_y", 4096)
        pair_b = region("vr_and_gr", 4096)
        r_kpad, r_qkT, r_X = region("keys"), region("qkT"), region("windows")
        hT = pair_a[:, 0:2048].rearrange("p (k t) -> p k t", k=KT)
        y = pair_a[:, 2048:4096].rearrange("p (t d) -> p t d", t=TT)
        vr = pair_b[:, 0:2048].rearrange("p (t d) -> p t d", t=TT)
        gr = pair_b[:, 2048:4096].rearrange("p (t d) -> p t d", t=TT)
        cst = sb("cst", [P, C_END])
        buckets = sb("buckets", [BUCKETS + 1, S + P])
        relb = sb("relb", [BUCKETS + 1, HEADS])
        vecs = sb("vecs", [NVEC, P])
        vecT = sb("vecT_sb", [P, NVEC])
        etab = sb("etab", [HEADS, 384])
        Tb = sb("Tb", [P, HEADS * S])
        qT = sb("qT", [P, PAIRS, S])
        Kpad = r_kpad
        vsel = sb("vsel", [P, TT, P])
        vwin = sb("vwin", [P, TT, P + 24])
        nsa = sb("nsa", [P, 6144])
        qkT = r_qkT[:, :].rearrange("p (s h t) -> p s h t", s=2, h=RH)
        yaT = sb("yaT", [P, PAIRS, S])
        X = r_X[:, 0:1024].rearrange("p (v g t) -> p v g t", v=2, g=GROUPS)
        Xb = r_X[:, 1024:2048].rearrange("p (v l g c) -> p v l g c", v=2, l=CMP_LEN // 2, g=GROUPS)
        w2 = sb("w2", [P, 2, 2, HD])
        hid = sb("hid", [P, 128])
        hid2 = sb("hid2", [P, 128])
        hidv = sb("hidv", [P, 2, P])
        Kc = sb("Kc", [P, GROUPS, 2, NC16])
        Vc = sb("Vc", [P, HEADS, HD])
        Pc = sb("Pc", [P, TT, HEADS, NC16])
        PcT = sb("PcT_sb", [P, S])
        sg = sb("sg", [P, TT, 24])
        st = sb("st", [P, 256])
        mneg = sb("mneg", [P, TT, HEADS, 2])
        mx = sb("mx", [P, TT, HEADS, 2])
        sums = sb("sums", [P, TT, HEADS, 2])
        coef = sb("coef", [P, TT, HEADS, 2])
        wr = sb("wr", [P, KT, NG + NE])
        rbias = sb("rbias", [P, NG + NE])
        comb = sb("comb", [P, TT, NE])
        comb1 = sb("member", [P, TT, NE])
        ones = sb("ones", [P, P])
        posm = sb("posm", [P, TT, NE])
        zeros = sb("zeros", [P, P])
        nround = sb("nround", [P, 16])
        nround_i = sb("nround_i", [P, 1], mybir.dt.int32)
        rt = sb("rt", [P, TT, 160])
        ri = sb("ri", [P, TT, 16], U32)
        nffn = yaT[:, :, :].rearrange("p a t -> p (a t)")
        nf = qT[:, :, :].rearrange("p a t -> p (a t)")
        rtmp = yaT[:, 0:2, :].rearrange("p a t -> p (a t)")
        bdram = nc.dram_tensor("bias_rows", (HEADS, 384), F32, kind="Internal").ap()

        ident = cst[:, C_ID:C_ID + P]
        flip = cst[:, C_J:C_J + P]
        maskc = cst[:, C_MC:C_MC + TT * NC16].rearrange("p (t c) -> p t c", t=TT)
        headmask = cst[:, C_HM:C_HM + HEADS]
        tri = cst[:, C_TRI:C_TRI + P]
        fold = cst[:, C_FOLD:C_FOLD + C]
        iota = cst[:, C_IO:C_IO + NE]
        rot = cst[:, C_ROT:C_ROT + TT * 2 * RQ].rearrange("p (t s d) -> p t s d", t=TT, s=2)
        decay = cst[:, C_DEC:C_DEC + RH * S].rearrange("p (h i) -> p h i", h=RH)
        Tt = Tb[:, :].rearrange("p (h j) -> p h j", h=HEADS)
        yrT = Tb[:, :].rearrange("p (k t) -> p k t", k=KT)
        Kp = Kpad[:, :].rearrange("p (g s n) -> p g s n", g=GROUPS, s=2)
        STs = Kpad[:, 0:RH * 384].rearrange("p (h n) -> p h n", h=RH)
        prob = nsa[:, 0:3072].rearrange("p (h b n) -> p h b n", h=4, b=2)
        PT = nsa[:, 3072:6144].rearrange("p (h b n) -> p h b n", h=4, b=2)
        gate = nsa[:, 0:2 * KT * S].rearrange("p (w k t) -> p w k t", w=2, k=KT)
        m0 = nsa[:, 0:4096]
        selG = m0[:, 0:256].rearrange("p (t e s) -> p t e s", t=TT, e=BE)
        selW = m0[:, 256:512].rearrange("p (t e s) -> p t e s", t=TT, e=BE)
        selWT = m0[:, 512:768]
        hg = m0[:, 768:1792].rearrange("p (k s) -> p k s", k=KT)
        gu_sb = m0[:, 1792:2816].rearrange("p (b n) -> p b n", b=2)
        o_sb = m0[:, 2816:3840].rearrange("p (h n) -> p h n", h=2)
        m1 = cst[:, C_DEC:C_DEC + 512].rearrange("p (a j f s) -> p a j f s", a=2, j=BE, f=2)
        hide, th_sb = m1[:, 0], m1[:, 1]
        h2T = Tb[:, :].rearrange("p (k t) -> p k t", k=KT)
        U = y[:, :, :].rearrange("p t d -> p (t d)")
        qkr = xs[:, :, :].rearrange("p t (s d) -> p t s d", s=2)

        s_cst, s_cst2, s_relone, s_vec, s_tab, s_small, s_rw, s_nf = (sem(n) for n in
            ("transposers_loaded", "cst_loaded", "bias_row_of_ones", "vecs_loaded", "tables_loaded", "small_loaded", "router_loaded", "nf_loaded"))
        s_x = [sem(f"x_loaded{t}") for t in range(TT)]
        s_plg = sem("pool_gelu_chain")
        s_slot = [sem(f"slot_loaded{i}") for i in range(NSLOT)]
        s_U = [sem(f"bias_rows_loaded{h}") for h in range(HEADS)]
        s_brow, s_out = sem("bias_rows_stored"), sem("out_stored")
        s_ms, s_pl = sem("memsets_done"), sem("pool_chain")
        s_dv = sem("vector_chain")
        s_ac = sem("scalar_chain")
        s_xs = sem("xs_ready")
        s_rs, s_rstd = sem("variance_ready"), sem("rstd_ready")
        s_neg, s_exp, s_prob = sem("negmax_ready"), sem("exp_done"), sem("prob_ready")
        s_garg, s_th, s_hid = sem("gelu_arg"), sem("gelu_tanh"), sem("hidden_ready")
        s_Xb = sem("cmp_blocks_ready")
        s_cm, s_ce, s_pc = sem("cmp_max"), sem("cmp_exp"), sem("cmp_prob_ready")
        s_sg, s_sgv = sem("branch_gates_tanh"), sem("branch_gates_ready")
        s_rot = sem("rotary_done")
        s_gt, s_G = sem("swish_tanh"), sem("swish_ready")
        s_y = sem("ret_y_ready")
        s_mrg = sem("merged_ready")
        s_rm, s_re, s_comb = sem("router_args"), sem("router_exps"), sem("combine_ready")
        s_gu = [sem(f"gate_up_loaded{j}") for j in range(BE)]
        s_dw = [sem(f"down_loaded{j}") for j in range(BE)]
        s_gu_res = [sem(f"resident_gate_up_loaded{j}") for j in range(NRES)]
        s_dw_res = [sem(f"resident_down_loaded{j}") for j in range(NRES)]
        s_out1 = sem("out1_loaded")
        s_sq, s_xn, s_xr, s_w = sem("squares_summed"), sem("x_normed"), sem("expert_input_done"), sem("selection_weights_ready")
        s_wr = sem("router_weights_scaled")
        s_nffn, s_h2, s_nr = sem("ffn_norm_loaded"), sem("expert_input_ready"), sem("rounds_ready")
        s_sel, s_tanh, s_added = sem("selection_ready"), sem("expert_tanh"), sem("batch_added")
        s_selg, s_shift = sem("selection_chain"), sem("slots_shifted")
        s_hch = sem("expert_vector_chain")
        s_M, s_seed, s_sum, s_fsq = sem("membership_ready"), sem("sums_seeded"), sem("sums_complete"), sem("final_squares")
        s_fin = sem("final_ready")

        def slot(block):
            if block == "out1":
                return pair_b[:, :]
            i = BLOCKS.index(block)
            return ring[:, (i % NSLOT) * SLOT:(i % NSLOT + 1) * SLOT]

        def loaded(block):
            if block == "out1":
                return s_out1, 16
            i = BLOCKS.index(block)
            return s_slot[i % NSLOT], 16 * (i // NSLOT + 1) + (16 * (PARTS0 - 1) if i % NSLOT == 0 else 0)

        def cols(block, n):
            return slot(block)[:, 0:KT * n].rearrange("p (k n) -> p k n", k=KT)

        w_in = a["w_in"][0].rearrange("(k p) n -> p k n", p=P)
        SRC = {
            "kv0": (w_in[:, :, 512:1024], 512), "kv1": (w_in[:, :, 1024:1304], 280), "q": (w_in[:, :, 0:512], 512),
            "qr": (w_in[:, :, 1304:1816], 512), "kr": (w_in[:, :, 1816:2328], 512),
            "vr0": (w_in[:, :, 2328:2840], 512), "vr1": (w_in[:, :, 2840:3352], 512),
            "gr0": (w_in[:, :, 3352:3864], 512), "gr1": (w_in[:, :, 3864:4376], 512),
            "ga0": (w_in[:, :, 4376:4888], 512), "ga1": (w_in[:, :, 4888:5400], 512),
            "gb0": (w_in[:, :, 5400:5912], 512), "gb1": (w_in[:, :, 5912:6424], 512),
        }
        for nm, src in (("w1k", "cmp_k_w1"), ("w1v", "cmp_v_w1")):
            SRC[nm] = (a[src][0].rearrange("(k p) n -> p k n", p=P), None)
        SRC["upn"] = (a["w_nsa_up"][0].rearrange("(k p) n -> p k n", p=P), None)
        for i in range(2):
            SRC[f"upr{i}"] = (a["w_ret_up"][0].rearrange("(k p) n -> p k n", p=P)[:, 4 * i:4 * i + 4, :], None)
            SRC[f"out{i}"] = (a["w_out"][0].rearrange("(k p) n -> p k n", p=P)[:, 4 * i:4 * i + 4, :], None)

        slots = [ring[:, i * SLOT:(i + 1) * SLOT] for i in range(NSLOT)]
        GU = [b.rearrange("p (k w f) -> p k w f", k=KT, w=2) for b in (pair_a[:, :], slots[0], slots[1], slots[3])]
        DW = [b.rearrange("p (k n) -> p k n", k=2) for b in (r_X[:, :], r_qkT[:, :], nsa[:, 4096:6144], r_kpad[:, :])]
        GU_res = [b.rearrange("p (k w f) -> p k w f", k=KT, w=2) for b in (slots[2], pair_b[:, :])]
        DW_res = [b.rearrange("p (k n) -> p k n", k=2) for b in (Tb[:, :], x[:, :, :].rearrange("p t d -> p (t d)"))]

        def step_full(job, n):
            b, i = STEP_AT[job]
            return full[b], n * STEP_N[b] + (LAST_N[b] + i + 1)

        def step_out(job, n):
            b, i = STEP_AT[job]
            return emptied[b], n * STEP_N[b] + (LAST_N[b] + i + 1)

        def rounds(eng, body):
            eng.wait_ge(s_nr, 1)
            left = eng.value_load(nround_i[0:1, 0:1], min_val=1, max_val=ROUNDS)
            with eng.Fori(0, ROUNDS) as r:
                with eng.If(r < left):
                    body(r)

        block = ctx.enter_context(nc.Block())

        @block.sync
        def _(sp):
            for t in range(TT):
                sp.dma_start(x[:, t, :], a["x"][0, t * P:(t + 1) * P, :]).then_inc(s_x[t], 16)
            sp.dma_start(cst[:, 0:C_MC], a["packed"][:, 0:C_MC]).then_inc(s_cst, 16)

            def load(bi):
                b = BLOCKS[bi]
                if bi >= NSLOT:
                    sp.wait_ge(*is_full(LAST_USE[BLOCKS[bi - NSLOT]]))
                src, n = SRC[b]
                dst = cols(b, n) if n else slot(b).rearrange("p (k n) -> p k n", k=src.shape[1])
                sp.dma_start(dst, src).then_inc(loaded(b)[0], 16)

            for i in range(PARTS0):
                ks = slice(i * KT // PARTS0, (i + 1) * KT // PARTS0)
                sp.dma_start(cols("kv0", 512)[:, ks, :], SRC["kv0"][0][:, ks, :]).then_inc(s_slot[0], 16)
            load(1)
            sp.dma_start(cst[:, C_MC:C_END], a["packed"][:, C_MC:C_END]).then_inc(s_cst2, 16)
            load(2)
            load(3)
            sp.wait_ge(*is_emptied("btab"))
            sp.dma_start(bdram, etab[:, :]).then_inc(s_brow, 16)
            sp.wait_ge(s_brow, 16)
            for h in range(HEADS):
                src = bass.AP(bdram.tensor, h * 384, [[1, P], [1, S]])
                sp.dma_start(U[:, h * S:(h + 1) * S], src).then_inc(s_U[h], 16)
            gate_v = a["moe_w_gate"][0].rearrange("e (k p) f -> e p k f", p=P)
            up_v = a["moe_w_up"][0].rearrange("e (k p) f -> e p k f", p=P)
            down_v = a["moe_w_down"][0].rearrange("e (k p) n -> e p k n", p=P)

            def expert(v, j, e):
                return v[j:NE - BE + j + 1][bass.ds(e, 1)].rearrange("e p k n -> (e p) k n")

            def load_gu(j, e):
                for w, v in enumerate((gate_v, up_v)):
                    sp.dma_start(GU[j][:, :, w, :], expert(v, j, e)).then_inc(s_gu[j], 16)

            def load_dw(j, e):
                sp.dma_start(DW[j], expert(down_v, j, e)).then_inc(s_dw[j], 16)

            for bi in range(4, BLOCKS.index("upr1") + 1):
                load(bi)
            load_dw(0, 0)
            load_dw(1, 0)
            sp.wait_ge(*is_full("Y11"))
            load_dw(2, 0)
            load_dw(3, 0)
            load(BLOCKS.index("out0"))
            sp.wait_ge(s_y, TT)
            sp.dma_start(slot("out1").rearrange("p (k n) -> p k n", k=4), SRC["out1"][0]).then_inc(s_out1, 16)

            def vec(dst, src, s):
                sp.dma_start(dst, src.rearrange("(a n) -> a n", a=1).broadcast_to((P, D))).then_inc(s, 16)
            sp.wait_ge(*is_full("yrT3"))
            load_gu(0, 0)
            sp.wait_ge(*is_full("up7"))
            vec(nffn, a["norm_ffn"][0], s_nffn)
            for j in range(1, BE):
                load_gu(j, 0)
            vec(nf, a["norm_final"], s_nf)
            sp.wait_ge(*is_full("out3"))
            for j in range(NRES):
                e = NE - BE + j
                for w, v in enumerate((gate_v, up_v)):
                    sp.dma_start(GU_res[j][:, :, w, :], v[e]).then_inc(s_gu_res[j], 16)
                if j == 0:
                    sp.wait_ge(*is_full("route1"))
                else:
                    sp.wait_ge(s_seed, 1)
                    sp.wait_ge(s_xn, TT)
                sp.dma_start(DW_res[j], down_v[e]).then_inc(s_dw_res[j], 16)

            def one_round(n0):
                with sp.Fori(0, NB - 2) as b:
                    for j in range(BE):
                        sp.wait_ge(*step_full(f"GU{j}", n0 + b))
                        load_gu(j, b * BE + BE)
                    sp.wait_ge(*step_full("O1", n0 + b))
                    for j in range(BE):
                        load_dw(j, b * BE + BE)
                for j in range(NRES, BE):
                    sp.wait_ge(*step_full(f"GU{j}", n0 + (NB - 2)))
                    load_gu(j, (NB - 1) * BE)
                sp.wait_ge(*step_full("O1", n0 + (NB - 2)))
                for j in range(NRES, BE):
                    load_dw(j, (NB - 1) * BE)
            one_round(0)
            sp.wait_ge(s_nr, 1)
            left = sp.value_load(nround_i[0:1, 0:1], min_val=1, max_val=ROUNDS)
            with sp.Fori(1, ROUNDS) as r:
                with sp.If(r < left):
                    sp.wait_ge(*step_full("O1", r * NB - 1))
                    for j in range(BE):
                        load_gu(j, 0)
                    for j in range(BE):
                        load_dw(j, 0)
                    one_round(r * NB)
            for t in range(TT):
                for n in range(2):
                    sp.wait_ge(s_fin, 2 * t + n + 1)
                    sp.dma_start(out[0, t * P:(t + 1) * P, n * 512:(n + 1) * 512], xs[:, t, n * 512:(n + 1) * 512]).then_inc(s_out, 16)
            sp.wait_ge(s_out, 64)

        @block.gpsimd
        def _(pool):
            pool.memset(st[:, 250:251], -0.5).then_inc(s_ms, 1)
            pool.wait_ge(s_ms, 1)

            def rstd(n, col):
                pool.wait_ge(s_rs, n)
                pool.tensor_tensor(st[:, col + 32:col + 34], st[:, col:col + 2],
                                   st[:, 250:251].broadcast_to((P, 2)), ALU.pow).then_inc(s_rstd, 1)
            pool.memset(relb[:, :], 1.0).then_inc(s_relone, 1)
            rstd(1, 0)
            pool.memset(Kpad[:, :], 0.0)
            pool.memset(X[:, :, :, :], 0.0)
            pool.memset(Xb[:, :, :, :, :], 0.0)
            pool.memset(Kc[:, :, :, :], 0.0)
            pool.memset(rt[:, :, :], -3e38)
            pool.memset(Pc[:, :, :, :], NEG)
            pool.memset(zeros[:, :], 0.0)
            pool.memset(ones[:, :], 1.0).then_inc(s_ms, 1)
            for i, nm in enumerate(("cmp_k_w2", "cmp_v_w2")):
                pool.dma_start(w2[:, i, :, :], a[nm][0].rearrange("(k p) d -> p k d", p=P)).then_inc(s_small, 16)
            pool.dma_start(wr[:, :, 0:NG], a["w_router_group"][0].rearrange("(k p) g -> p k g", p=P)).then_inc(s_rw, 16)
            pool.dma_start(wr[:, :, NG:NG + NE], a["w_router_expert"][0].rearrange("(k p) g -> p k g", p=P)).then_inc(s_rw, 16)
            pool.dma_start(rbias[:, 0:NG], a["b_router_group"].broadcast_to((P, NG))).then_inc(s_rw, 16)
            pool.dma_start(rbias[:, NG:NG + NE], a["b_router_expert"].broadcast_to((P, NE))).then_inc(s_rw, 16)
            pool.wait_ge(*is_emptied("kvcT"))
            pool.wait_ge(*is_emptied("vecT"))
            for i in range(2):
                for g in range(GROUPS):
                    win = X[:, i, g, :].rearrange("p (c u two) -> p u c two", u=8, two=2)
                    for hi in range(2):
                        ins = pool.tensor_tensor(Xb[:, i, 8 * hi:8 * hi + 8, g, 0:NCMP], win[:, :, hi:hi + NCMP, 0],
                                                 vecT[:, 24 + 16 * i + 8 * hi:32 + 16 * i + 8 * hi].unsqueeze(2).broadcast_to((P, 8, NCMP)), ALU.add)
            ins.then_inc(s_Xb, 1)

            k = [0]

            def link(ins):
                k[0] += 1
                ins.then_inc(s_plg, 1)
                pool.wait_ge(s_plg, k[0])
            pool.wait_ge(*is_emptied("hidk"))
            pool.wait_ge(*is_emptied("hidv"))
            link(pool.tensor_tensor(hid2[:, :], hid[:, :], hid[:, :], ALU.mult))
            link(pool.tensor_scalar(hid2[:, :], hid2[:, :], 0.044715, 1.0, ALU.mult, ALU.add))
            pool.tensor_tensor(hid2[:, :], hid2[:, :], hid[:, :], ALU.mult).then_inc(s_garg, 1)
            pool.wait_ge(s_th, 1)
            link(pool.tensor_scalar(hid2[:, :], hid2[:, :], 1.0, 1.0, ALU.mult, ALU.add))
            link(pool.tensor_tensor(hid2[:, :], hid2[:, :], hid[:, :], ALU.mult))
            for n in range(2):
                for g in range(GROUPS):
                    c0 = 64 + n * 32 + g * 16
                    ins = pool.tensor_copy(hidv[:, n, g * 64:(g + 1) * 64].rearrange("p (h c) -> p h c", h=4),
                                           hid2[:, c0:c0 + 16].unsqueeze(1).broadcast_to((P, 4, 16)))
            ins.then_inc(s_hid, 1)
            for i in range(4):
                rstd(2 + i, 8 + 4 * i)
            for t in range(TT):
                pool.wait_ge(s_rs, 6 + t)
                pool.tensor_tensor(st[:, 36 + t:37 + t], st[:, 4 + t:5 + t], st[:, 250:251], ALU.pow).then_inc(s_rstd, 1)
            pool.wait_ge(s_nffn, 16)
            for t in range(TT):
                pool.wait_ge(s_xn, t + 1)
                pool.tensor_tensor(xs[:, t, :], xs[:, t, :], nffn, ALU.mult).then_inc(s_xr, 1)
            rstd(8, 6)

        @block.tensor
        def _(pe):
            def begin(job):
                b, n = PLACE[job]
                if n > 0:
                    pe.wait_ge(emptied[b], n)
                return bank[b]

            def done(job, ins):
                ins.then_inc(full[PLACE[job][0]], 1)

            def have(*jobs):
                for j in jobs:
                    pe.wait_ge(*is_emptied(j))

            def mm(o, l, r, s, e):
                return nc.tensor.matmul(o, l, r, start=s, stop=e)

            def features(job, block, c0s, n=512):
                o = begin(job)
                pe.wait_ge(*loaded(block))
                for i, c0 in enumerate(c0s):
                    for k in range(KT):
                        ins = mm(o[:, i * S:(i + 1) * S], cols(block, n)[:, k, c0:c0 + P], hT[:, k, :], k == 0, k == KT - 1)
                done(job, ins)

            def tokens(job, block, ts, c0, w, n=512):
                o = begin(job)
                pe.wait_ge(*loaded(block))
                for i, t in enumerate(ts):
                    for k in range(KT):
                        ins = mm(o[:, i * w:(i + 1) * w], hT[:, k, t * P:(t + 1) * P], cols(block, n)[:, k, c0:c0 + w],
                                 k == 0, k == KT - 1)
                done(job, ins)

            def transposes(job, srcs):
                o = begin(job)
                for i, s in enumerate(srcs):
                    ins = nc.tensor.transpose(o[:, i * P:(i + 1) * P], s, ident)
                done(job, ins)

            def norm_transposes(pre, n_ready):
                pe.wait_ge(s_xs, n_ready)
                for i in range(4):
                    transposes(f"{pre}{i}", [xs[:, t, k * P:(k + 1) * P] for k in (2 * i, 2 * i + 1) for t in range(TT)])

            def scores(t, h):
                j = f"S{t}.{h}"
                o = begin(j)
                w = (t + 1) * P
                for b in range(2):
                    ins = mm(o[:, b * S:b * S + w], qT[:, h // 2, t * P:(t + 1) * P],
                             Kp[:, h // 4, h % 2, b * S:b * S + w], True, True)
                done(j, ins)

            def prob_transposes(h):
                pe.wait_ge(s_prob, h + 1)
                for b in range(2):
                    transposes(f"PT{h}.{b}", [prob[:, h % 4, b, i * P:(i + 1) * P] for i in range(3)])

            def attend(pr):
                j = f"PV{pr}"
                have(*[f"PT{2 * pr + i}.{b}" for i in range(2) for b in range(2)])
                o = begin(j)
                g = pr // 2
                for i in range(2):
                    h = 2 * pr + i
                    oo = o[i * HD:(i + 1) * HD, :]
                    for b, v in ((0, vsel), (1, vwin)):
                        pt = PT[:, h % 4, b, :]
                        mm(oo[:, 0:S], v[:, 0, g * HD:(g + 1) * HD], pt[:, 0:S], b == 0, False)
                        mm(oo[:, P:S], v[:, 1, g * HD:(g + 1) * HD], pt[:, S:384], False, False)
                    ins = mm(oo[:, 0:S], Vc[:, h, :], PcT[:, :], False, True)
                done(j, ins)

            o = begin("vecT")
            pe.wait_ge(s_cst, 16)
            pe.wait_ge(s_vec, 80)
            done("vecT", nc.tensor.transpose(o[:, 0:NVEC], vecs[:, :], ident[0:NVEC, 0:NVEC]))
            norm_transposes("xT", TT)
            pe.wait_ge(s_tab, 32)
            o = begin("btab")
            done("btab", mm(o[0:HEADS, 0:384], relb[:, :], buckets[:, :], True, True))
            have(*[f"xT{i}" for i in range(4)])
            features("kvcT", "kv0", (0, 128))
            features("ksT", "kv0", (256,))
            tokens("vs", "kv0", (0, 1), 384, 128)
            features("kwT", "kv1", (0,), 280)
            tokens("vwg", "kv1", (0, 1), 128, 152, 280)
            features("qT0", "q", (0, 128))
            features("qT1", "q", (256, 384))
            for i in range(HEADS):
                pe.wait_ge(s_U[i], 16)
            for i in range(4):
                o = begin(f"U{i}")
                done(f"U{i}", mm(o[:, :], flip, U[:, i * 512:(i + 1) * 512], True, True))
            tokens("qr0", "qr", (0,), 0, 512)
            tokens("qr1", "qr", (1,), 0, 512)
            have("qT0", "qT1", "ksT", "kwT")
            for h in range(2):
                scores(0, h)
                scores(1, h)
            tokens("kr0", "kr", (0,), 0, 512)
            tokens("kr1", "kr", (1,), 0, 512)
            for h in range(2, 4):
                scores(0, h)
                scores(1, h)
            def compress_hidden(i, block):
                j = "hid" + "kv"[i]
                o = begin(j)
                pe.wait_ge(*loaded(block))
                w = slot(block).rearrange("p (l n) -> p l n", l=16)
                for n in range(2):
                    for l in range(16):
                        ins = mm(o[:, n * 32:(n + 1) * 32], w[:, l, n * P:(n + 1) * P],
                                 Xb[:, i, l, :, :].rearrange("p g c -> p (g c)"), l == 0, l == 15)
                done(j, ins)
            pe.wait_ge(s_Xb, 1)
            compress_hidden(0, "w1k")
            tokens("vr00", "vr0", (0,), 0, 512)
            tokens("vr01", "vr0", (1,), 0, 512)
            compress_hidden(1, "w1v")
            prob_transposes(0)
            prob_transposes(1)
            tokens("vr10", "vr1", (0,), 0, 512)
            tokens("vr11", "vr1", (1,), 0, 512)
            o = begin("cmpkv")
            pe.wait_ge(s_small, 32)
            pe.wait_ge(s_hid, 1)
            for r in range(2):
                for n in range(2):
                    mm(o[r * HD:(r + 1) * HD, 0:32], w2[:, 0, n, :], hid2[:, n * 32:(n + 1) * 32], n == 0, n == 1)
            for n in range(2):
                ins = mm(o[:, 64:128], hidv[:, n, :], w2[:, 1, n, :], n == 0, n == 1)
            done("cmpkv", ins)
            prob_transposes(2)
            prob_transposes(3)
            for h in range(4, 6):
                scores(0, h)
                scores(1, h)
            have("cmpkv")
            o = begin("Sc")
            for t in range(TT):
                for pr in range(PAIRS):
                    ins = mm(o[:, t * P + pr * 32:t * P + pr * 32 + 32], qT[:, pr, t * P:(t + 1) * P],
                             Kc[:, pr // 2, :, :].rearrange("p a c -> p (a c)"), True, True)
            done("Sc", ins)
            tokens("gr00", "gr0", (0,), 0, 512)
            tokens("gr01", "gr0", (1,), 0, 512)
            pe.wait_ge(s_pc, 1)
            transposes("PcT", [Pc[:, t, :, :].rearrange("p h c -> p (h c)") for t in range(TT)])
            for h in range(6, 8):
                scores(0, h)
                scores(1, h)
            have("vs", "vwg", "PcT")
            attend(0)
            attend(1)
            tokens("gr10", "gr1", (0,), 0, 512)
            tokens("gr11", "gr1", (1,), 0, 512)
            prob_transposes(4)
            prob_transposes(5)
            for s, nm in enumerate("qk"):
                for t in range(TT):
                    pe.wait_ge(*is_emptied(f"{nm}r{t}"))
                    transposes(f"rT{nm}{t}", [qkr[:, t, s, h * P:(h + 1) * P] for h in range(RH)])
            attend(2)
            prob_transposes(6)
            prob_transposes(7)
            features("ga0", "ga0", (0, 128))
            attend(3)
            have("rTq0", "rTq1", "rTk0", "rTk1")
            for h in range(RH):
                o = begin(f"ST{h}")
                mm(o[:, 0:S], qkT[:, 1, h, 0:P], qkT[:, 0, h, :], True, True)
                done(f"ST{h}", mm(o[:, S:384], qkT[:, 1, h, P:S], qkT[:, 0, h, P:S], True, True))
            features("ga1", "ga0", (256, 384))
            features("ga2", "ga1", (0, 128))
            features("ga3", "ga1", (256, 384))

            def retain(t, hp):
                j = f"Y{t}{hp}"
                o = begin(j)
                for i in range(2):
                    h = 2 * hp + i
                    oo = o[:, i * RV:(i + 1) * RV]
                    ins = mm(oo, STs[:, h, t * P:(t + 1) * P], vr[:, 0, h * RV:(h + 1) * RV], True, t == 0)
                    if t == 1:
                        ins = mm(oo, STs[:, h, S:384], vr[:, 1, h * RV:(h + 1) * RV], False, True)
                done(j, ins)
            have(*[f"ST{h}" for h in range(RH)])
            have("vr00", "vr01", "vr10", "vr11")
            retain(0, 0)
            retain(0, 1)
            features("gb0", "gb0", (0, 128))
            retain(1, 0)
            retain(1, 1)
            features("gb1", "gb0", (256, 384))
            features("gb2", "gb1", (0, 128))
            features("gb3", "gb1", (256, 384))
            pe.wait_ge(s_y, TT)
            for i in range(4):
                transposes(f"yrT{i}", [y[:, t, k * P:(k + 1) * P] for k in (2 * i, 2 * i + 1) for t in range(TT)])
            have(*[f"PV{i}" for i in range(4)])
            have(*[f"yrT{i}" for i in range(4)])
            for b in ("upn", "upr0", "upr1"):
                pe.wait_ge(*loaded(b))
            wn = slot("upn").rearrange("p (k n) -> p k n", k=4)
            for i in range(KT):
                o = begin(f"up{i}")
                for k in range(4):
                    mm(o[:, 0:S], wn[:, k, i * P:(i + 1) * P], yaT[:, k, :], k == 0, k == 3)
                for k in range(KT):
                    w = slot(f"upr{k // 4}").rearrange("p (k n) -> p k n", k=4)
                    ins = mm(o[:, S:2 * S], w[:, k % 4, i * P:(i + 1) * P], yrT[:, k, :], k == 0, k == KT - 1)
                done(f"up{i}", ins)
            for b in ("out0", "out1"):
                pe.wait_ge(*loaded(b))
            pe.wait_ge(s_mrg, KT)
            def project(t, n):
                o = begin(f"out{2 * t + n}")
                for k in range(KT):
                    w = slot(f"out{k // 4}").rearrange("p (k n) -> p k n", k=4)
                    ins = mm(o[:, :], gate[:, 0, k, t * P:(t + 1) * P], w[:, k % 4, n * 512:(n + 1) * 512],
                             k == 0, k == KT - 1)
                done(f"out{2 * t + n}", ins)

            def stream_transposes(t, n):
                have(f"out{2 * t + n}")
                transposes(f"x2T{t}{n}", [x[:, t, k * P:(k + 1) * P] for k in range(4 * n, 4 * n + 4)])

            def route(t):
                have(f"x2T{t}0", f"x2T{t}1")
                o = begin(f"route{t}")
                for k in range(KT):
                    ins = mm(o[:, 0:NG + NE], h2T[:, k, t * P:(t + 1) * P], wr[:, k, :], k == 0, k == KT - 1)
                done(f"route{t}", ins)
            project(0, 0)
            project(0, 1)
            project(1, 0)
            stream_transposes(0, 0)
            stream_transposes(0, 1)
            project(1, 1)
            stream_transposes(1, 0)
            pe.wait_ge(s_wr, 1)
            route(0)
            stream_transposes(1, 1)
            route(1)
            for b in range(4, NBANK):
                pe.wait_ge(emptied[b], LAST_N[b])

            def add(q, l, r, s, e, w=512):
                return nc.tensor.matmul(bank[4 + q][:, 0:w], l, r, start=s, stop=e, skip_group_check=True)
            for q in range(4):
                ins = add(q, ident, x[:, q // 2, (q % 2) * 512:(q % 2 + 1) * 512], True, False)
            ins.then_inc(s_seed, 1)

            o = begin("pos")
            pe.wait_ge(s_M, 1)
            mm(o[:, 0:2 * NE], tri, comb1[:, :, :].rearrange("p t e -> p (t e)"), True, False)
            mm(o[:, NE:2 * NE], ones[:, :], comb1[:, 0, :], False, True)
            for t in range(TT):
                ins = mm(o[:, 2 * NE:3 * NE], ones[:, :], comb1[:, t, :], t == 0, t == 1)
            done("pos", ins)
            pe.wait_ge(s_xr, TT)

            def batch(n, weights):
                def start(job):
                    b, i = STEP_AT[job]
                    pe.wait_ge(emptied[b], n * STEP_N[b] + (LAST_N[b] + i))
                    return bank[b]

                def end(job, ins):
                    ins.then_inc(full[STEP_AT[job][0]], 1)

                pe.wait_ge(s_sel, n * TT + TT)
                for h in range(2):
                    o = start(f"G{h}")
                    for k in range(4):
                        for t in range(TT):
                            ins = mm(o[:, k * P:(k + 1) * P], xs[:, t, (4 * h + k) * P:(4 * h + k + 1) * P],
                                     selG[:, t, :, :].rearrange("p e s -> p (e s)"), t == 0, t == 1)
                    end(f"G{h}", ins)
                pe.wait_ge(s_w, n + 1)
                o = start("WT")
                for t in range(TT):
                    ins = nc.tensor.transpose(o[:, t * P:(t + 1) * P], selW[:, t, :, :].rearrange("p e s -> p (e s)"), ident)
                end("WT", ins)

                def gate_up(j):
                    gate_up_w, _, wait, _ = weights[j]
                    pe.wait_ge(*wait)
                    o = start(f"GU{j}")
                    for kk in range(2):
                        for c in range(4):
                            k = 4 * kk + c
                            ins = mm(o[c * C:(c + 1) * C, :], hg[:, k, j * C:(j + 1) * C],
                                     gate_up_w[:, k, :, :].rearrange("p w f -> p (w f)"), kk == 0, kk == 1)
                    end(f"GU{j}", ins)

                def turn(j):
                    pe.wait_ge(*step_out(f"GU{j}", n))
                    o = start(f"T{j}")
                    for q in range(4):
                        ins = mm(o[:, q * C:(q + 1) * C], gu_sb[:, j % 2, q * P:(q + 1) * P], fold, True, True)
                    end(f"T{j}", ins)

                pe.wait_ge(*step_out("G0", n))
                pe.wait_ge(*step_out("G1", n))
                gate_up(0)
                gate_up(1)
                turn(0)
                gate_up(2)
                turn(1)
                gate_up(3)
                turn(2)
                turn(3)
                for j in range(BE):
                    pe.wait_ge(*weights[j][3])
                for j in range(BE):
                    pe.wait_ge(*step_out(f"T{j}", n))
                for h in range(2):
                    o = start(f"O{h}")
                    for f in range(2):
                        for j in range(BE):
                            ins = mm(o[j * C:(j + 1) * C, :], hide[:, j, f, :], weights[j][1][:, f, h * 512:(h + 1) * 512], f == 0, f == 1)
                    end(f"O{h}", ins)
                pe.wait_ge(*step_out("WT", n))
                for h in range(2):
                    pe.wait_ge(*step_out(f"O{h}", n))
                    for t in range(TT):
                        ins = add(2 * t + h, selWT[:, t * P:(t + 1) * P], o_sb[:, h, :], False, False)
                ins.then_inc(s_added, 1)

            def streamed(j, m):
                return GU[j], DW[j], (s_gu[j], m * 32 + 32), (s_dw[j], m * 16 + 16)
            resident = [(GU_res[j], DW_res[j], (s_gu_res[j], 32), (s_dw_res[j], 16)) for j in range(NRES)]

            def one_round(r):
                with pe.Fori(0, NB - 1) as b:
                    batch(r * NB + b, [streamed(j, r * (NB - (j < NRES)) + b) for j in range(BE)])
                batch(r * NB + (NB - 1), resident + [streamed(j, r * NB + (NB - 1)) for j in range(NRES, BE)])
            rounds(pe, one_round)
            for q in range(4):
                ins = add(q, zeros[:, :], zeros[:, 0:1], False, True, 1)
            ins.then_inc(s_sum, 1)

        @block.scalar
        def _(act):
            def take(job):
                act.wait_ge(*is_full(job))
                return ps(job)

            def freed(job, ins):
                ins.then_inc(emptied[PLACE[job][0]], 1)

            def norm_cols(pre, i, c0):
                o = take(f"{pre}{i}")
                act.wait_ge(*is_emptied("vecT"))
                for j in range(2):
                    k = 2 * i + j
                    ins = nc.scalar.activation(hT[:, k, :], o[:, j * S:(j + 1) * S], ACT.Copy, scale=vecT[:, c0 + k:c0 + k + 1])
                freed(f"{pre}{i}", ins)

            def copy(job, dst, src, scale=1.0):
                freed(job, nc.scalar.activation(dst, src, ACT.Copy, scale=scale))

            act.dma_start(vecs[0:8, :], a["norm_mix"][0].rearrange("(k p) -> k p", p=P)).then_inc(s_vec, 16)
            act.dma_start(vecs[8:16, :], a["norm_ffn"][0].rearrange("(k p) -> k p", p=P)).then_inc(s_vec, 16)
            act.dma_start(vecs[16:24, :], a["ret_norm"][0].rearrange("(k p) -> k p", p=P)).then_inc(s_vec, 16)
            for i, nm in enumerate(("cmp_pos_k", "cmp_pos_v")):
                act.dma_start(vecs[24 + 16 * i:40 + 16 * i, :],
                              a[nm][0].rearrange("(l two) d -> l (two d)", two=2)).then_inc(s_vec, 16)
            act.dma_start(buckets[:, :], a["buckets"]).then_inc(s_tab, 16)
            act.wait_ge(s_relone, 1)
            act.dma_start(relb[0:BUCKETS, :], a["rel_bias"]).then_inc(s_tab, 16)
            o = take("vecT")
            copy("vecT", vecT[:, :], o[:, 0:NVEC])
            norm_cols("xT", 1, 0)
            norm_cols("xT", 3, 0)
            o = take("btab")
            copy("btab", etab[:, :], o[0:HEADS, 0:384])
            o = take("vs")
            copy("vs", vsel[:, :, :], o[:, 0:2 * P].rearrange("p (t d) -> p t d", t=TT))
            o = take("vwg")
            copy("vwg", vwin[:, :, :], o[:, 0:304].rearrange("p (t d) -> p t d", t=TT))
            act.wait_ge(*is_emptied("vwg"))
            nc.scalar.activation(sg[:, :, :], vwin[:, :, P:P + 24], ACT.Tanh, scale=0.5).then_inc(s_sg, 1)
            for i in range(2):
                o = take(f"qT{i}")
                copy(f"qT{i}", qT[:, 2 * i:2 * i + 2, :], o[:, :].rearrange("p (a t) -> p a t", a=2), HD ** -0.5)
            for i in range(4):
                o = take(f"U{i}")
                copy(f"U{i}", Tb[:, i * 512:(i + 1) * 512], o[:, :])

            def exps(h):
                act.wait_ge(s_neg, h + 1)
                for t in range(TT):
                    for b in range(2):
                        p = prob[:, h % 4, b, t * P:(2 * t + 1) * P] if t == 0 else prob[:, h % 4, b, P:384]
                        ins = nc.scalar.activation(p, p, ACT.Exp, bias=mneg[:, t, h, b:b + 1],
                                                   accum_out=sums[:, t, h, b:b + 1])
                ins.then_inc(s_exp, 1)

            def probs_out(h):
                for b in range(2):
                    o = take(f"PT{h}.{b}")
                    if h >= 4:
                        act.wait_ge(*is_full(f"PV{(h - 4) // 2}"))
                    copy(f"PT{h}.{b}", PT[:, h % 4, b, :], o[:, 0:384])

            def swish(t, n):
                o = take(f"gr{n}{t}")
                nc.scalar.activation(gr[:, t, n * 512:(n + 1) * 512], o[:, :], ACT.Tanh, scale=0.5).then_inc(s_gt, 1)

            exps(0)
            exps(1)
            o = take("hidk")
            copy("hidk", hid[:, 0:64], o[:, 0:64])
            exps(2)
            exps(3)
            for t in range(TT):
                o = take(f"vr0{t}")
                copy(f"vr0{t}", vr[:, t, 0:512], o[:, :])
            o = take("hidv")
            copy("hidv", hid[:, 64:128], o[:, 0:64])
            act.wait_ge(s_garg, 1)
            nc.scalar.activation(hid2[:, :], hid2[:, :], ACT.Tanh, scale=0.7978845608028654).then_inc(s_th, 1)
            probs_out(0)
            probs_out(1)
            for t in range(TT):
                o = take(f"vr1{t}")
                copy(f"vr1{t}", vr[:, t, 512:1024], o[:, :])
            o = take("cmpkv")
            act.wait_ge(s_ms, 2)
            for g in range(GROUPS):
                for r in range(2):
                    nc.scalar.activation(Kc[r * HD:(r + 1) * HD, g, r, :], o[r * HD:(r + 1) * HD, g * 16:(g + 1) * 16],
                                         ACT.Copy, scale=0.5).then_inc(s_ac, 1)
            probs_out(2)
            probs_out(3)
            exps(4)
            exps(5)
            act.wait_ge(s_cm, 1)
            pcf = Pc[:, :, :, :].rearrange("p t h c -> p (t h c)")
            nc.scalar.activation(pcf, pcf, ACT.Exp).then_inc(s_ce, 1)
            swish(0, 0)
            swish(1, 0)
            o = take("PcT")
            copy("PcT", PcT[:, :], o[:, 0:S])
            exps(6)
            exps(7)
            for pr in range(2):
                o = take(f"PV{pr}")
                copy(f"PV{pr}", yaT[:, pr, :], o[:, 0:S])
            swish(0, 1)
            swish(1, 1)
            probs_out(4)
            probs_out(5)
            for s, nm in enumerate("qk"):
                for t in range(TT):
                    o = take(f"rT{nm}{t}")
                    copy(f"rT{nm}{t}", qkT[:, s, :, t * P:(t + 1) * P], o[:, :].rearrange("p (h i) -> p h i", h=RH))
            o = take("PV2")
            copy("PV2", yaT[:, 2, :], o[:, 0:S])
            probs_out(6)
            probs_out(7)

            def merge_gate(w, i):
                j = f"g{'ab'[w]}{i}"
                o = take(j)
                freed(j, nc.scalar.activation(gate[:, w, 2 * i:2 * i + 2, :], o[:, :].rearrange("p (a t) -> p a t", a=2),
                                              ACT.Tanh, scale=0.5))
            act.wait_ge(*is_full("PV3"))
            merge_gate(0, 0)
            o = take("PV3")
            copy("PV3", yaT[:, 3, :], o[:, 0:S])
            for i in range(1, 4):
                merge_gate(0, i)
            for i in range(4):
                merge_gate(1, i)
            def squares(t, n):
                act.wait_ge(*is_emptied(f"out{2 * t + n}"))
                nc.scalar.activation(xs[:, t, n * 512:(n + 1) * 512], x[:, t, n * 512:(n + 1) * 512], ACT.Square,
                                     accum_out=st[:, 204 + 2 * t + n:205 + 2 * t + n]).then_inc(s_sq, 1)

            def normed(t):
                act.wait_ge(s_rstd, 6 + t)
                nc.scalar.activation(xs[:, t, :], x[:, t, :], ACT.Copy, scale=st[:, 36 + t:37 + t]).then_inc(s_xn, 1)
            squares(0, 0)
            squares(0, 1)
            squares(1, 0)
            o = take("x2T00")
            copy("x2T00", h2T[:, 0:4, 0:P], o[:, :].rearrange("p (k t) -> p k t", k=4))
            normed(0)
            squares(1, 1)
            o = take("x2T11")
            copy("x2T11", h2T[:, 4:8, P:S], o[:, :].rearrange("p (k t) -> p k t", k=4))
            normed(1)
            act.wait_ge(s_rm, 1)
            for t in range(TT):
                nc.scalar.activation(rt[:, t, 110:114], rt[:, t, 0:4], ACT.Exp, bias=rt[:, t, 108:109],
                                     accum_out=rt[:, t, 109:110]).then_inc(s_re, 1)
            act.wait_ge(s_rm, 2)
            nc.scalar.activation(rt[:, :, 106:107], rt[:, :, 106:107], ACT.Exp).then_inc(s_re, 1)

            def batch(n):
                def out_of(job, dst, src=slice(0, 512)):
                    b, _ = STEP_AT[job]
                    act.wait_ge(*step_full(job, n))
                    nc.scalar.activation(dst, bank[b][:, src], ACT.Copy).then_inc(emptied[b], 1)

                def tanh(j):
                    act.wait_ge(*step_full(f"T{j}", n))
                    b, _ = STEP_AT[f"T{j}"]
                    nc.scalar.activation(th_sb[:, j, :, :].rearrange("p f s -> p (f s)"), bank[b][:, 0:2 * C],
                                         ACT.Tanh, scale=0.5).then_inc(s_tanh, 1)
                out_of("G0", hg[:, 0:4, :].rearrange("p k s -> p (k s)"))
                out_of("WT", selWT[:, :], slice(0, S))
                out_of("GU1", gu_sb[:, 1, :])
                tanh(0)
                tanh(1)
                out_of("GU3", gu_sb[:, 1, :])
                tanh(2)
                tanh(3)
                out_of("O0", o_sb[:, 0, :])

            def one_round(r):
                with act.Fori(0, NB) as b:
                    batch(r * NB + b)
            rounds(act, one_round)
            act.wait_ge(s_sum, 1)
            for q in range(4):
                nc.scalar.activation(m0[:, 512 * (q + 1):512 * (q + 2)], bank[4 + q][:, :], ACT.Square,
                                     accum_out=st[:, 210 + q:211 + q]).then_inc(s_fsq, 1)

        @block.vector
        def _(dve):
            chain = [0]

            def link(ins):
                chain[0] += 1
                ins.then_inc(s_dv, 1)
                dve.wait_ge(s_dv, chain[0])

            V = nc.vector

            def take(job):
                dve.wait_ge(*is_full(job))
                return ps(job)

            def freed(job, ins):
                ins.then_inc(emptied[PLACE[job][0]], 1)

            def tsc(o, i, s1, s2, op0, op1):
                return V.tensor_scalar(o, i, s1, s2, op0, op1)

            def rms_scale(col, n_rstd, n_x):
                for t in range(TT):
                    if n_x:
                        dve.wait_ge(s_x[t], 16)
                    ins = V.tensor_tensor_reduce(xs[:, t, :], x[:, t, :], x[:, t, :], 1.0, 0.0, ALU.mult, ALU.add,
                                                 st[:, 200 + t:201 + t])
                link(ins)
                tsc(st[:, col:col + 2], st[:, 200:202], 1.0 / D, EPS, ALU.mult, ALU.add).then_inc(s_rs, 1)
                dve.wait_ge(s_rstd, n_rstd)

            def norm_cols(pre, i, c0):
                o = take(f"{pre}{i}")
                dve.wait_ge(*is_emptied("vecT"))
                for j in range(2):
                    k = 2 * i + j
                    ins = tsc(hT[:, k, :], o[:, j * S:(j + 1) * S], vecT[:, c0 + k:c0 + k + 1], None, ALU.mult, ALU.bypass)
                freed(f"{pre}{i}", ins)

            rms_scale(0, 1, True)
            for t in range(TT):
                tsc(xs[:, t, :], x[:, t, :], st[:, 32 + t:33 + t], None, ALU.mult, ALU.bypass).then_inc(s_xs, 1)
            norm_cols("xT", 0, 0)
            norm_cols("xT", 2, 0)
            o = take("kvcT")
            dve.wait_ge(s_ms, 2)
            for par in range(2):
                for g in range(GROUPS):
                    src = o[g * HD:(g + 1) * HD, :].rearrange("p (v t) -> p v t", v=2)[:, :, par:S]
                    ins = V.tensor_copy(X[par * HD:(par + 1) * HD, :, g, 0:S - par], src)
            freed("kvcT", ins)
            for job, n0 in (("ksT", 0), ("kwT", S)):
                o = take(job)
                for par in range(2):
                    for g in range(GROUPS):
                        ins = V.tensor_copy(Kp[par * HD:(par + 1) * HD, g, par, n0:n0 + S], o[g * HD:(g + 1) * HD, 0:S])
                freed(job, ins)
            dve.wait_ge(s_sg, 1)
            link(tsc(sg[:, :, :], sg[:, :, :], 1.0, 0.5, ALU.add, ALU.mult))

            dve.wait_ge(*is_full("xT3"))

            def rotate(nm, s, t):
                o = take(f"{nm}r{t}").rearrange("p (h a d) -> p h a d", h=RH, a=2) if False else take(f"{nm}r{t}")
                ov = o[:, :].rearrange("p (h d) -> p h d", h=RH)
                q = qkr[:, t, s, :].rearrange("p (h d) -> p h d", h=RH)
                tmp = rtmp.rearrange("p (h d) -> p h d", h=RH)
                V.tensor_tensor(q, ov, rot[:, t, 0:1, :].broadcast_to((P, RH, RQ)), ALU.mult)
                V.tensor_tensor(tmp[:, :, 0:64], ov[:, :, 64:128], rot[:, t, 1:2, 0:64].broadcast_to((P, RH, 64)), ALU.mult)
                link(V.tensor_tensor(tmp[:, :, 64:128], ov[:, :, 0:64], rot[:, t, 1:2, 64:128].broadcast_to((P, RH, 64)), ALU.mult))
                freed(f"{nm}r{t}", V.tensor_tensor(q, q, tmp, ALU.add))
                dve.wait_ge(*is_emptied(f"{nm}r{t}"))

            def biased(h):
                if h == 0:
                    for i in range(4):
                        dve.wait_ge(*is_emptied(f"U{i}"))
                if h >= 4:
                    dve.wait_ge(*is_full(f"PT{h - 4}.1"))
                for t in range(TT):
                    j = f"S{t}.{h}"
                    o = take(j)
                    w = (t + 1) * P
                    for b in range(2):
                        dst = prob[:, h % 4, b, 0:P] if t == 0 else prob[:, h % 4, b, P:384]
                        ins = V.tensor_tensor_reduce(dst, o[:, b * S:b * S + w], Tt[:, h, S - w:S], 1.0, -3e38, ALU.add, ALU.max,
                                                     mx[:, t, h, b:b + 1])
                    freed(j, ins)
                for t in range(TT):
                    dve.wait_ge(*is_emptied(f"S{t}.{h}"))
                tsc(mneg[:, :, h, :], mx[:, :, h, :], -1.0, None, ALU.mult, ALU.bypass).then_inc(s_neg, 1)

            def scaled(h):
                dve.wait_ge(s_exp, h + 1)
                link(V.reciprocal(coef[:, :, h, :], sums[:, :, h, :]))
                link(V.tensor_tensor(coef[:, :, h, :], coef[:, :, h, :],
                                     sg[:, :, :].rearrange("p t (b h) -> p t b h", b=3)[:, :, 1:3, h], ALU.mult))
                for b in range(2):
                    for t in range(TT):
                        p = prob[:, h % 4, b, 0:P] if t == 0 else prob[:, h % 4, b, P:384]
                        ins = tsc(p, p, coef[:, t, h, b:b + 1], None, ALU.mult, ALU.bypass)
                ins.then_inc(s_prob, 1)

            dve.wait_ge(s_cst2, 16)
            rotate("q", 0, 0)
            rotate("q", 0, 1)
            biased(0)
            biased(1)
            rotate("k", 1, 0)
            rotate("k", 1, 1)
            scaled(0)
            scaled(1)
            biased(2)
            biased(3)
            scaled(2)
            scaled(3)
            o = take("cmpkv")
            dve.wait_ge(s_ac, 4)
            freed("cmpkv", V.scalar_tensor_tensor(Vc[:, :, :], o[:, 64:128].unsqueeze(1).broadcast_to((P, HEADS, HD)), 0.5,
                                                  headmask.unsqueeze(2).broadcast_to((P, HEADS, HD)), ALU.mult, ALU.mult))
            biased(4)
            biased(5)
            o = take("Sc")
            p3 = Pc[:, :, :, :].rearrange("p t h c -> p (t h) c")
            m16, s16 = st[:, 64:80], st[:, 80:96]

            def over_blocks(v):
                return v.unsqueeze(2).broadcast_to((P, TT * HEADS, NC16))
            for t in range(TT):
                j0 = (TT - 1 - t) * P + CMP_LEN - 1
                n = min(NCMP, (S - 1 - j0) // CMP_STRIDE + 1)
                ins = V.tensor_tensor(Pc[:, t, :, 0:n], o[:, t * P:(t + 1) * P].rearrange("p (h c) -> p h c", c=NC16)[:, :, 0:n],
                                      Tt[:, :, j0:j0 + (n - 1) * CMP_STRIDE + 1:CMP_STRIDE], ALU.add)
            freed("Sc", ins)
            dve.wait_ge(*is_emptied("Sc"))
            link(V.tensor_reduce(m16, p3, AX, ALU.max))
            V.tensor_tensor(p3, p3, over_blocks(m16), ALU.subtract).then_inc(s_cm, 1)
            scaled(4)
            dve.wait_ge(s_ce, 1)
            for t in range(TT):
                ins = V.tensor_tensor(Pc[:, t, :, :], Pc[:, t, :, :], maskc[:, t:t + 1, :].broadcast_to((P, HEADS, NC16)), ALU.mult)
            link(ins)
            link(V.tensor_reduce(s16, p3, AX, ALU.add))
            link(tsc(s16, s16, 1e-30, None, ALU.max, ALU.bypass))
            link(V.reciprocal(s16, s16))
            link(V.tensor_tensor(s16.rearrange("p (t h) -> p t h", t=TT), s16.rearrange("p (t h) -> p t h", t=TT),
                                 sg[:, :, 0:HEADS], ALU.mult))
            V.tensor_tensor(p3, p3, over_blocks(s16), ALU.mult).then_inc(s_pc, 1)
            scaled(5)

            n_sw = [0]

            def swish(t, n):
                o = take(f"gr{n}{t}")
                n_sw[0] += 1
                dve.wait_ge(s_gt, n_sw[0])
                g = gr[:, t, n * 512:(n + 1) * 512]
                freed(f"gr{n}{t}", V.scalar_tensor_tensor(g, g, 1.0, o[:, :], ALU.add, ALU.mult))
            swish(0, 0)
            swish(1, 0)
            biased(6)
            biased(7)
            scaled(6)
            scaled(7)
            swish(0, 1)
            swish(1, 1)
            for h in range(RH):
                o = take(f"ST{h}")
                V.tensor_tensor(STs[:, h, 0:S], o[:, 0:S], decay[:, h, :], ALU.mult)
                freed(f"ST{h}", V.tensor_tensor(STs[:, h, S:384], o[:, S:384], decay[:, h, 0:P], ALU.mult))
            for i, (t, hp) in enumerate(((0, 0), (0, 1), (1, 0), (1, 1))):
                o = take(f"Y{t}{hp}")
                for j in range(2):
                    ins = V.bn_stats(st[:, 100 + 6 * j:106 + 6 * j], o[:, j * RV:(j + 1) * RV])
                link(ins)
                for j in range(2):
                    ins = V.bn_aggr(st[:, 120 + 2 * j:122 + 2 * j], st[:, 100 + 6 * j:106 + 6 * j])
                link(ins)
                tsc(st[:, 8 + 4 * i:10 + 4 * i], st[:, 120:124].rearrange("p (a b) -> p b a", b=2)[:, 1, :], EPS, None,
                    ALU.add, ALU.bypass).then_inc(s_rs, 1)
                dve.wait_ge(s_rstd, 2 + i)
                if i == 0:
                    for q in range(4):
                        dve.wait_ge(*is_full(f"U{q}"))
                for j in range(2):
                    ins = tsc(y[:, t, (2 * hp + j) * RV:(2 * hp + j + 1) * RV], o[:, j * RV:(j + 1) * RV],
                              st[:, 120 + 2 * j:121 + 2 * j], st[:, 40 + 4 * i + j:41 + 4 * i + j], ALU.subtract, ALU.mult)
                freed(f"Y{t}{hp}", ins)
                if hp == 1:
                    for q in range(2):
                        dve.wait_ge(*is_emptied(f"Y{t}{q}"))
                    if t == 0:
                        for q in ("gr00", "gr01", "gr10", "gr11"):
                            dve.wait_ge(*is_emptied(q))
                    V.tensor_tensor(y[:, t, :], y[:, t, :], gr[:, t, :], ALU.mult).then_inc(s_y, 1)
            for i in range(4):
                o = take(f"yrT{i}")
                for j in range(2):
                    k = 2 * i + j
                    ins = tsc(yrT[:, k, :], o[:, j * S:(j + 1) * S], vecT[:, 16 + k:17 + k], 0.5, ALU.mult, ALU.mult)
                freed(f"yrT{i}", ins)
            for i in range(KT):
                o = take(f"up{i}")
                if i % 2 == 0:
                    for w in "ab":
                        dve.wait_ge(*is_emptied(f"g{w}{i // 2}"))
                V.scalar_tensor_tensor(gate[:, 0, i, :], gate[:, 0, i, :], 1.0, o[:, 0:S], ALU.add, ALU.mult)
                freed(f"up{i}", V.scalar_tensor_tensor(gate[:, 1, i, :], gate[:, 1, i, :], 1.0, o[:, S:2 * S], ALU.add, ALU.mult))
                dve.wait_ge(*is_emptied(f"up{i}"))
                V.tensor_tensor(gate[:, 0, i, :], gate[:, 0, i, :], gate[:, 1, i, :], ALU.add).then_inc(s_mrg, 1)
            dve.wait_ge(s_rw, 64)
            V.tensor_tensor(wr[:, :, :], wr[:, :, :], vecT[:, KT:2 * KT].unsqueeze(2).broadcast_to((P, KT, NG + NE)), ALU.mult).then_inc(s_wr, 1)

            def residual(t, n):
                o = take(f"out{2 * t + n}")
                xx = x[:, t, n * 512:(n + 1) * 512]
                freed(f"out{2 * t + n}", V.scalar_tensor_tensor(xx, o[:, :], 0.5, xx, ALU.mult, ALU.add))

            def variance(t):
                dve.wait_ge(s_sq, 2 * t + 2)
                link(V.tensor_tensor(st[:, 200 + t:201 + t], st[:, 204 + 2 * t:205 + 2 * t], st[:, 205 + 2 * t:206 + 2 * t], ALU.add))
                tsc(st[:, 4 + t:5 + t], st[:, 200 + t:201 + t], 1.0 / D, EPS, ALU.mult, ALU.add).then_inc(s_rs, 1)

            def stream_out(t, n):
                o = take(f"x2T{t}{n}")
                freed(f"x2T{t}{n}", V.tensor_copy(h2T[:, 4 * n:4 * n + 4, t * P:(t + 1) * P], o[:, :].rearrange("p (k t) -> p k t", k=4)))
            residual(0, 0)
            residual(0, 1)
            variance(0)
            residual(1, 0)
            stream_out(0, 1)
            residual(1, 1)
            stream_out(1, 0)
            variance(1)

            dve.wait_ge(s_ms, 2)
            dve.wait_ge(s_rstd, 7)
            for t in range(TT):
                o = take(f"route{t}")
                freed(f"route{t}", V.scalar_tensor_tensor(rt[:, t, 0:36], o[:, 0:36], st[:, 36 + t:37 + t], rbias[:, :], ALU.mult, ALU.add))
            for t in range(TT):
                dve.wait_ge(*is_emptied(f"route{t}"))
            link(V.tensor_copy(rt[:, :, 40:44], rt[:, :, 0:4]))
            for t in range(TT):
                ins = V.max(rt[:, t, 48:56], rt[:, t, 40:48])
            link(ins)
            tsc(rt[:, :, 108:109], rt[:, :, 48:49], -1.0, None, ALU.mult, ALU.bypass).then_inc(s_rm, 1)
            for t in range(TT):
                ins = V.max_index(ri[:, t, 0:8], rt[:, t, 48:56], rt[:, t, 40:48])
            link(ins)
            link(V.tensor_copy(rt[:, :, 104:105], ri[:, :, 0:1]))
            for t in range(TT):
                ins = tsc(rt[:, t, 56:60], iota[:, 0:4], rt[:, t, 104:105], None, ALU.is_equal, ALU.bypass)
            link(ins)
            V.tensor_scalar(rt[:, :, 60:64], rt[:, :, 56:60], -1.0, 1e30, ALU.add, ALU.mult)
            for t in range(TT):
                ins = V.tensor_tensor(rt[:, t, 64:96].rearrange("p (g e) -> p g e", g=NG),
                                      rt[:, t, 4:36].rearrange("p (g e) -> p g e", g=NG),
                                      rt[:, t, 56:60].unsqueeze(2).broadcast_to((P, NG, EPG)), ALU.mult)
            link(ins)
            for t in range(TT):
                ins = V.tensor_tensor(rt[:, t, 64:96].rearrange("p (g e) -> p g e", g=NG),
                                      rt[:, t, 64:96].rearrange("p (g e) -> p g e", g=NG),
                                      rt[:, t, 60:64].unsqueeze(2).broadcast_to((P, NG, EPG)), ALU.add)
            link(ins)
            for t in range(TT):
                ins = V.max(rt[:, t, 96:104], rt[:, t, 64:96])
            link(ins)
            V.tensor_tensor(rt[:, :, 106:107], rt[:, :, 97:98], rt[:, :, 96:97], ALU.subtract).then_inc(s_rm, 1)
            for t in range(TT):
                ins = V.max_index(ri[:, t, 8:16], rt[:, t, 96:104], rt[:, t, 64:96])
            link(ins)
            link(V.tensor_copy(rt[:, :, 104:106], ri[:, :, 8:10]))
            for t in range(TT):
                tsc(comb1[:, t, :], iota, rt[:, t, 104:105], None, ALU.is_equal, ALU.bypass)
                ins = tsc(rt[:, t, 124:156], iota, rt[:, t, 105:106], None, ALU.is_equal, ALU.bypass)
            link(ins)
            V.tensor_tensor(comb1[:, :, :], comb1[:, :, :], rt[:, :, 124:156], ALU.add).then_inc(s_M, 1)
            dve.wait_ge(s_re, 3)
            link(tsc(rt[:, :, 107:108], rt[:, :, 106:107], 1.0, None, ALU.add, ALU.bypass))
            link(V.tensor_tensor(rt[:, :, 107:108], rt[:, :, 107:108], rt[:, :, 109:110], ALU.mult))
            link(V.reciprocal(rt[:, :, 107:108], rt[:, :, 107:108]))
            link(tsc(rt[:, :, 120:121], rt[:, :, 107:108], 0.5, None, ALU.mult, ALU.bypass))
            link(V.tensor_tensor(rt[:, :, 121:122], rt[:, :, 120:121], rt[:, :, 106:107], ALU.mult))
            for t in range(TT):
                ins = tsc(comb[:, t, :], iota, rt[:, t, 104:105], rt[:, t, 120:121], ALU.is_equal, ALU.mult)
                ins = tsc(rt[:, t, 124:156], iota, rt[:, t, 105:106], rt[:, t, 121:122], ALU.is_equal, ALU.mult)
            link(ins)
            link(V.tensor_tensor(comb[:, :, :], comb[:, :, :], rt[:, :, 124:156], ALU.add))
            o = take("pos")
            V.tensor_reduce(nround[:, 0:1], o[:, 2 * NE:3 * NE], AX, ALU.max)
            link(tsc(posm[:, :, :], comb1[:, :, :], -1.0, 1e9, ALU.add, ALU.mult))
            V.scalar_tensor_tensor(posm[:, :, :], o[:, 0:2 * NE].rearrange("p (t e) -> p t e", t=TT), float(C),
                                   posm[:, :, :], ALU.add, ALU.add).then_inc(emptied[PLACE["pos"][0]], 1)
            link(tsc(nround[:, 8:16], iota[:, 0:ROUNDS], -float(C), nround[:, 0:1], ALU.mult, ALU.add))
            link(tsc(nround[:, 8:16], nround[:, 8:16], 0.0, None, ALU.is_gt, ALU.bypass))
            link(V.tensor_reduce(nround[:, 1:2], nround[:, 8:16], AX, ALU.add))
            V.tensor_copy(nround_i[:, :], nround[:, 1:2]).then_inc(s_nr, 1)
            dve.wait_ge(*is_emptied("pos"))

            def batch(n, b):
                def out_of(job, dst, src=slice(0, 512)):
                    bk, _ = STEP_AT[job]
                    dve.wait_ge(*step_full(job, n))
                    V.tensor_copy(dst, bank[bk][:, src]).then_inc(emptied[bk], 1)

                def hidden(j):
                    dve.wait_ge(s_tanh, n * BE + j + 1)
                    bk, _ = STEP_AT[f"T{j}"]
                    h, t = (v[:, j, :, :].rearrange("p f s -> p (f s)") for v in (hide, th_sb))
                    V.scalar_tensor_tensor(h, t, 1.0, bank[bk][:, 0:2 * C], ALU.add, ALU.mult).then_inc(s_hch, 1)
                    dve.wait_ge(s_hch, n * BE + j + 1)
                    V.tensor_tensor(h, h, bank[bk][:, 2 * C:4 * C], ALU.mult).then_inc(emptied[bk], 1)

                for t in range(TT):
                    V.tensor_tensor(selG[:, t, :, :], iota[:, 0:C].unsqueeze(1).broadcast_to((P, BE, C)),
                                    posm[:, t, bass.ds(b * BE, BE)].unsqueeze(2).broadcast_to((P, BE, C)),
                                    ALU.is_equal).then_inc(s_sel, 1)
                dve.wait_ge(s_sel, n * TT + TT)
                for t in range(TT):
                    ins = V.tensor_tensor(selW[:, t, :, :], selG[:, t, :, :],
                                          comb[:, t, bass.ds(b * BE, BE)].unsqueeze(2).broadcast_to((P, BE, C)), ALU.mult)
                ins.then_inc(s_w, 1)
                out_of("G1", hg[:, 4:8, :].rearrange("p k s -> p (k s)"))
                out_of("GU0", gu_sb[:, 0, :])
                hidden(0)
                out_of("GU2", gu_sb[:, 0, :])
                hidden(1)
                hidden(2)
                hidden(3)
                out_of("O1", o_sb[:, 1, :])

            def one_round(r):
                V.tensor_scalar(posm[:, :, :], posm[:, :, :], -float(C), None, ALU.add, ALU.bypass).then_inc(s_shift, 1)
                with dve.Fori(0, NB) as b:
                    dve.wait_ge(s_shift, r + 1)
                    batch(r * NB + b, b)
            rounds(dve, one_round)

            dve.wait_ge(s_fsq, 4)
            link(V.tensor_reduce(st[:, 200:202], st[:, 210:214].rearrange("p (t n) -> p t n", t=TT), AX, ALU.add))
            tsc(st[:, 6:8], st[:, 200:202], 1.0 / D, EPS, ALU.mult, ALU.add).then_inc(s_rs, 1)
            dve.wait_ge(s_rstd, 8)
            dve.wait_ge(s_nf, 16)
            for q in range(4):
                t, w = q // 2, slice((q % 2) * 512, (q % 2 + 1) * 512)
                V.scalar_tensor_tensor(xs[:, t, w], bank[4 + q][:, :], st[:, 38 + t:39 + t], nf[:, w], ALU.mult, ALU.mult).then_inc(s_fin, 1)


_INS = ["x", "rel_bias", "norm_mix", "w_in", "cmp_pos_k", "cmp_k_w1", "cmp_k_w2", "cmp_pos_v", "cmp_v_w1", "cmp_v_w2",
        "ret_norm", "w_nsa_up", "w_ret_up", "w_out", "norm_ffn", "w_router_group", "b_router_group",
        "w_router_expert", "b_router_expert", "moe_w_gate", "moe_w_up", "moe_w_down", "norm_final"]


def kernel(**inputs):
    import concourse.bacc as bacc
    from concourse.bass_utils import run_bass_kernel_spmd

    nc = bacc.Bacc("TRN2", target_bir_lowering=False, num_devices=1)
    arrays, aps = {}, {}
    tables = shape_tables()
    for name in _INS + list(tables):
        v = np.ascontiguousarray(inputs[name] if name in inputs else tables[name])
        arrays[f"in_{name}"] = v
        aps[name] = nc.dram_tensor(f"in_{name}", v.shape, mybir.dt.from_np(v.dtype), kind="ExternalInput").ap()
    out = nc.dram_tensor("out_0", (1, S, D), F32, kind="ExternalOutput").ap()
    build(nc, aps, out)
    r = run_bass_kernel_spmd(nc, [arrays], core_ids=[0])
    return r.results[0]["out_0"]
```

```python
from contextlib import ExitStack

import numpy as np
import concourse.bass as bass
from concourse import mybir

F32 = mybir.dt.float32
U32 = mybir.dt.uint32
ALU = mybir.AluOpType
ACT = mybir.ActivationFunctionType
AX = mybir.AxisListType.X

P = 128
D, S = 1024, 256
KT = D // P
TT = S // P
HEADS, GROUPS, HD = 8, 2, 64
PAIRS = HEADS // 2
CMP_LEN, CMP_STRIDE, CMP_HID = 32, 16, 256
NCMP = (S - CMP_LEN) // CMP_STRIDE + 1
NC16 = 16
BUCKETS, MAX_DIST = 32, 128
RH, RQ, RV = 4, 128, 256
NG, EPG, NE, FF = 4, 8, 32, 256
EPS = 1e-6
C = 32
BE = P // C
NRES = 2
NB = NE // BE
ROUNDS = S // C
NVEC = 3 * KT + CMP_LEN
NEG = -1e30
COLS = dict(q=0, kv=512, ga=1280, qr=1304, kr=1816, vr=2328, gr=3352, gate_a=4376, gate_r=5400)
SLOT = KT * 512
NSLOT = 4
PARTS0 = 4


def t5_bucket(dist):
    dist = np.maximum(dist, 0)
    exact = BUCKETS // 2
    d = np.maximum(dist, 1).astype(np.float32)
    large = exact + (np.log(d / np.float32(exact)) / np.float32(np.log(MAX_DIST / exact))
                     * np.float32(BUCKETS - exact)).astype(np.int32)
    return np.where(dist < exact, dist, np.minimum(large, BUCKETS - 1))


def shape_tables():
    def onehot(dist):
        t = np.zeros((BUCKETS + 1, dist.size), np.float32)
        t[t5_bucket(dist), np.arange(dist.size)] = 1.0
        t[BUCKETS] = np.where(dist < 0, np.float32(NEG), 0)
        return t
    buckets = onehot(S - 1 - np.arange(S + P))
    ident = np.eye(P, dtype=np.float32)
    pos = np.arange(S, dtype=np.float32)
    half = RQ // 2
    inv = (np.float32(10000.0) ** (-np.arange(half, dtype=np.float32) / np.float32(half))).astype(np.float32)
    ang = (pos[:, None] * inv[None, :]).astype(np.float32)
    cos, sin = np.cos(ang).astype(np.float32), np.sin(ang).astype(np.float32)
    rot = np.stack([np.concatenate([cos, cos], 1), np.concatenate([-sin, sin], 1)], 1)
    rot = rot.reshape(TT, P, 2, RQ).transpose(1, 0, 2, 3).reshape(P, -1)
    logg = np.log(1.0 - 2.0 ** (-5.0 - np.arange(RH)))
    diff = np.arange(S)[None, :] - np.arange(P)[:, None]
    dec = np.where(diff[None] >= 0, np.exp(np.maximum(diff, 0)[None] * logg[:, None, None]), 0) * RQ ** -0.5
    dec = dec.transpose(1, 0, 2).astype(np.float32).reshape(P, -1)
    t = np.arange(S)
    mc = (t[:, None] - (np.arange(NC16) * CMP_STRIDE + CMP_LEN - 1)[None, :] >= 0).astype(np.float32)
    mc = mc.reshape(TT, P, NC16).transpose(1, 0, 2).reshape(P, -1)
    hm = (np.arange(P)[:, None] // NC16 == np.arange(HEADS)[None, :]).astype(np.float32)
    io = np.broadcast_to(np.arange(NE, dtype=np.float32), (P, NE))
    tri = (np.arange(P)[:, None] < np.arange(P)[None, :]).astype(np.float32)
    fold = np.tile(np.eye(C, dtype=np.float32), (P // C, 1))
    packed = np.concatenate([ident, ident[::-1], mc, hm, io, rot, dec, tri, fold], 1)
    return dict(buckets=buckets, packed=np.ascontiguousarray(packed))


C_ID, C_J = 0, P
C_MC = 2 * P
C_HM = C_MC + TT * NC16
C_IO = C_HM + HEADS
C_ROT = C_IO + NE
C_DEC = C_ROT + TT * 2 * RQ
C_TRI = C_DEC + RH * S
C_FOLD = C_TRI + P
C_END = C_FOLD + C


BLOCKS = ["kv0", "kv1", "q", "qr", "kr", "w1k", "vr0", "w1v", "vr1", "gr0", "gr1",
          "ga0", "ga1", "gb0", "gb1", "upn", "upr0", "upr1", "out0"]

JOBS = (["vecT"] + [f"xT{i}" for i in range(4)]
        + ["btab", "kvcT", "ksT", "vs", "kwT", "vwg", "qT0", "qT1", "U0", "U1", "U2", "U3", "qr0", "qr1"]
        + ["S0.0", "S1.0", "S0.1", "S1.1", "kr0", "kr1", "S0.2", "S1.2", "S0.3", "S1.3", "hpk", "vr00", "hidk", "vr01", "hpv"]
        + ["PT0.0", "PT0.1", "hidv", "PT1.0", "PT1.1", "vr10", "vr11", "cmpkv", "PT2.0", "PT2.1", "PT3.0", "PT3.1"]
        + ["S0.4", "S1.4", "S0.5", "S1.5", "Sc", "gr00", "gr01", "PcT", "S0.6", "S1.6", "S0.7", "S1.7", "PV0", "PV1"]
        + ["gr10", "gr11", "PT4.0", "PT4.1", "PT5.0", "PT5.1", "rTq0", "rTq1", "rTk0", "rTk1", "PV2"]
        + ["PT6.0", "PT6.1", "PT7.0", "PT7.1", "ga0", "PV3", "ST0", "ST1", "ST2", "ST3", "ga1", "ga2", "ga3"]
        + ["Y00", "Y01", "gb0", "Y10", "Y11", "gb1", "gb2"]
        + [f"yrT{i}" for i in range(4)] + ["gb3"] + [f"up{i}" for i in range(8)])
END_JOBS = [("out0", 4), ("out1", 5), ("out2", 6), ("x2T00", 0), ("x2T01", 1), ("route0", 3), ("out3", 7),
            ("x2T10", 2), ("x2T11", 0), ("route1", 1), ("pos", 2)]
BATCH_C = ["GU0.c", "GU1.c", "T0.c", "GU2.c", "T1.c", "GU3.c", "T2.c", "T3.c", "WT.c"]
GATHER_N, DOWN_C = ["G0.n", "G1.n"], ["O0.c", "O1.c"]
SEG = dict(first=GATHER_N, body=BATCH_C + GATHER_N + DOWN_C, last=BATCH_C + DOWN_C)
SEG_BANK0 = dict(first=len(BATCH_C) % 4, body=0, last=0)
SEG_N = {s: [sum((i + SEG_BANK0[s]) % 4 == b for i in range(len(js))) for b in range(4)] for s, js in SEG.items()}
ROUND_N = [SEG_N["first"][b] + (NB - 1) * SEG_N["body"][b] + SEG_N["last"][b] for b in range(4)]
NBANK = 8
PLACE = {j: (i % NBANK, i // NBANK) for i, j in enumerate(JOBS)}
LAST_N = [len(range(b, len(JOBS), NBANK)) for b in range(NBANK)]
for _job, _b in END_JOBS:
    PLACE[_job] = (_b, LAST_N[_b])
    LAST_N[_b] += 1
LAST_USE = dict(kv0="vs", kv1="vwg", q="qT1", qr="qr1", kr="kr1", w1k="hpk", w1v="hpv", vr0="vr01", vr1="vr11",
                gr0="gr01", gr1="gr11", ga0="ga1", ga1="ga3", gb0="gb1", gb1="gb3",
                upn="up7", upr0="up7", upr1="up7", out0="out3", out1="out3")


def build(nc, a, out):
    with ExitStack() as ctx:
        def sb(name, shape, dt=F32):
            return ctx.enter_context(nc.sbuf_tensor(name, shape, dt))

        def sem(name):
            return ctx.enter_context(nc.semaphore(name))

        bank = [ctx.enter_context(nc.psum_tensor(f"bank{i}", [P, 512], F32)) for i in range(NBANK)]
        full = [sem(f"full{i}") for i in range(NBANK)]
        emptied = [sem(f"emptied{i}") for i in range(NBANK)]

        def ps(job):
            return bank[PLACE[job][0]]

        def is_full(job):
            b, n = PLACE[job]
            return full[b], n + 1

        def is_emptied(job):
            b, n = PLACE[job]
            return emptied[b], n + 1

        ring = sb("ring", [P, NSLOT * SLOT])
        x = sb("x", [P, TT, D])
        xs = sb("xs", [P, TT, D])
        def region(name, n=2048):
            return sb(name, [P, n])
        pair_a = region("hT_and_y", 4096)
        pair_b = region("vr_and_gr", 4096)
        r_kpad, r_qkT, r_X = region("keys"), region("qkT"), region("windows")
        hT = pair_a[:, 0:2048].rearrange("p (k t) -> p k t", k=KT)
        y = pair_a[:, 2048:4096].rearrange("p (t d) -> p t d", t=TT)
        vr = pair_b[:, 0:2048].rearrange("p (t d) -> p t d", t=TT)
        gr = pair_b[:, 2048:4096].rearrange("p (t d) -> p t d", t=TT)
        cst = sb("cst", [P, C_END])
        buckets = sb("buckets", [BUCKETS + 1, S + P])
        relb = sb("relb", [BUCKETS + 1, HEADS])
        vecs = sb("vecs", [NVEC, P])
        vecT = sb("vecT_sb", [P, NVEC])
        etab = sb("etab", [HEADS, 384])
        Tb = sb("Tb", [P, HEADS * S])
        q_and_ya = region("queries_and_attention")
        qT = q_and_ya[:, 0:1024].rearrange("p (a t) -> p a t", a=PAIRS)
        yaT = q_and_ya[:, 1024:2048].rearrange("p (a t) -> p a t", a=PAIRS)
        Kpad = r_kpad
        attention = region("attention_small")
        take_at = [0]

        def small(*shape):
            n = int(np.prod(shape))
            v = attention[:, take_at[0]:take_at[0] + n]
            take_at[0] += n
            names = "abcd"[:len(shape)]
            return v.rearrange(f"p ({' '.join(names)}) -> p {' '.join(names)}", **dict(zip(names, shape)))
        vsel = small(TT, P)
        vwin = small(TT, P + 24)
        nsa = sb("nsa", [P, 6144])
        qkT = r_qkT[:, :].rearrange("p (s h t) -> p s h t", s=2, h=RH)
        X = r_X[:, 0:1024].rearrange("p (v g t) -> p v g t", v=2, g=GROUPS)
        Xb = r_X[:, 1024:2048].rearrange("p (v l g c) -> p v l g c", v=2, l=CMP_LEN // 2, g=GROUPS)
        w2 = small(2, 2, HD)
        hpart = sb("hidden_partial", [P, 2, CMP_HID])
        hid = sb("hid", [P, 128])
        hid2 = sb("hid2", [P, 128])
        hidv = sb("hidv", [P, 2, P])
        Kc = sb("Kc", [P, GROUPS, 2, NC16])
        Vc = small(HEADS, HD)
        Pc = small(TT, HEADS, NC16)
        PcT = small(S)
        sg = sb("sg", [P, TT, 24])
        st = sb("st", [P, 256])
        mneg = sb("mneg", [P, TT, HEADS, 2])
        mx = sb("mx", [P, TT, HEADS, 2])
        sums = sb("sums", [P, TT, HEADS, 2])
        coef = sb("coef", [P, TT, HEADS, 2])
        wr = sb("wr", [P, KT, NG + NE])
        rbias = sb("rbias", [P, NG + NE])
        comb = sb("comb", [P, TT, NE])
        comb1 = sb("member", [P, TT, NE])
        ones = sb("ones", [P, P])
        posm = sb("posm", [P, TT, NE])
        zeros = sb("zeros", [P, P])
        nround = sb("nround", [P, 16])
        nround_i = sb("nround_i", [P, 1], mybir.dt.int32)
        rt = sb("rt", [P, TT, 160])
        ri = sb("ri", [P, TT, 16], U32)
        nffn = yaT[:, :, :].rearrange("p a t -> p (a t)")
        nf = cst[:, C_ROT:C_ROT + D]
        rtmp = yaT[:, 0:2, :].rearrange("p a t -> p (a t)")
        bdram = nc.dram_tensor("bias_rows", (HEADS, 384), F32, kind="Internal").ap()

        ident = cst[:, C_ID:C_ID + P]
        flip = cst[:, C_J:C_J + P]
        maskc = cst[:, C_MC:C_MC + TT * NC16].rearrange("p (t c) -> p t c", t=TT)
        headmask = cst[:, C_HM:C_HM + HEADS]
        tri = cst[:, C_TRI:C_TRI + P]
        fold = cst[:, C_FOLD:C_FOLD + C]
        iota = cst[:, C_IO:C_IO + NE]
        rot = cst[:, C_ROT:C_ROT + TT * 2 * RQ].rearrange("p (t s d) -> p t s d", t=TT, s=2)
        decay = cst[:, C_DEC:C_DEC + RH * S].rearrange("p (h i) -> p h i", h=RH)
        Tt = Tb[:, :].rearrange("p (h j) -> p h j", h=HEADS)
        yrT = Tb[:, :].rearrange("p (k t) -> p k t", k=KT)
        Kp = Kpad[:, :].rearrange("p (g s n) -> p g s n", g=GROUPS, s=2)
        STs = Kpad[:, 0:RH * 384].rearrange("p (h n) -> p h n", h=RH)
        prob = nsa[:, 0:3072].rearrange("p (h b n) -> p h b n", h=4, b=2)
        PT = nsa[:, 3072:6144].rearrange("p (h b n) -> p h b n", h=4, b=2)
        gate = nsa[:, 0:2 * KT * S].rearrange("p (w k t) -> p w k t", w=2, k=KT)
        m0 = nsa[:, 0:4096]
        selG = m0[:, 0:256].rearrange("p (t e s) -> p t e s", t=TT, e=BE)
        selW = m0[:, 256:512].rearrange("p (t e s) -> p t e s", t=TT, e=BE)
        selWT = m0[:, 512:768]
        hg = m0[:, 768:1792].rearrange("p (k s) -> p k s", k=KT)
        gu_sb = m0[:, 1792:2816].rearrange("p (b n) -> p b n", b=2)
        o_sb = m0[:, 2816:3840].rearrange("p (h n) -> p h n", h=2)
        m1 = cst[:, C_ROT + D:C_ROT + D + 512].rearrange("p (a j f s) -> p a j f s", a=2, j=BE, f=2)
        hide, th_sb = m1[:, 0], m1[:, 1]
        h2T = nsa[:, 2048:4096].rearrange("p (k t) -> p k t", k=KT)
        xe = Tb[:, :].rearrange("p (t d) -> p t d", t=TT)
        U = y[:, :, :].rearrange("p t d -> p (t d)")
        qkr = xs[:, :, :].rearrange("p t (s d) -> p t s d", s=2)

        s_cst, s_cst2, s_relone, s_vec, s_tab, s_small, s_rw, s_nf = (sem(n) for n in
            ("transposers_loaded", "cst_loaded", "bias_row_of_ones", "vecs_loaded", "tables_loaded", "small_loaded", "router_loaded", "nf_loaded"))
        s_x = [sem(f"x_loaded{t}") for t in range(TT)]
        s_plg = sem("pool_gelu_chain")
        s_slot = [sem(f"slot_loaded{i}") for i in range(NSLOT)]
        s_U = [sem(f"bias_rows_loaded{h}") for h in range(HEADS)]
        s_brow, s_out = sem("bias_rows_stored"), sem("out_stored")
        s_ms = sem("memsets_done")
        s_dv = sem("vector_chain")
        s_ac = sem("scalar_chain")
        s_xs = sem("xs_ready")
        s_rs, s_rstd = sem("variance_ready"), sem("rstd_ready")
        s_neg, s_exp, s_prob = sem("negmax_ready"), sem("exp_done"), sem("prob_ready")
        s_garg, s_th, s_hid = sem("gelu_arg"), sem("gelu_tanh"), sem("hidden_ready")
        s_Xb = sem("cmp_blocks_ready")
        s_cm, s_ce, s_pc = sem("cmp_max"), sem("cmp_exp"), sem("cmp_prob_ready")
        s_sg, s_gt = sem("branch_gates_tanh"), sem("swish_tanh")
        s_y = sem("ret_y_ready")
        s_mrg = sem("merged_ready")
        s_rm, s_re = sem("router_args"), sem("router_exps")
        s_gu = [sem(f"gate_up_loaded{j}") for j in range(BE)]
        s_dw = [[sem(f"down_half{h}_loaded{j}") for h in range(2)] for j in range(BE)]
        s_gu_res = [sem(f"resident_gate_up_loaded{j}") for j in range(NRES)]
        s_dw_res = [sem(f"resident_down_loaded{j}") for j in range(BE)]
        s_out1, s_out0_used = sem("out1_loaded"), sem("out0_used")
        s_sq, s_xn, s_xr, s_w = sem("squares_summed"), sem("x_normed"), sem("expert_input_done"), sem("selection_weights_ready")
        s_wr = sem("router_weights_scaled")
        s_nffn, s_nr = sem("ffn_norm_loaded"), sem("rounds_ready")
        s_sel, s_tanh = sem("selection_ready"), sem("expert_tanh")
        s_shift = sem("slots_shifted")
        s_hch = sem("expert_vector_chain")
        s_M, s_seed, s_sum, s_fsq = sem("membership_ready"), sem("sums_seeded"), sem("sums_complete"), sem("final_squares")
        s_fin, s_fq, s_flast = sem("final_ready"), sem("last_quarter_scaled"), sem("last_quarter_ready")

        def slot(block):
            if block == "out1":
                return pair_b[:, :]
            i = BLOCKS.index(block)
            return ring[:, (i % NSLOT) * SLOT:(i % NSLOT + 1) * SLOT]

        def loaded(block):
            if block == "out1":
                return s_out1, 16
            i = BLOCKS.index(block)
            return s_slot[i % NSLOT], 16 * (i // NSLOT + 1) + (16 * (PARTS0 - 1) if i % NSLOT == 0 else 0)

        def cols(block, n):
            return slot(block)[:, 0:KT * n].rearrange("p (k n) -> p k n", k=KT)

        w_in = a["w_in"][0].rearrange("(k p) n -> p k n", p=P)
        SRC = {
            "kv0": (w_in[:, :, 512:1024], 512), "kv1": (w_in[:, :, 1024:1304], 280), "q": (w_in[:, :, 0:512], 512),
            "qr": (w_in[:, :, 1304:1816], 512), "kr": (w_in[:, :, 1816:2328], 512),
            "vr0": (w_in[:, :, 2328:2840], 512), "vr1": (w_in[:, :, 2840:3352], 512),
            "gr0": (w_in[:, :, 3352:3864], 512), "gr1": (w_in[:, :, 3864:4376], 512),
            "ga0": (w_in[:, :, 4376:4888], 512), "ga1": (w_in[:, :, 4888:5400], 512),
            "gb0": (w_in[:, :, 5400:5912], 512), "gb1": (w_in[:, :, 5912:6424], 512),
        }
        for nm, src in (("w1k", "cmp_k_w1"), ("w1v", "cmp_v_w1")):
            SRC[nm] = (a[src][0].rearrange("(k p) n -> p k n", p=P), None)
        SRC["upn"] = (a["w_nsa_up"][0].rearrange("(k p) n -> p k n", p=P), None)
        for i in range(2):
            SRC[f"upr{i}"] = (a["w_ret_up"][0].rearrange("(k p) n -> p k n", p=P)[:, 4 * i:4 * i + 4, :], None)
            SRC[f"out{i}"] = (a["w_out"][0].rearrange("(k p) n -> p k n", p=P)[:, 4 * i:4 * i + 4, :], None)

        slots = [ring[:, i * SLOT:(i + 1) * SLOT] for i in range(NSLOT)]
        GU = [b.rearrange("p (k w f) -> p k w f", k=KT, w=2) for b in (pair_a[:, :], slots[0], slots[1], slots[3])]
        DW = [b.rearrange("p (k n) -> p k n", k=2) for b in (r_X[:, :], r_qkT[:, :], nsa[:, 4096:6144], r_kpad[:, :])]
        GU_res = [b.rearrange("p (k w f) -> p k w f", k=KT, w=2) for b in (slots[2], pair_b[:, :])]
        DW_res = [b.rearrange("p (k n) -> p k n", k=2)
                  for b in (xs[:, :, :].rearrange("p t d -> p (t d)"), x[:, :, :].rearrange("p t d -> p (t d)"), q_and_ya[:, :], attention[:, :])]

        def place(seg, job, r, b=0):
            i = SEG[seg].index(job)
            k = (i + SEG_BANK0[seg]) % 4
            base = LAST_N[k] + i // 4
            if seg != "first":
                base += SEG_N["first"][k]
            if seg == "last":
                base += (NB - 1) * SEG_N["body"][k]
            return k, r * ROUND_N[k] + b * SEG_N["body"][k] + base

        def step_full(*at):
            k, n = place(*at)
            return full[k], n + 1

        def step_out(*at):
            k, n = place(*at)
            return emptied[k], n + 1

        def rounds(eng, body):
            body(0)
            eng.wait_ge(s_nr, 1)
            left = eng.value_load(nround_i[0:1, 0:1], min_val=1, max_val=ROUNDS)
            with eng.If(left > 1):
                with eng.Fori(1, ROUNDS) as r:
                    with eng.If(r < left):
                        body(r)

        block = ctx.enter_context(nc.Block())

        @block.sync
        def _(sp):
            for t in range(TT):
                sp.dma_start(x[:, t, :], a["x"][0, t * P:(t + 1) * P, :]).then_inc(s_x[t], 16)
            sp.dma_start(cst[:, 0:C_MC], a["packed"][:, 0:C_MC]).then_inc(s_cst, 16)

            def load(bi):
                b = BLOCKS[bi]
                if bi >= NSLOT:
                    sp.wait_ge(*is_full(LAST_USE[BLOCKS[bi - NSLOT]]))
                src, n = SRC[b]
                dst = cols(b, n) if n else slot(b).rearrange("p (k n) -> p k n", k=src.shape[1])
                sp.dma_start(dst, src).then_inc(loaded(b)[0], 16)

            for i in range(PARTS0):
                ks = slice(i * KT // PARTS0, (i + 1) * KT // PARTS0)
                sp.dma_start(cols("kv0", 512)[:, ks, :], SRC["kv0"][0][:, ks, :]).then_inc(s_slot[0], 16)
            load(1)
            sp.dma_start(cst[:, C_MC:C_END], a["packed"][:, C_MC:C_END]).then_inc(s_cst2, 16)
            load(2)
            load(3)
            sp.wait_ge(*is_emptied("btab"))
            sp.dma_start(bdram, etab[:, :]).then_inc(s_brow, 16)
            sp.wait_ge(s_brow, 16)
            for h in range(HEADS):
                src = bass.AP(bdram.tensor, h * 384, [[1, P], [1, S]])
                sp.dma_start(U[:, h * S:(h + 1) * S], src).then_inc(s_U[h], 16)
            gate_v = a["moe_w_gate"][0].rearrange("e (k p) f -> e p k f", p=P)
            up_v = a["moe_w_up"][0].rearrange("e (k p) f -> e p k f", p=P)
            down_v = a["moe_w_down"][0].rearrange("e (k p) n -> e p k n", p=P)

            def expert(v, j, e):
                return v[j:NE - BE + j + 1][bass.ds(e, 1)].rearrange("e p k n -> (e p) k n")

            def load_gu(j, e):
                for w, v in enumerate((gate_v, up_v)):
                    sp.dma_start(GU[j][:, :, w, :], expert(v, j, e)).then_inc(s_gu[j], 16)

            def load_dw(js, e):
                for h in range(2):
                    for j in js:
                        cs = slice(h * 512, (h + 1) * 512)
                        sp.dma_start(DW[j][:, :, cs], expert(down_v[:, :, :, cs], j, e)).then_inc(s_dw[j][h], 16)

            def load_dw_res(j):
                sp.dma_start(DW_res[j], down_v[BE + j]).then_inc(s_dw_res[j], 16)

            for bi in range(4, BLOCKS.index("upr1") + 1):
                load(bi)
            load_dw((0, 1), 0)
            sp.wait_ge(*is_full("Y11"))
            load_dw((2, 3), 0)
            load_dw_res(0)
            sp.wait_ge(*is_full("PV3"))
            load_dw_res(3)
            load(BLOCKS.index("out0"))
            sp.wait_ge(s_y, TT)
            sp.dma_start(slot("out1").rearrange("p (k n) -> p k n", k=4), SRC["out1"][0]).then_inc(s_out1, 16)

            def vec(dst, src, s):
                sp.dma_start(dst, src.rearrange("(a n) -> a n", a=1).broadcast_to((P, D))).then_inc(s, 16)
            sp.wait_ge(*is_full("yrT3"))
            load_gu(0, 0)
            sp.wait_ge(*is_full("up7"))
            vec(nffn, a["norm_ffn"][0], s_nffn)
            vec(nf, a["norm_final"], s_nf)
            for j in range(1, BE):
                load_gu(j, 0)

            for j in range(NRES):
                if j == 0:
                    sp.wait_ge(s_out0_used, 1)
                else:
                    sp.wait_ge(*is_full("out3"))
                for w, v in enumerate((gate_v, up_v)):
                    sp.dma_start(GU_res[j][:, :, w, :], v[BE + j]).then_inc(s_gu_res[j], 16)
            sp.wait_ge(s_seed, 1)
            sp.wait_ge(s_xn, TT)
            load_dw_res(1)
            sp.wait_ge(s_xr, TT)
            load_dw_res(2)

            def one_round(r):
                if not isinstance(r, int):
                    sp.wait_ge(*step_full("last", "O1.c", r - 1))
                    for j in range(BE):
                        load_gu(j, 0)
                    load_dw(range(BE), 0)

                def behind(b, job):
                    sp.wait_ge(*step_full("body", job, r, b))
                behind(0, "GU0.c")
                load_gu(0, 2 * BE)
                for j in range(NRES, BE):
                    behind(0, f"GU{j}.c")
                    load_gu(j, BE)
                behind(0, "O1.c")
                for j in range(1, NRES):
                    load_gu(j, 2 * BE)
                load_dw(range(BE), 2 * BE)
                for j in range(NRES, BE):
                    behind(1, f"GU{j}.c")
                    load_gu(j, 2 * BE)
                with sp.Fori(2, NB - 1) as b:
                    for j in range(BE):
                        behind(b, f"GU{j}.c")
                        load_gu(j, b * BE + BE)
                    behind(b, "O1.c")
                    load_dw(range(BE), b * BE + BE)
            rounds(sp, one_round)
            for t in range(TT):
                for n in range(2):
                    if 2 * t + n < 3:
                        sp.wait_ge(s_fin, 2 * t + n + 1)
                    else:
                        sp.wait_ge(s_flast, 1)
                    sp.dma_start(out[0, t * P:(t + 1) * P, n * 512:(n + 1) * 512], xe[:, t, n * 512:(n + 1) * 512]).then_inc(s_out, 16)
            sp.wait_ge(s_out, 64)

        @block.gpsimd
        def _(pool):
            pool.memset(st[:, 250:251], -0.5).then_inc(s_ms, 1)
            pool.wait_ge(s_ms, 1)

            def rstd(n, col):
                pool.wait_ge(s_rs, n)
                pool.tensor_tensor(st[:, col + 32:col + 34], st[:, col:col + 2],
                                   st[:, 250:251].broadcast_to((P, 2)), ALU.pow).then_inc(s_rstd, 1)
            pool.memset(relb[:, :], 1.0).then_inc(s_relone, 1)
            rstd(1, 0)
            pool.memset(Kpad[:, :], 0.0)
            pool.memset(X[:, :, :, :], 0.0)
            pool.memset(Xb[:, :, :, :, :], 0.0)
            pool.memset(Kc[:, :, :, :], 0.0)
            pool.memset(rt[:, :, :], -3e38)
            pool.memset(Pc[:, :, :, :], NEG)
            pool.memset(zeros[:, :], 0.0)
            pool.memset(ones[:, :], 1.0).then_inc(s_ms, 1)
            for i, nm in enumerate(("cmp_k_w2", "cmp_v_w2")):
                pool.dma_start(w2[:, i, :, :], a[nm][0].rearrange("(k p) d -> p k d", p=P)).then_inc(s_small, 16)
            pool.dma_start(wr[:, :, 0:NG], a["w_router_group"][0].rearrange("(k p) g -> p k g", p=P)).then_inc(s_rw, 16)
            pool.dma_start(wr[:, :, NG:NG + NE], a["w_router_expert"][0].rearrange("(k p) g -> p k g", p=P)).then_inc(s_rw, 16)
            pool.dma_start(rbias[:, 0:NG], a["b_router_group"].broadcast_to((P, NG))).then_inc(s_rw, 16)
            pool.dma_start(rbias[:, NG:NG + NE], a["b_router_expert"].broadcast_to((P, NE))).then_inc(s_rw, 16)
            pool.wait_ge(*is_emptied("kvcT"))
            pool.wait_ge(*is_emptied("vecT"))
            for i in range(2):
                for g in range(GROUPS):
                    win = X[:, i, g, :].rearrange("p (c u two) -> p u c two", u=8, two=2)
                    for hi in range(2):
                        ins = pool.tensor_tensor(Xb[:, i, 8 * hi:8 * hi + 8, g, 0:NCMP], win[:, :, hi:hi + NCMP, 0],
                                                 vecT[:, 24 + 16 * i + 8 * hi:32 + 16 * i + 8 * hi].unsqueeze(2).broadcast_to((P, 8, NCMP)), ALU.add)
            ins.then_inc(s_Xb, 1)

            k = [0]

            def link(ins):
                k[0] += 1
                ins.then_inc(s_plg, 1)
                pool.wait_ge(s_plg, k[0])
            pool.wait_ge(*is_emptied("hidk"))
            pool.wait_ge(*is_emptied("hidv"))
            link(pool.tensor_tensor(hid2[:, :], hid[:, :], hid[:, :], ALU.mult))
            link(pool.tensor_scalar(hid2[:, :], hid2[:, :], 0.044715, 1.0, ALU.mult, ALU.add))
            pool.tensor_tensor(hid2[:, :], hid2[:, :], hid[:, :], ALU.mult).then_inc(s_garg, 1)
            pool.wait_ge(s_th, 1)
            link(pool.tensor_scalar(hid2[:, :], hid2[:, :], 1.0, 1.0, ALU.mult, ALU.add))
            link(pool.tensor_tensor(hid2[:, :], hid2[:, :], hid[:, :], ALU.mult))
            for n in range(2):
                for g in range(GROUPS):
                    c0 = 64 + n * 32 + g * 16
                    ins = pool.tensor_copy(hidv[:, n, g * 64:(g + 1) * 64].rearrange("p (h c) -> p h c", h=4),
                                           hid2[:, c0:c0 + 16].unsqueeze(1).broadcast_to((P, 4, 16)))
            ins.then_inc(s_hid, 1)
            for i in range(4):
                rstd(2 + i, 8 + 4 * i)
            for t in range(TT):
                pool.wait_ge(s_rs, 6 + t)
                pool.tensor_tensor(st[:, 36 + t:37 + t], st[:, 4 + t:5 + t], st[:, 250:251], ALU.pow).then_inc(s_rstd, 1)
            pool.wait_ge(s_nffn, 16)
            for t in range(TT):
                pool.wait_ge(s_xn, t + 1)
                pool.tensor_tensor(xe[:, t, :], xe[:, t, :], nffn, ALU.mult).then_inc(s_xr, 1)
            for t in range(TT):
                pool.wait_ge(s_rs, 8 + t)
                pool.tensor_tensor(st[:, 38 + t:39 + t], st[:, 6 + t:7 + t], st[:, 250:251], ALU.pow).then_inc(s_rstd, 1)
            pool.wait_ge(s_nf, 16)
            pool.wait_ge(s_fq, 1)
            pool.tensor_tensor(xe[:, 1, 512:D], xe[:, 1, 512:D], nf[:, 512:D], ALU.mult).then_inc(s_flast, 1)

        @block.tensor
        def _(pe):
            def begin(job):
                b, n = PLACE[job]
                if n > 0:
                    pe.wait_ge(emptied[b], n)
                return bank[b]

            def done(job, ins):
                ins.then_inc(full[PLACE[job][0]], 1)

            def have(*jobs):
                for j in jobs:
                    pe.wait_ge(*is_emptied(j))

            def mm(o, l, r, s, e):
                return nc.tensor.matmul(o, l, r, start=s, stop=e)

            def features(job, block, c0s, n=512):
                o = begin(job)
                pe.wait_ge(*loaded(block))
                for i, c0 in enumerate(c0s):
                    for k in range(KT):
                        ins = mm(o[:, i * S:(i + 1) * S], cols(block, n)[:, k, c0:c0 + P], hT[:, k, :], k == 0, k == KT - 1)
                done(job, ins)

            def tokens(job, block, ts, c0, w, n=512):
                o = begin(job)
                pe.wait_ge(*loaded(block))
                for i, t in enumerate(ts):
                    for k in range(KT):
                        ins = mm(o[:, i * w:(i + 1) * w], hT[:, k, t * P:(t + 1) * P], cols(block, n)[:, k, c0:c0 + w],
                                 k == 0, k == KT - 1)
                done(job, ins)

            def transposes(job, srcs):
                o = begin(job)
                for i, s in enumerate(srcs):
                    ins = nc.tensor.transpose(o[:, i * P:(i + 1) * P], s, ident)
                done(job, ins)

            def scores(t, h):
                j = f"S{t}.{h}"
                o = begin(j)
                w = (t + 1) * P
                for b in range(2):
                    ins = mm(o[:, b * S:b * S + w], qT[:, h // 2, t * P:(t + 1) * P],
                             Kp[:, h // 4, h % 2, b * S:b * S + w], True, True)
                done(j, ins)

            def prob_transposes(h):
                pe.wait_ge(s_prob, h + 1)
                for b in range(2):
                    transposes(f"PT{h}.{b}", [prob[:, h % 4, b, i * P:(i + 1) * P] for i in range(3)])

            def attend(pr):
                j = f"PV{pr}"
                have(*[f"PT{2 * pr + i}.{b}" for i in range(2) for b in range(2)])
                o = begin(j)
                g = pr // 2
                heads = [(2 * pr + i, o[i * HD:(i + 1) * HD, :]) for i in range(2)]
                for b, v in ((0, vsel), (1, vwin)):
                    for h, oo in heads:
                        mm(oo[:, 0:S], v[:, 0, g * HD:(g + 1) * HD], PT[:, h % 4, b, 0:S], b == 0, False)
                    for h, oo in heads:
                        mm(oo[:, P:S], v[:, 1, g * HD:(g + 1) * HD], PT[:, h % 4, b, S:384], False, False)
                for h, oo in heads:
                    ins = mm(oo[:, 0:S], Vc[:, h, :], PcT[:, :], False, True)
                done(j, ins)

            o = begin("vecT")
            pe.wait_ge(s_cst, 16)
            pe.wait_ge(s_vec, 80)
            done("vecT", nc.tensor.transpose(o[:, 0:NVEC], vecs[:, :], ident[0:NVEC, 0:NVEC]))
            pe.wait_ge(s_xs, TT)
            for i in range(4):
                transposes(f"xT{i}", [xs[:, t, k * P:(k + 1) * P] for k in (2 * i, 2 * i + 1) for t in range(TT)])
            pe.wait_ge(s_tab, 32)
            o = begin("btab")
            done("btab", mm(o[0:HEADS, 0:384], relb[:, :], buckets[:, :], True, True))
            have(*[f"xT{i}" for i in range(4)])
            features("kvcT", "kv0", (0, 128))
            features("ksT", "kv0", (256,))
            tokens("vs", "kv0", (0, 1), 384, 128)
            features("kwT", "kv1", (0,), 280)
            tokens("vwg", "kv1", (0, 1), 128, 152, 280)
            features("qT0", "q", (0, 128))
            features("qT1", "q", (256, 384))
            for i in range(HEADS):
                pe.wait_ge(s_U[i], 16)
            for i in range(4):
                o = begin(f"U{i}")
                done(f"U{i}", mm(o[:, :], flip, U[:, i * 512:(i + 1) * 512], True, True))
            tokens("qr0", "qr", (0,), 0, 512)
            tokens("qr1", "qr", (1,), 0, 512)
            have("qT0", "qT1", "ksT", "kwT")
            for h in range(2):
                scores(0, h)
                scores(1, h)
            tokens("kr0", "kr", (0,), 0, 512)
            tokens("kr1", "kr", (1,), 0, 512)
            for h in range(2, 4):
                scores(0, h)
                scores(1, h)
            def compress_hidden(i, block):
                j = "hp" + "kv"[i]
                o = begin(j)
                pe.wait_ge(*loaded(block))
                w = slot(block).rearrange("p (l n) -> p l n", l=16)
                for l in range(16):
                    c = l % 4
                    ins = mm(o[c * 32:(c + 1) * 32, 0:CMP_HID], Xb[:, i, l, :, :].rearrange("p g c -> p (g c)"), w[:, l, :],
                             l < 4, l >= 12)
                done(j, ins)

            def fold_hidden(i):
                have("hp" + "kv"[i])
                j = "hid" + "kv"[i]
                o = begin(j)
                for n in range(2):
                    ins = mm(o[:, n * 32:(n + 1) * 32], hpart[:, i, n * P:(n + 1) * P], fold, True, True)
                done(j, ins)
            pe.wait_ge(s_Xb, 1)
            compress_hidden(0, "w1k")
            tokens("vr00", "vr0", (0,), 0, 512)
            pe.wait_ge(s_cst2, 16)
            fold_hidden(0)
            tokens("vr01", "vr0", (1,), 0, 512)
            compress_hidden(1, "w1v")
            prob_transposes(0)
            fold_hidden(1)
            prob_transposes(1)
            tokens("vr10", "vr1", (0,), 0, 512)
            tokens("vr11", "vr1", (1,), 0, 512)
            o = begin("cmpkv")
            pe.wait_ge(s_small, 32)
            pe.wait_ge(s_hid, 1)
            for n in range(2):
                for r in range(2):
                    mm(o[r * HD:(r + 1) * HD, 0:32], w2[:, 0, n, :], hid2[:, n * 32:(n + 1) * 32], n == 0, n == 1)
            for n in range(2):
                ins = mm(o[:, 64:128], hidv[:, n, :], w2[:, 1, n, :], n == 0, n == 1)
            done("cmpkv", ins)
            prob_transposes(2)
            prob_transposes(3)
            for h in range(4, 6):
                scores(0, h)
                scores(1, h)
            have("cmpkv")
            o = begin("Sc")
            for t in range(TT):
                for pr in range(PAIRS):
                    ins = mm(o[:, t * P + pr * 32:t * P + pr * 32 + 32], qT[:, pr, t * P:(t + 1) * P],
                             Kc[:, pr // 2, :, :].rearrange("p a c -> p (a c)"), True, True)
            done("Sc", ins)
            tokens("gr00", "gr0", (0,), 0, 512)
            tokens("gr01", "gr0", (1,), 0, 512)
            pe.wait_ge(s_pc, 1)
            transposes("PcT", [Pc[:, t, :, :].rearrange("p h c -> p (h c)") for t in range(TT)])
            for h in range(6, 8):
                scores(0, h)
                scores(1, h)
            have("vs", "vwg", "PcT")
            attend(0)
            attend(1)
            tokens("gr10", "gr1", (0,), 0, 512)
            tokens("gr11", "gr1", (1,), 0, 512)
            prob_transposes(4)
            prob_transposes(5)
            for s, nm in enumerate("qk"):
                for t in range(TT):
                    pe.wait_ge(*is_emptied(f"{nm}r{t}"))
                    transposes(f"rT{nm}{t}", [qkr[:, t, s, h * P:(h + 1) * P] for h in range(RH)])
            attend(2)
            prob_transposes(6)
            prob_transposes(7)
            features("ga0", "ga0", (0, 128))
            attend(3)
            have("rTq0", "rTq1", "rTk0", "rTk1")
            for h in range(RH):
                o = begin(f"ST{h}")
                mm(o[:, 0:S], qkT[:, 1, h, 0:P], qkT[:, 0, h, :], True, True)
                done(f"ST{h}", mm(o[:, S:384], qkT[:, 1, h, P:S], qkT[:, 0, h, P:S], True, True))
            features("ga1", "ga0", (256, 384))
            features("ga2", "ga1", (0, 128))
            features("ga3", "ga1", (256, 384))

            def retain(t, hp):
                j = f"Y{t}{hp}"
                o = begin(j)
                for i in range(2):
                    h = 2 * hp + i
                    oo = o[:, i * RV:(i + 1) * RV]
                    ins = mm(oo, STs[:, h, t * P:(t + 1) * P], vr[:, 0, h * RV:(h + 1) * RV], True, t == 0)
                    if t == 1:
                        ins = mm(oo, STs[:, h, S:384], vr[:, 1, h * RV:(h + 1) * RV], False, True)
                done(j, ins)
            have(*[f"ST{h}" for h in range(RH)])
            have("vr00", "vr01", "vr10", "vr11")
            retain(0, 0)
            retain(0, 1)
            features("gb0", "gb0", (0, 128))
            retain(1, 0)
            retain(1, 1)
            features("gb1", "gb0", (256, 384))
            features("gb2", "gb1", (0, 128))
            pe.wait_ge(s_y, TT)
            for i in range(4):
                transposes(f"yrT{i}", [y[:, t, k * P:(k + 1) * P] for k in (2 * i, 2 * i + 1) for t in range(TT)])
            features("gb3", "gb1", (256, 384))
            have(*[f"PV{i}" for i in range(4)])
            have(*[f"yrT{i}" for i in range(4)])
            for b in ("upn", "upr0", "upr1"):
                pe.wait_ge(*loaded(b))
            wn = slot("upn").rearrange("p (k n) -> p k n", k=4)
            for i in range(KT):
                o = begin(f"up{i}")
                for k in range(4):
                    mm(o[:, 0:S], wn[:, k, i * P:(i + 1) * P], yaT[:, k, :], k == 0, k == 3)
                for k in range(KT):
                    w = slot(f"upr{k // 4}").rearrange("p (k n) -> p k n", k=4)
                    ins = mm(o[:, S:2 * S], w[:, k % 4, i * P:(i + 1) * P], yrT[:, k, :], k == 0, k == KT - 1)
                done(f"up{i}", ins)
            for b in ("out0", "out1"):
                pe.wait_ge(*loaded(b))
            def project(t, n, ks):
                j = f"out{2 * t + n}"
                o = begin(j) if ks[0] == 0 else ps(j)
                for k in ks:
                    w = slot(f"out{k // 4}").rearrange("p (k n) -> p k n", k=4)
                    if t == 0 and n == 0:
                        pe.wait_ge(s_mrg, k + 1)
                    ins = mm(o[:, :], gate[:, 0, k, t * P:(t + 1) * P], w[:, k % 4, n * 512:(n + 1) * 512],
                             k == 0, k == KT - 1)
                    if k == 3 and t == 1 and n == 1:
                        ins.then_inc(s_out0_used, 1)
                if ks[-1] == KT - 1:
                    done(j, ins)

            def stream_transposes(t, n):
                have(f"out{2 * t + n}")
                transposes(f"x2T{t}{n}", [x[:, t, k * P:(k + 1) * P] for k in range(4 * n, 4 * n + 4)])

            def route(t):
                have(f"x2T{t}0", f"x2T{t}1")
                o = begin(f"route{t}")
                for k in range(KT):
                    ins = mm(o[:, 0:NG + NE], h2T[:, k, t * P:(t + 1) * P], wr[:, k, :], k == 0, k == KT - 1)
                done(f"route{t}", ins)
            for q in range(4):
                project(q // 2, q % 2, range(0, 4))
            project(0, 0, range(4, KT))
            project(0, 1, range(4, KT))
            project(1, 0, range(4, 6))
            stream_transposes(0, 0)
            stream_transposes(0, 1)
            project(1, 0, range(6, KT))
            pe.wait_ge(s_wr, 1)
            route(0)
            project(1, 1, range(4, KT))
            stream_transposes(1, 0)
            stream_transposes(1, 1)
            route(1)
            for b in range(4, NBANK):
                pe.wait_ge(emptied[b], LAST_N[b])

            def add(q, l, r, s, e, w=512):
                return nc.tensor.matmul(bank[4 + q][:, 0:w], l, r, start=s, stop=e, skip_group_check=True)
            def seed(q):
                return add(q, ident, x[:, q // 2, (q % 2) * 512:(q % 2 + 1) * 512], True, False)
            for q in range(4):
                ins = seed(q)
            ins.then_inc(s_seed, 1)

            o = begin("pos")
            pe.wait_ge(s_M, TT)
            mm(o[:, 0:2 * NE], tri, comb1[:, :, :].rearrange("p t e -> p (t e)"), True, False)
            mm(o[:, NE:2 * NE], ones[:, :], comb1[:, 0, :], False, True)
            for t in range(TT):
                ins = mm(o[:, 2 * NE:3 * NE], ones[:, :], comb1[:, t, :], t == 0, t == 1)
            done("pos", ins)
            pe.wait_ge(s_xr, TT)

            def steps(seg, r, b, weights):
                def start(job):
                    k, n = place(seg, job, r, b)
                    pe.wait_ge(emptied[k], n)
                    return bank[k]

                def end(job, ins):
                    ins.then_inc(full[place(seg, job, r, b)[0]], 1)

                def out(job):
                    pe.wait_ge(*step_out(seg, job, r, b))

                def gather(n):
                    pe.wait_ge(s_sel, n * TT + TT)
                    for h in range(2):
                        o = start(f"G{h}.n")
                        for k in range(4):
                            for t in range(TT):
                                ins = mm(o[:, k * P:(k + 1) * P], xe[:, t, (4 * h + k) * P:(4 * h + k + 1) * P],
                                         selG[:, t, :, :].rearrange("p e s -> p (e s)"), t == 0, t == 1)
                        end(f"G{h}.n", ins)

                def weight_transposes(n):
                    pe.wait_ge(s_w, n + 1)
                    o = start(f"WT.c")
                    for t in range(TT):
                        ins = nc.tensor.transpose(o[:, t * P:(t + 1) * P], selW[:, t, :, :].rearrange("p e s -> p (e s)"), ident)
                    end(f"WT.c", ins)

                def gate_up(j):
                    gate_up_w, _, wait, _ = weights[j]
                    pe.wait_ge(*wait)
                    o = start(f"GU{j}.c")
                    for kk in range(2):
                        if j == 0:
                            pe.wait_ge(*step_out("body", f"G{kk}.n", r, (NB - 1 if seg == "last" else b) - 1))
                        for c in range(4):
                            k = 4 * kk + c
                            ins = mm(o[c * C:(c + 1) * C, :], hg[:, k, j * C:(j + 1) * C],
                                     gate_up_w[:, k, :, :].rearrange("p w f -> p (w f)"), kk == 0, kk == 1)
                    end(f"GU{j}.c", ins)

                def turn(j):
                    out(f"GU{j}.c")
                    o = start(f"T{j}.c")
                    for q in range(4):
                        ins = mm(o[:, q * C:(q + 1) * C], gu_sb[:, j % 2, q * P:(q + 1) * P], fold, True, True)
                    end(f"T{j}.c", ins)

                def down(h):
                    for j in range(BE):
                        pe.wait_ge(*weights[j][3][h])
                    o = start(f"O{h}.c")
                    for f in range(2):
                        for j in range(BE):
                            ins = mm(o[j * C:(j + 1) * C, :], hide[:, j, f, :],
                                     weights[j][1][:, f, h * 512:(h + 1) * 512], f == 0, f == 1)
                    end(f"O{h}.c", ins)

                def combine(h):
                    out(f"O{h}.c")
                    for t in range(TT):
                        ins = add(2 * t + h, selWT[:, t * P:(t + 1) * P], o_sb[:, h, :], False, False)

                n = r * NB + (NB - 1 if seg == "last" else b)
                if seg == "first":
                    gather(n)
                    return
                gate_up(0)
                gate_up(1)
                turn(0)
                gate_up(2)
                turn(1)
                gate_up(3)
                turn(2)
                turn(3)
                weight_transposes(n)
                if seg == "body":
                    gather(n + 1)
                for j in range(BE):
                    out(f"T{j}.c")
                down(0)
                down(1)
                out("WT.c")
                combine(0)
                combine(1)

            def one_round(r):
                def weights(b):
                    second = isinstance(b, int) and b == 1
                    ws = []
                    for j in range(BE):
                        def count(resident):
                            skipped = 1 if resident and not (isinstance(b, int) and b == 0) else 0
                            return (r * (NB - 1) if resident else r * NB) + (b - skipped) + 1
                        gu = (GU[j], (s_gu[j], count(j < NRES) * 32))
                        dw = (DW[j], [(s_dw[j][h], count(True) * 16) for h in range(2)])
                        if second and j < NRES:
                            gu = (GU_res[j], (s_gu_res[j], 32))
                        if second:
                            dw = (DW_res[j], [(s_dw_res[j], 16)] * 2)
                        ws.append((gu[0], dw[0], gu[1], dw[1]))
                    return ws
                steps("first", r, 0, None)
                for b in range(2):
                    steps("body", r, b, weights(b))
                with pe.Fori(2, NB - 1) as b:
                    steps("body", r, b, weights(b))
                steps("last", r, 0, weights(NB - 1))
            rounds(pe, one_round)
            for q in range(4):
                ins = add(q, zeros[:, :], zeros[:, 0:1], False, True, 1)
            ins.then_inc(s_sum, 1)

        @block.scalar
        def _(act):
            def take(job):
                act.wait_ge(*is_full(job))
                return ps(job)

            def freed(job, ins):
                ins.then_inc(emptied[PLACE[job][0]], 1)

            def norm_cols(pre, i, c0):
                o = take(f"{pre}{i}")
                act.wait_ge(*is_emptied("vecT"))
                for j in range(2):
                    k = 2 * i + j
                    ins = nc.scalar.activation(hT[:, k, :], o[:, j * S:(j + 1) * S], ACT.Copy, scale=vecT[:, c0 + k:c0 + k + 1])
                freed(f"{pre}{i}", ins)

            def copy(job, dst, src, scale=1.0):
                freed(job, nc.scalar.activation(dst, src, ACT.Copy, scale=scale))

            act.dma_start(vecs[0:8, :], a["norm_mix"][0].rearrange("(k p) -> k p", p=P)).then_inc(s_vec, 16)
            act.dma_start(vecs[8:16, :], a["norm_ffn"][0].rearrange("(k p) -> k p", p=P)).then_inc(s_vec, 16)
            act.dma_start(vecs[16:24, :], a["ret_norm"][0].rearrange("(k p) -> k p", p=P)).then_inc(s_vec, 16)
            for i, nm in enumerate(("cmp_pos_k", "cmp_pos_v")):
                act.dma_start(vecs[24 + 16 * i:40 + 16 * i, :],
                              a[nm][0].rearrange("(l two) d -> l (two d)", two=2)).then_inc(s_vec, 16)
            act.dma_start(buckets[:, :], a["buckets"]).then_inc(s_tab, 16)
            act.wait_ge(s_relone, 1)
            act.dma_start(relb[0:BUCKETS, :], a["rel_bias"]).then_inc(s_tab, 16)
            o = take("vecT")
            copy("vecT", vecT[:, :], o[:, 0:NVEC])
            norm_cols("xT", 1, 0)
            norm_cols("xT", 3, 0)
            o = take("btab")
            copy("btab", etab[:, :], o[0:HEADS, 0:384])
            o = take("vs")
            copy("vs", vsel[:, :, :], o[:, 0:2 * P].rearrange("p (t d) -> p t d", t=TT))
            o = take("vwg")
            copy("vwg", vwin[:, :, :], o[:, 0:304].rearrange("p (t d) -> p t d", t=TT))
            act.wait_ge(*is_emptied("vwg"))
            nc.scalar.activation(sg[:, :, :], vwin[:, :, P:P + 24], ACT.Tanh, scale=0.5).then_inc(s_sg, 1)
            for i in range(2):
                o = take(f"qT{i}")
                copy(f"qT{i}", qT[:, 2 * i:2 * i + 2, :], o[:, :].rearrange("p (a t) -> p a t", a=2), HD ** -0.5)
            for i in range(4):
                o = take(f"U{i}")
                copy(f"U{i}", Tb[:, i * 512:(i + 1) * 512], o[:, :])

            def exps(h):
                act.wait_ge(s_neg, h + 1)
                for t in range(TT):
                    for b in range(2):
                        p = prob[:, h % 4, b, t * P:(2 * t + 1) * P] if t == 0 else prob[:, h % 4, b, P:384]
                        ins = nc.scalar.activation(p, p, ACT.Exp, bias=mneg[:, t, h, b:b + 1],
                                                   accum_out=sums[:, t, h, b:b + 1])
                ins.then_inc(s_exp, 1)

            def probs_out(h):
                for b in range(2):
                    o = take(f"PT{h}.{b}")
                    if h >= 4:
                        act.wait_ge(*is_full(f"PV{(h - 4) // 2}"))
                    copy(f"PT{h}.{b}", PT[:, h % 4, b, :], o[:, 0:384])

            def swish(t, n):
                o = take(f"gr{n}{t}")
                nc.scalar.activation(gr[:, t, n * 512:(n + 1) * 512], o[:, :], ACT.Tanh, scale=0.5).then_inc(s_gt, 1)

            exps(0)
            exps(1)
            def hidden_part(i):
                o = take("hp" + "kv"[i])
                copy("hp" + "kv"[i], hpart[:, i, :], o[:, 0:CMP_HID])
            hidden_part(0)
            exps(2)
            exps(3)
            o = take("vr00")
            copy("vr00", vr[:, 0, 0:512], o[:, :])
            o = take("hidk")
            copy("hidk", hid[:, 0:64], o[:, 0:64])
            o = take("vr01")
            copy("vr01", vr[:, 1, 0:512], o[:, :])
            hidden_part(1)
            probs_out(0)
            o = take("hidv")
            copy("hidv", hid[:, 64:128], o[:, 0:64])
            probs_out(1)
            act.wait_ge(s_garg, 1)
            nc.scalar.activation(hid2[:, :], hid2[:, :], ACT.Tanh, scale=0.7978845608028654).then_inc(s_th, 1)
            for t in range(TT):
                o = take(f"vr1{t}")
                copy(f"vr1{t}", vr[:, t, 512:1024], o[:, :])
            o = take("cmpkv")
            act.wait_ge(s_ms, 2)
            for g in range(GROUPS):
                for r in range(2):
                    nc.scalar.activation(Kc[r * HD:(r + 1) * HD, g, r, :], o[r * HD:(r + 1) * HD, g * 16:(g + 1) * 16],
                                         ACT.Copy, scale=0.5).then_inc(s_ac, 1)
            probs_out(2)
            probs_out(3)
            exps(4)
            exps(5)
            act.wait_ge(s_cm, 1)
            pcf = Pc[:, :, :, :].rearrange("p t h c -> p (t h c)")
            nc.scalar.activation(pcf, pcf, ACT.Exp).then_inc(s_ce, 1)
            swish(0, 0)
            swish(1, 0)
            o = take("PcT")
            copy("PcT", PcT[:, :], o[:, 0:S])
            exps(6)
            exps(7)
            for pr in range(2):
                o = take(f"PV{pr}")
                copy(f"PV{pr}", yaT[:, pr, :], o[:, 0:S])
            swish(0, 1)
            swish(1, 1)
            probs_out(4)
            probs_out(5)
            for s, nm in enumerate("qk"):
                for t in range(TT):
                    o = take(f"rT{nm}{t}")
                    copy(f"rT{nm}{t}", qkT[:, s, :, t * P:(t + 1) * P], o[:, :].rearrange("p (h i) -> p h i", h=RH))
            o = take("PV2")
            copy("PV2", yaT[:, 2, :], o[:, 0:S])
            probs_out(6)
            probs_out(7)

            def merge_gate(w, i):
                j = f"g{'ab'[w]}{i}"
                o = take(j)
                freed(j, nc.scalar.activation(gate[:, w, 2 * i:2 * i + 2, :], o[:, :].rearrange("p (a t) -> p a t", a=2),
                                              ACT.Tanh, scale=0.5))
            act.wait_ge(*is_full("PV3"))
            merge_gate(0, 0)
            o = take("PV3")
            copy("PV3", yaT[:, 3, :], o[:, 0:S])
            for i in range(1, 4):
                merge_gate(0, i)
            for i in range(4):
                merge_gate(1, i)
            def squares(t, n):
                act.wait_ge(*is_emptied(f"out{2 * t + n}"))
                nc.scalar.activation(xe[:, t, n * 512:(n + 1) * 512], x[:, t, n * 512:(n + 1) * 512], ACT.Square,
                                     accum_out=st[:, 204 + 2 * t + n:205 + 2 * t + n]).then_inc(s_sq, 1)

            def normed(t):
                act.wait_ge(s_rstd, 6 + t)
                nc.scalar.activation(xe[:, t, :], x[:, t, :], ACT.Copy, scale=st[:, 36 + t:37 + t]).then_inc(s_xn, 1)

            def exps_router(t):
                act.wait_ge(s_rm, 2 * t + 1)
                nc.scalar.activation(rt[:, t, 110:114], rt[:, t, 40:44], ACT.Exp, bias=rt[:, t, 108:109],
                                     accum_out=rt[:, t, 109:110]).then_inc(s_re, 1)
                act.wait_ge(s_rm, 2 * t + 2)
                nc.scalar.activation(rt[:, t, 106:107], rt[:, t, 106:107], ACT.Exp).then_inc(s_re, 1)
            squares(0, 0)
            squares(0, 1)
            o = take("x2T00")
            copy("x2T00", h2T[:, 0:4, 0:P], o[:, :].rearrange("p (k t) -> p k t", k=4))
            squares(1, 0)
            normed(0)
            exps_router(0)
            squares(1, 1)
            o = take("x2T11")
            copy("x2T11", h2T[:, 4:8, P:S], o[:, :].rearrange("p (k t) -> p k t", k=4))
            normed(1)
            exps_router(1)

            def steps(seg, r, b):
                def out_of(job, dst, src=slice(0, 512)):
                    k, _ = place(seg, job, r, b)
                    act.wait_ge(*step_full(seg, job, r, b))
                    nc.scalar.activation(dst, bank[k][:, src], ACT.Copy).then_inc(emptied[k], 1)

                def gathered():
                    out_of("G0.n", hg[:, 0:4, :].rearrange("p k s -> p (k s)"))

                def tanh(j):
                    job = f"T{j}.c"
                    act.wait_ge(*step_full(seg, job, r, b))
                    nc.scalar.activation(th_sb[:, j, :, :].rearrange("p f s -> p (f s)"), bank[place(seg, job, r, b)[0]][:, 0:2 * C],
                                         ACT.Tanh, scale=0.5).then_inc(s_tanh, 1)
                if seg == "first":
                    gathered()
                    return
                out_of("GU1.c", gu_sb[:, 1, :])
                tanh(0)
                tanh(1)
                out_of("GU3.c", gu_sb[:, 1, :])
                tanh(2)
                tanh(3)
                out_of("WT.c", selWT[:, :], slice(0, S))
                if seg == "body":
                    gathered()
                out_of("O0.c", o_sb[:, 0, :])

            def one_round(r):
                steps("first", r, 0)
                for b in range(2):
                    steps("body", r, b)
                with act.Fori(2, NB - 1) as b:
                    steps("body", r, b)
                steps("last", r, 0)
            rounds(act, one_round)
            act.wait_ge(s_sum, 1)
            for q in range(3):
                nc.scalar.activation(m0[:, 512 * (q + 1):512 * (q + 2)], bank[4 + q][:, :], ACT.Square,
                                     accum_out=st[:, 210 + q:211 + q]).then_inc(s_fsq, 1)
            act.wait_ge(s_rstd, 9)
            nc.scalar.activation(xe[:, 1, 512:D], bank[7][:, :], ACT.Copy, scale=st[:, 39:40]).then_inc(s_fq, 1)

        @block.vector
        def _(dve):
            chain = [0]

            def link(ins):
                chain[0] += 1
                ins.then_inc(s_dv, 1)
                dve.wait_ge(s_dv, chain[0])

            V = nc.vector

            def take(job):
                dve.wait_ge(*is_full(job))
                return ps(job)

            def freed(job, ins):
                ins.then_inc(emptied[PLACE[job][0]], 1)

            def tsc(o, i, s1, s2, op0, op1):
                return V.tensor_scalar(o, i, s1, s2, op0, op1)

            def norm_cols(pre, i, c0):
                o = take(f"{pre}{i}")
                dve.wait_ge(*is_emptied("vecT"))
                for j in range(2):
                    k = 2 * i + j
                    ins = tsc(hT[:, k, :], o[:, j * S:(j + 1) * S], vecT[:, c0 + k:c0 + k + 1], None, ALU.mult, ALU.bypass)
                freed(f"{pre}{i}", ins)

            for t in range(TT):
                dve.wait_ge(s_x[t], 16)
                ins = V.tensor_tensor_reduce(xs[:, t, :], x[:, t, :], x[:, t, :], 1.0, 0.0, ALU.mult, ALU.add,
                                             st[:, 200 + t:201 + t])
            link(ins)
            tsc(st[:, 0:2], st[:, 200:202], 1.0 / D, EPS, ALU.mult, ALU.add).then_inc(s_rs, 1)
            dve.wait_ge(s_rstd, 1)
            for t in range(TT):
                tsc(xs[:, t, :], x[:, t, :], st[:, 32 + t:33 + t], None, ALU.mult, ALU.bypass).then_inc(s_xs, 1)
            norm_cols("xT", 0, 0)
            norm_cols("xT", 2, 0)
            o = take("kvcT")
            dve.wait_ge(s_ms, 2)
            for par in range(2):
                for g in range(GROUPS):
                    src = o[g * HD:(g + 1) * HD, :].rearrange("p (v t) -> p v t", v=2)[:, :, par:S]
                    ins = V.tensor_copy(X[par * HD:(par + 1) * HD, :, g, 0:S - par], src)
            freed("kvcT", ins)
            for job, n0 in (("ksT", 0), ("kwT", S)):
                o = take(job)
                for par in range(2):
                    for g in range(GROUPS):
                        ins = V.tensor_copy(Kp[par * HD:(par + 1) * HD, g, par, n0:n0 + S], o[g * HD:(g + 1) * HD, 0:S])
                freed(job, ins)
            dve.wait_ge(s_sg, 1)
            link(tsc(sg[:, :, :], sg[:, :, :], 1.0, 0.5, ALU.add, ALU.mult))

            dve.wait_ge(*is_full("xT3"))

            def rotate(nm, s, t):
                o = take(f"{nm}r{t}")
                ov = o[:, :].rearrange("p (h d) -> p h d", h=RH)
                q = qkr[:, t, s, :].rearrange("p (h d) -> p h d", h=RH)
                tmp = rtmp.rearrange("p (h d) -> p h d", h=RH)
                V.tensor_tensor(q, ov, rot[:, t, 0:1, :].broadcast_to((P, RH, RQ)), ALU.mult)
                V.tensor_tensor(tmp[:, :, 0:64], ov[:, :, 64:128], rot[:, t, 1:2, 0:64].broadcast_to((P, RH, 64)), ALU.mult)
                link(V.tensor_tensor(tmp[:, :, 64:128], ov[:, :, 0:64], rot[:, t, 1:2, 64:128].broadcast_to((P, RH, 64)), ALU.mult))
                freed(f"{nm}r{t}", V.tensor_tensor(q, q, tmp, ALU.add))
                dve.wait_ge(*is_emptied(f"{nm}r{t}"))

            def biased(h):
                if h == 0:
                    for i in range(4):
                        dve.wait_ge(*is_emptied(f"U{i}"))
                if h >= 4:
                    dve.wait_ge(*is_full(f"PT{h - 4}.1"))
                for t in range(TT):
                    j = f"S{t}.{h}"
                    o = take(j)
                    w = (t + 1) * P
                    for b in range(2):
                        dst = prob[:, h % 4, b, 0:P] if t == 0 else prob[:, h % 4, b, P:384]
                        ins = V.tensor_tensor_reduce(dst, o[:, b * S:b * S + w], Tt[:, h, S - w:S], 1.0, -3e38, ALU.add, ALU.max,
                                                     mx[:, t, h, b:b + 1])
                    freed(j, ins)
                for t in range(TT):
                    dve.wait_ge(*is_emptied(f"S{t}.{h}"))
                tsc(mneg[:, :, h, :], mx[:, :, h, :], -1.0, None, ALU.mult, ALU.bypass).then_inc(s_neg, 1)

            def scaled(h):
                dve.wait_ge(s_exp, h + 1)
                link(V.reciprocal(coef[:, :, h, :], sums[:, :, h, :]))
                link(V.tensor_tensor(coef[:, :, h, :], coef[:, :, h, :],
                                     sg[:, :, :].rearrange("p t (b h) -> p t b h", b=3)[:, :, 1:3, h], ALU.mult))
                for b in range(2):
                    for t in range(TT):
                        p = prob[:, h % 4, b, 0:P] if t == 0 else prob[:, h % 4, b, P:384]
                        ins = tsc(p, p, coef[:, t, h, b:b + 1], None, ALU.mult, ALU.bypass)
                ins.then_inc(s_prob, 1)

            dve.wait_ge(s_cst2, 16)
            rotate("q", 0, 0)
            rotate("q", 0, 1)
            biased(0)
            biased(1)
            rotate("k", 1, 0)
            rotate("k", 1, 1)
            scaled(0)
            scaled(1)
            biased(2)
            biased(3)
            scaled(2)
            scaled(3)
            o = take("cmpkv")
            dve.wait_ge(s_ac, 4)
            freed("cmpkv", V.scalar_tensor_tensor(Vc[:, :, :], o[:, 64:128].unsqueeze(1).broadcast_to((P, HEADS, HD)), 0.5,
                                                  headmask.unsqueeze(2).broadcast_to((P, HEADS, HD)), ALU.mult, ALU.mult))
            biased(4)
            biased(5)
            o = take("Sc")
            p3 = Pc[:, :, :, :].rearrange("p t h c -> p (t h) c")
            m16, s16 = st[:, 64:80], st[:, 80:96]

            def over_blocks(v):
                return v.unsqueeze(2).broadcast_to((P, TT * HEADS, NC16))
            for t in range(TT):
                j0 = (TT - 1 - t) * P + CMP_LEN - 1
                n = min(NCMP, (S - 1 - j0) // CMP_STRIDE + 1)
                ins = V.tensor_tensor(Pc[:, t, :, 0:n], o[:, t * P:(t + 1) * P].rearrange("p (h c) -> p h c", c=NC16)[:, :, 0:n],
                                      Tt[:, :, j0:j0 + (n - 1) * CMP_STRIDE + 1:CMP_STRIDE], ALU.add)
            freed("Sc", ins)
            dve.wait_ge(*is_emptied("Sc"))
            link(V.tensor_reduce(m16, p3, AX, ALU.max))
            V.tensor_tensor(p3, p3, over_blocks(m16), ALU.subtract).then_inc(s_cm, 1)
            scaled(4)
            dve.wait_ge(s_ce, 1)
            for t in range(TT):
                ins = V.tensor_tensor(Pc[:, t, :, :], Pc[:, t, :, :], maskc[:, t:t + 1, :].broadcast_to((P, HEADS, NC16)), ALU.mult)
            link(ins)
            link(V.tensor_reduce(s16, p3, AX, ALU.add))
            link(tsc(s16, s16, 1e-30, None, ALU.max, ALU.bypass))
            link(V.reciprocal(s16, s16))
            link(V.tensor_tensor(s16.rearrange("p (t h) -> p t h", t=TT), s16.rearrange("p (t h) -> p t h", t=TT),
                                 sg[:, :, 0:HEADS], ALU.mult))
            V.tensor_tensor(p3, p3, over_blocks(s16), ALU.mult).then_inc(s_pc, 1)
            scaled(5)

            n_sw = [0]

            def swish(t, n):
                o = take(f"gr{n}{t}")
                n_sw[0] += 1
                dve.wait_ge(s_gt, n_sw[0])
                g = gr[:, t, n * 512:(n + 1) * 512]
                freed(f"gr{n}{t}", V.scalar_tensor_tensor(g, g, 1.0, o[:, :], ALU.add, ALU.mult))
            swish(0, 0)
            swish(1, 0)
            biased(6)
            biased(7)
            scaled(6)
            scaled(7)
            swish(0, 1)
            swish(1, 1)
            for h in range(RH):
                o = take(f"ST{h}")
                V.tensor_tensor(STs[:, h, 0:S], o[:, 0:S], decay[:, h, :], ALU.mult)
                freed(f"ST{h}", V.tensor_tensor(STs[:, h, S:384], o[:, S:384], decay[:, h, 0:P], ALU.mult))
            for i, (t, hp) in enumerate(((0, 0), (0, 1), (1, 0), (1, 1))):
                o = take(f"Y{t}{hp}")
                for j in range(2):
                    ins = V.bn_stats(st[:, 100 + 6 * j:106 + 6 * j], o[:, j * RV:(j + 1) * RV])
                link(ins)
                for j in range(2):
                    ins = V.bn_aggr(st[:, 120 + 2 * j:122 + 2 * j], st[:, 100 + 6 * j:106 + 6 * j])
                link(ins)
                tsc(st[:, 8 + 4 * i:10 + 4 * i], st[:, 120:124].rearrange("p (a b) -> p b a", b=2)[:, 1, :], EPS, None,
                    ALU.add, ALU.bypass).then_inc(s_rs, 1)
                dve.wait_ge(s_rstd, 2 + i)
                if i == 0:
                    for q in range(4):
                        dve.wait_ge(*is_full(f"U{q}"))
                for j in range(2):
                    ins = tsc(y[:, t, (2 * hp + j) * RV:(2 * hp + j + 1) * RV], o[:, j * RV:(j + 1) * RV],
                              st[:, 120 + 2 * j:121 + 2 * j], st[:, 40 + 4 * i + j:41 + 4 * i + j], ALU.subtract, ALU.mult)
                freed(f"Y{t}{hp}", ins)
                if hp == 1:
                    for q in range(2):
                        dve.wait_ge(*is_emptied(f"Y{t}{q}"))
                    if t == 0:
                        for q in ("gr00", "gr01", "gr10", "gr11"):
                            dve.wait_ge(*is_emptied(q))
                    V.tensor_tensor(y[:, t, :], y[:, t, :], gr[:, t, :], ALU.mult).then_inc(s_y, 1)
            for i in range(4):
                o = take(f"yrT{i}")
                for j in range(2):
                    k = 2 * i + j
                    ins = tsc(yrT[:, k, :], o[:, j * S:(j + 1) * S], vecT[:, 16 + k:17 + k], 0.5, ALU.mult, ALU.mult)
                freed(f"yrT{i}", ins)
            for i in range(KT):
                o = take(f"up{i}")
                if i % 2 == 0:
                    for w in "ab":
                        dve.wait_ge(*is_emptied(f"g{w}{i // 2}"))
                V.scalar_tensor_tensor(gate[:, 0, i, :], gate[:, 0, i, :], 1.0, o[:, 0:S], ALU.add, ALU.mult)
                freed(f"up{i}", V.scalar_tensor_tensor(gate[:, 1, i, :], gate[:, 1, i, :], 1.0, o[:, S:2 * S], ALU.add, ALU.mult))
                dve.wait_ge(*is_emptied(f"up{i}"))
                V.tensor_tensor(gate[:, 0, i, :], gate[:, 0, i, :], gate[:, 1, i, :], ALU.add).then_inc(s_mrg, 1)
            dve.wait_ge(s_rw, 64)
            V.tensor_tensor(wr[:, :, :], wr[:, :, :], vecT[:, KT:2 * KT].unsqueeze(2).broadcast_to((P, KT, NG + NE)), ALU.mult).then_inc(s_wr, 1)

            def residual(t, n):
                o = take(f"out{2 * t + n}")
                xx = x[:, t, n * 512:(n + 1) * 512]
                freed(f"out{2 * t + n}", V.scalar_tensor_tensor(xx, o[:, :], 0.5, xx, ALU.mult, ALU.add))

            def variance(t):
                dve.wait_ge(s_sq, 2 * t + 2)
                link(V.tensor_tensor(st[:, 200 + t:201 + t], st[:, 204 + 2 * t:205 + 2 * t], st[:, 205 + 2 * t:206 + 2 * t], ALU.add))
                tsc(st[:, 4 + t:5 + t], st[:, 200 + t:201 + t], 1.0 / D, EPS, ALU.mult, ALU.add).then_inc(s_rs, 1)

            def stream_out(t, n):
                o = take(f"x2T{t}{n}")
                freed(f"x2T{t}{n}", V.tensor_copy(h2T[:, 4 * n:4 * n + 4, t * P:(t + 1) * P], o[:, :].rearrange("p (k t) -> p k t", k=4)))

            def router(t):
                le = rt[:, t, 4:36].rearrange("p (g e) -> p g e", g=NG)
                masked = rt[:, t, 64:96].rearrange("p (g e) -> p g e", g=NG)
                dve.wait_ge(s_rstd, 6 + t)
                o = take(f"route{t}")
                link(V.scalar_tensor_tensor(rt[:, t, 40:44], o[:, 0:NG], st[:, 36 + t:37 + t], rbias[:, 0:NG], ALU.mult, ALU.add))
                freed(f"route{t}", V.scalar_tensor_tensor(rt[:, t, 4:36], o[:, NG:NG + NE], st[:, 36 + t:37 + t],
                                                          rbias[:, NG:NG + NE], ALU.mult, ALU.add))
                link(V.max(rt[:, t, 48:56], rt[:, t, 40:48]))
                tsc(rt[:, t, 108:109], rt[:, t, 48:49], -1.0, None, ALU.mult, ALU.bypass).then_inc(s_rm, 1)
                link(V.max_index(ri[:, t, 0:8], rt[:, t, 48:56], rt[:, t, 40:48]))
                link(V.tensor_copy(rt[:, t, 104:105], ri[:, t, 0:1]))
                link(tsc(rt[:, t, 60:64], iota[:, 0:NG], rt[:, t, 104:105], NEG, ALU.not_equal, ALU.mult))
                dve.wait_ge(*is_emptied(f"route{t}"))
                link(V.tensor_tensor(masked, le, rt[:, t, 60:64].unsqueeze(2).broadcast_to((P, NG, EPG)), ALU.add))
                link(V.max(rt[:, t, 96:104], rt[:, t, 64:96]))
                V.tensor_tensor(rt[:, t, 106:107], rt[:, t, 97:98], rt[:, t, 96:97], ALU.subtract).then_inc(s_rm, 1)
                link(V.max_index(ri[:, t, 8:16], rt[:, t, 96:104], rt[:, t, 64:96]))
                link(V.tensor_copy(rt[:, t, 104:106], ri[:, t, 8:10]))
                tsc(comb1[:, t, :], iota, rt[:, t, 104:105], None, ALU.is_equal, ALU.bypass)
                link(tsc(rt[:, t, 124:156], iota, rt[:, t, 105:106], None, ALU.is_equal, ALU.bypass))
                V.tensor_tensor(comb1[:, t, :], comb1[:, t, :], rt[:, t, 124:156], ALU.add).then_inc(s_M, 1)
            residual(0, 0)
            residual(0, 1)
            variance(0)
            stream_out(0, 1)
            residual(1, 0)
            dve.wait_ge(s_ms, 2)
            router(0)
            residual(1, 1)
            stream_out(1, 0)
            variance(1)
            router(1)
            dve.wait_ge(s_M, TT)
            link(tsc(posm[:, :, :], comb1[:, :, :], -1.0, 1e9, ALU.add, ALU.mult))
            o = take("pos")
            V.tensor_reduce(nround[:, 0:1], o[:, 2 * NE:3 * NE], AX, ALU.max)
            V.tensor_tensor(posm[:, :, :], o[:, 0:2 * NE].rearrange("p (t e) -> p t e", t=TT),
                            posm[:, :, :], ALU.add).then_inc(emptied[PLACE["pos"][0]], 1)
            dve.wait_ge(*is_emptied("pos"))

            def routing_weights():
                link(tsc(nround[:, 8:16], iota[:, 0:ROUNDS], -float(C), nround[:, 0:1], ALU.mult, ALU.add))
                link(tsc(nround[:, 8:16], nround[:, 8:16], 0.0, None, ALU.is_gt, ALU.bypass))
                link(V.tensor_reduce(nround[:, 1:2], nround[:, 8:16], AX, ALU.add))
                V.tensor_copy(nround_i[:, :], nround[:, 1:2]).then_inc(s_nr, 1)
                dve.wait_ge(s_re, 4)
                link(tsc(rt[:, :, 107:108], rt[:, :, 106:107], 1.0, None, ALU.add, ALU.bypass))
                link(V.tensor_tensor(rt[:, :, 107:108], rt[:, :, 107:108], rt[:, :, 109:110], ALU.mult))
                link(V.reciprocal(rt[:, :, 107:108], rt[:, :, 107:108]))
                link(tsc(rt[:, :, 120:121], rt[:, :, 107:108], 0.5, None, ALU.mult, ALU.bypass))
                link(V.tensor_tensor(rt[:, :, 121:122], rt[:, :, 120:121], rt[:, :, 106:107], ALU.mult))
                for t in range(TT):
                    ins = tsc(comb[:, t, :], iota, rt[:, t, 104:105], rt[:, t, 120:121], ALU.is_equal, ALU.mult)
                    ins = tsc(rt[:, t, 124:156], iota, rt[:, t, 105:106], rt[:, t, 121:122], ALU.is_equal, ALU.mult)
                link(ins)
                link(V.tensor_tensor(comb[:, :, :], comb[:, :, :], rt[:, :, 124:156], ALU.add))

            def steps(seg, r, b):
                n = r * NB + b

                def out_of(job, dst, src=slice(0, 512)):
                    k, _ = place(seg, job, r, b if seg == "body" else 0)
                    dve.wait_ge(*step_full(seg, job, r, b if seg == "body" else 0))
                    V.tensor_copy(dst, bank[k][:, src]).then_inc(emptied[k], 1)

                def gathered():
                    out_of("G1.n", hg[:, 4:8, :].rearrange("p k s -> p (k s)"))

                def hidden(j):
                    dve.wait_ge(s_tanh, n * BE + j + 1)
                    k, _ = place(seg, f"T{j}.c", r, 0)
                    h, t = (v[:, j, :, :].rearrange("p f s -> p (f s)") for v in (hide, th_sb))
                    V.scalar_tensor_tensor(h, t, 1.0, bank[k][:, 0:2 * C], ALU.add, ALU.mult).then_inc(s_hch, 1)
                    dve.wait_ge(s_hch, n * BE + j + 1)
                    V.tensor_tensor(h, h, bank[k][:, 2 * C:4 * C], ALU.mult).then_inc(emptied[k], 1)

                def batch_cols(v, t, c):
                    return v[:, t, bass.ds(c * BE, BE)].unsqueeze(2).broadcast_to((P, BE, C))

                def select(c):
                    for t in range(TT):
                        V.tensor_tensor(selG[:, t, :, :], iota[:, 0:C].unsqueeze(1).broadcast_to((P, BE, C)),
                                        batch_cols(posm, t, c), ALU.is_equal).then_inc(s_sel, 1)

                def select_weights(m, c):
                    dve.wait_ge(s_sel, m * TT + TT)
                    for t in range(TT):
                        ins = V.tensor_tensor(selW[:, t, :, :], selG[:, t, :, :], batch_cols(comb, t, c), ALU.mult)
                    ins.then_inc(s_w, 1)
                if seg == "first":
                    if not isinstance(r, int):
                        V.tensor_scalar(posm[:, :, :], posm[:, :, :], -float(C), None, ALU.add, ALU.bypass).then_inc(s_shift, 1)
                        dve.wait_ge(s_shift, r)
                    select(0)
                    if isinstance(r, int):
                        routing_weights()
                    select_weights(n, 0)
                    gathered()
                    return
                out_of("GU0.c", gu_sb[:, 0, :])
                hidden(0)
                if seg == "body":
                    select(b + 1)
                out_of("GU2.c", gu_sb[:, 0, :])
                hidden(1)
                hidden(2)
                hidden(3)
                if seg == "body":
                    dve.wait_ge(*step_full(seg, "WT.c", r, b))
                    select_weights(n + 1, b + 1)
                    gathered()
                out_of("O1.c", o_sb[:, 1, :])

            def one_round(r):
                steps("first", r, 0)
                for b in range(2):
                    steps("body", r, b)
                with dve.Fori(2, NB - 1) as b:
                    steps("body", r, b)
                steps("last", r, NB - 1)
            rounds(dve, one_round)

            dve.wait_ge(s_sum, 1)
            link(V.tensor_copy(m0[:, 2048:2560], bank[7][:, :]))
            link(V.tensor_tensor_reduce(m0[:, 2560:3072], m0[:, 2048:2560], m0[:, 2048:2560], 1.0, 0.0, ALU.mult, ALU.add, st[:, 213:214]))
            for t in range(TT):
                dve.wait_ge(s_fsq, 2 + t)
                link(V.tensor_tensor(st[:, 202 + t:203 + t], st[:, 210 + 2 * t:211 + 2 * t], st[:, 211 + 2 * t:212 + 2 * t], ALU.add))
                tsc(st[:, 6 + t:7 + t], st[:, 202 + t:203 + t], 1.0 / D, EPS, ALU.mult, ALU.add).then_inc(s_rs, 1)
            dve.wait_ge(s_nf, 16)
            for q in range(3):
                t, w = q // 2, slice((q % 2) * 512, (q % 2 + 1) * 512)
                dve.wait_ge(s_rstd, 8 + t)
                V.scalar_tensor_tensor(xe[:, t, w], bank[4 + q][:, :], st[:, 38 + t:39 + t], nf[:, w], ALU.mult, ALU.mult).then_inc(s_fin, 1)


_INS = ["x", "rel_bias", "norm_mix", "w_in", "cmp_pos_k", "cmp_k_w1", "cmp_k_w2", "cmp_pos_v", "cmp_v_w1", "cmp_v_w2",
        "ret_norm", "w_nsa_up", "w_ret_up", "w_out", "norm_ffn", "w_router_group", "b_router_group",
        "w_router_expert", "b_router_expert", "moe_w_gate", "moe_w_up", "moe_w_down", "norm_final"]


def kernel(**inputs):
    import concourse.bacc as bacc
    from concourse.bass_utils import run_bass_kernel_spmd

    nc = bacc.Bacc("TRN2", target_bir_lowering=False, num_devices=1)
    arrays, aps = {}, {}
    tables = shape_tables()
    for name in _INS + list(tables):
        v = np.ascontiguousarray(inputs[name] if name in inputs else tables[name])
        arrays[f"in_{name}"] = v
        aps[name] = nc.dram_tensor(f"in_{name}", v.shape, mybir.dt.from_np(v.dtype), kind="ExternalInput").ap()
    out = nc.dram_tensor("out_0", (1, S, D), F32, kind="ExternalOutput").ap()
    build(nc, aps, out)
    r = run_bass_kernel_spmd(nc, [arrays], core_ids=[0])
    return r.results[0]["out_0"]
```
